# Optimizing a Trainium2 kernel written in Bass

```python
import math
import jax, jax.numpy as jnp
from jax import lax
import numpy as np

D_MODEL = 1024
BATCH = 1
SEQ = 1024
DEPTH = 1
DEC_BATCH = 8
DEC_SEQ = 8
PAST_LEN = 8192
PAGE_SIZE = 128

N_BRANCH = 4
BRANCH_WIDTH = 512
H_A = 4
DK_A = 128
DV_A = 128
HK_A = H_A * DK_A
HV_A = H_A * DV_A
H_B = 4
DK_B = 128
DV_B = 128
HK_B = H_B * DK_B
HV_B = H_B * DV_B
D_C = BRANCH_WIDTH
CONV_C = 3
D_D = BRANCH_WIDTH
CONV_D = 31
D_FF = 4 * D_MODEL
CHUNK = 64
EPS = 1e-6
SPLIT_SIZES = (HK_A, HK_A, HV_A, HV_A, HK_B, HK_B, HV_B, HV_B, H_B, H_B, D_C, D_C, D_C, D_D, D_D, N_BRANCH * D_MODEL)
D_IN = 2 * HK_A + 2 * HV_A + 2 * HK_B + 2 * HV_B + 2 * H_B + 3 * D_C + 2 * D_D + N_BRANCH * D_MODEL

kernel_name = 'hybrid_hgrn2_mlstm_conv_decoder_step'

def _split_points():
    pts, acc = [], 0
    for s in SPLIT_SIZES[:-1]:
        acc += s
        pts.append(acc)
    return pts

def rms_norm(x, g):
    xf = x.astype(jnp.float32)
    y = xf * lax.rsqrt(jnp.mean(xf * xf, axis=-1, keepdims=True) + EPS)
    return (y * g.astype(jnp.float32)).astype(x.dtype)

def head_rms_norm(o, g, n_heads):
    y = o * lax.rsqrt(jnp.mean(o * o, axis=-1, keepdims=True) + EPS)
    return y * g.astype(jnp.float32).reshape(n_heads, -1)

def layer_norm(x, g, b):
    xf = x.astype(jnp.float32)
    mu = jnp.mean(xf, axis=-1, keepdims=True)
    xc = xf - mu
    y = xc * lax.rsqrt(jnp.mean(xc * xc, axis=-1, keepdims=True) + EPS)
    return y * g.astype(jnp.float32) + b.astype(jnp.float32)

def causal_depthwise_conv(u, buf, w):
    width, ch = w.shape
    ext = jnp.concatenate([buf.astype(u.dtype), u], axis=1)
    y = lax.conv_general_dilated(ext, w[:, None, :].astype(u.dtype), (1,), 'VALID',
                                 dimension_numbers=('NWC', 'WIO', 'NWC'), feature_group_count=ch)
    return y, ext[:, ext.shape[1] - (width - 1):]

def _chunks(a, n_chunks):
    b, t = a.shape[:2]
    return jnp.moveaxis(a.reshape(b, n_chunks, t // n_chunks, *a.shape[2:]), 1, 0)

def _unchunk(a):
    n, b, l = a.shape[:3]
    return jnp.moveaxis(a, 0, 1).reshape(b, n * l, *a.shape[3:])

def hgrn2_recurrence(q, k, v, log_f, s0):
    t = q.shape[1]
    length = math.gcd(t, CHUNK)
    n = t // length
    causal = jnp.tril(jnp.ones((length, length), dtype=bool))

    def chunk_step(s, xs):
        qc, kc, vc, gc = xs
        g_cum = jnp.cumsum(gc, axis=1)
        rel = g_cum[:, :, None] - g_cum[:, None]
        decay = jnp.exp(jnp.where(causal[None, :, :, None, None], rel, -jnp.inf))
        scores = jnp.einsum('blhd,bmhd,blmhd->bhlm', qc, kc, decay)
        o = (jnp.einsum('bhlm,bmhv->blhv', scores, vc)
             + jnp.einsum('blhd,bhdv->blhv', qc * jnp.exp(g_cum), s))
        g_last = g_cum[:, -1]
        k_dec = kc * jnp.exp(g_last[:, None] - g_cum)
        s_new = jnp.exp(g_last)[..., None] * s + jnp.einsum('blhd,blhv->bhdv', k_dec, vc)
        return s_new, o

    xs = (_chunks(q, n), _chunks(k, n), _chunks(v, n), _chunks(log_f, n))
    s_fin, o = lax.scan(chunk_step, s0, xs)
    return _unchunk(o), s_fin

def mlstm_recurrence(q, k, v, i_pre, log_f, c0, n0, m0):
    t = q.shape[1]
    length = math.gcd(t, CHUNK)
    n = t // length
    causal = jnp.tril(jnp.ones((length, length), dtype=bool))

    def chunk_step(carry, xs):
        c, nv, m = carry
        qc, kc, vc, ic, fc = xs
        b = jnp.cumsum(fc, axis=1)
        d = jnp.where(causal[None, :, :, None], b[:, :, None] - b[:, None] + ic[:, None], -jnp.inf)
        m_inter = b + m[:, None]
        m_t = jnp.maximum(m_inter, jnp.max(d, axis=2))
        w = jnp.exp(d - m_t[:, :, None])
        w_inter = jnp.exp(m_inter - m_t)
        qk = jnp.einsum('blhd,bmhd->blmh', qc, kc) * w
        num = (jnp.einsum('blmh,bmhv->blhv', qk, vc)
               + w_inter[..., None] * jnp.einsum('blhd,bhdv->blhv', qc, c))
        den = qk.sum(axis=2) + w_inter * jnp.einsum('blhd,bhd->blh', qc, nv)
        h = num / jnp.maximum(jnp.abs(den), jnp.exp(-m_t))[..., None]
        m_new = m_t[:, -1]
        w_state = jnp.exp(b[:, -1:] - b + ic - m_new[:, None])
        carry_decay = jnp.exp(b[:, -1] + m - m_new)
        c_new = carry_decay[..., None, None] * c + jnp.einsum('blh,blhd,blhv->bhdv', w_state, kc, vc)
        n_new = carry_decay[..., None] * nv + jnp.einsum('blh,blhd->bhd', w_state, kc)
        return (c_new, n_new, m_new), h

    xs = (_chunks(q, n), _chunks(k, n), _chunks(v, n), _chunks(i_pre, n), _chunks(log_f, n))
    (c_fin, n_fin, m_fin), h = lax.scan(chunk_step, (c0, n0, m0), xs)
    return _unchunk(h), c_fin, n_fin, m_fin

def hybrid_mixer(h, lw, st):
    (w_in, w_branch, w_out, lb, norm_hgrn, i_bias, f_bias, norm_mlstm, conv_short_w,
     conv_conf_w, conv_conf_b, ln_conf_g, ln_conf_b) = lw
    s_hgrn, s_c, s_n, s_m, buf_short, buf_conf = st
    bt, t, _ = h.shape
    f32 = jnp.float32
    proj = h @ w_in
    (qa, fa, ia, ga, qb, kb, vb, ob, igb, fgb, bc, cc, xc, ad, gd, gates) = jnp.split(proj, _split_points(), axis=-1)

    forget = lb + (1.0 - lb) * jax.nn.sigmoid(qa.astype(f32) * 0.0 + fa.astype(f32)) if False else lb + (1.0 - lb) * jax.nn.sigmoid(fa.astype(f32))
    log_fa = jnp.log(forget).reshape(bt, t, H_A, DK_A)
    k_a = (1.0 - forget).reshape(bt, t, H_A, DK_A)
    q_a = jax.nn.silu(qa.astype(f32)).reshape(bt, t, H_A, DK_A)
    v_a = ia.astype(f32).reshape(bt, t, H_A, DV_A)
    o_a, s_hgrn_new = hgrn2_recurrence(q_a, k_a, v_a, log_fa, s_hgrn.astype(f32))
    o_a = (head_rms_norm(o_a, norm_hgrn, H_A).reshape(bt, t, HV_A) * jax.nn.silu(ga.astype(f32))).astype(h.dtype)

    q_b = qb.astype(f32).reshape(bt, t, H_B, DK_B) * (DK_B ** -0.5)
    k_b = kb.astype(f32).reshape(bt, t, H_B, DK_B)
    v_b = vb.astype(f32).reshape(bt, t, H_B, DV_B)
    i_pre = igb.astype(f32) + i_bias.astype(f32)
    log_fb = jax.nn.log_sigmoid(fgb.astype(f32) + f_bias.astype(f32))
    h_b, c_new, n_new, m_new = mlstm_recurrence(q_b, k_b, v_b, i_pre, log_fb,
                                                s_c.astype(f32), s_n.astype(f32), s_m.astype(f32))
    o_b = (jax.nn.sigmoid(ob.astype(f32)) * head_rms_norm(h_b, norm_mlstm, H_B).reshape(bt, t, HV_B)).astype(h.dtype)

    y_c, buf_short_new = causal_depthwise_conv(cc * xc, buf_short, conv_short_w)
    o_c = (bc * y_c).astype(h.dtype)

    glu = ad * jax.nn.sigmoid(gd)
    y_d, buf_conf_new = causal_depthwise_conv(glu, buf_conf, conv_conf_w)
    o_d = jax.nn.silu(layer_norm(y_d + conv_conf_b.astype(y_d.dtype), ln_conf_g, ln_conf_b)).astype(h.dtype)

    branches = jnp.stack([o_a, o_b, o_c, o_d], axis=2)
    proj_br = jnp.einsum('btnc,ncd->btnd', branches, w_branch)
    gate = jax.nn.sigmoid(gates.reshape(bt, t, N_BRANCH, D_MODEL))
    merged = jnp.sum(gate * proj_br, axis=2)
    out = merged @ w_out
    return out, (s_hgrn_new, c_new, n_new, m_new, buf_short_new, buf_conf_new)

def trunk_layer(x, lw, norm_mix, norm_mlp, w_up, w_down, st):
    y, st_new = hybrid_mixer(rms_norm(x, norm_mix), lw, st)
    x = x + y
    hm = rms_norm(x, norm_mlp)
    x = x + jnp.square(jax.nn.relu(hm @ w_up)) @ w_down
    return x, st_new

def setup_inputs(seed: int = 0) -> dict:
    key = jax.random.key(seed)
    ks = jax.random.split(key, 26)

    def nrm(k, shape, scale):
        return jax.random.normal(k, shape, jnp.float32) * scale

    return {
        'x_prompt': nrm(ks[0], (BATCH, SEQ, D_MODEL), 1.0),
        'x_sample': nrm(ks[1], (DEC_BATCH, DEC_SEQ, D_MODEL), 1.0),
        'state_hgrn': nrm(ks[2], (DEPTH, DEC_BATCH, H_A, DK_A, DV_A), 0.3),
        'state_mlstm_c': nrm(ks[3], (DEPTH, DEC_BATCH, H_B, DK_B, DV_B), 0.1),
        'state_mlstm_n': nrm(ks[4], (DEPTH, DEC_BATCH, H_B, DK_B), 0.3),
        'state_mlstm_m': jax.random.uniform(ks[5], (DEPTH, DEC_BATCH, H_B), jnp.float32, 0.0, 4.0),
        'state_conv_short': nrm(ks[6], (DEPTH, DEC_BATCH, CONV_C - 1, D_C), 0.5),
        'state_conv_conformer': nrm(ks[7], (DEPTH, DEC_BATCH, CONV_D - 1, D_D), 0.5),
        'w_in': nrm(ks[8], (DEPTH, D_MODEL, D_IN), D_MODEL ** -0.5),
        'w_branch': nrm(ks[9], (DEPTH, N_BRANCH, BRANCH_WIDTH, D_MODEL), BRANCH_WIDTH ** -0.5),
        'w_out': nrm(ks[10], (DEPTH, D_MODEL, D_MODEL), D_MODEL ** -0.5),
        'lb_logits': nrm(ks[11], (DEPTH, HK_A), 0.5),
        'norm_hgrn': 1.0 + nrm(ks[12], (DEPTH, HV_A), 0.1),
        'mlstm_i_bias': nrm(ks[13], (DEPTH, H_B), 0.1),
        'mlstm_f_bias': jnp.linspace(3.0, 6.0, H_B, dtype=jnp.float32)[None, :] + nrm(ks[14], (DEPTH, H_B), 0.1),
        'norm_mlstm': 1.0 + nrm(ks[15], (DEPTH, HV_B), 0.1),
        'conv_short_w': nrm(ks[16], (DEPTH, CONV_C, D_C), CONV_C ** -0.5),
        'conv_conformer_w': nrm(ks[17], (DEPTH, CONV_D, D_D), CONV_D ** -0.5),
        'conv_conformer_b': nrm(ks[18], (DEPTH, D_D), 0.02),
        'ln_conformer_g': 1.0 + nrm(ks[19], (DEPTH, D_D), 0.1),
        'ln_conformer_b': nrm(ks[20], (DEPTH, D_D), 0.02),
        'norm_mix': 1.0 + nrm(ks[21], (DEPTH, D_MODEL), 0.1),
        'norm_mlp': 1.0 + nrm(ks[22], (DEPTH, D_MODEL), 0.1),
        'w_up': nrm(ks[23], (DEPTH, D_MODEL, D_FF), D_MODEL ** -0.5),
        'w_down': nrm(ks[24], (DEPTH, D_FF, D_MODEL), D_FF ** -0.5),
        'norm_final': 1.0 + nrm(ks[25], (D_MODEL,), 0.1),
    }

def reference(x_prompt, x_sample, state_hgrn, state_mlstm_c, state_mlstm_n, state_mlstm_m,
              state_conv_short, state_conv_conformer, w_in, w_branch, w_out, lb_logits, norm_hgrn,
              mlstm_i_bias, mlstm_f_bias, norm_mlstm, conv_short_w, conv_conformer_w, conv_conformer_b,
              ln_conformer_g, ln_conformer_b, norm_mix, norm_mlp, w_up, w_down, norm_final):
    lb_soft = jax.nn.softmax(lb_logits.astype(jnp.float32), axis=0)
    lower_bounds = jnp.cumsum(lb_soft, axis=0) - lb_soft[0]

    bp = x_prompt.shape[0]
    xp, xs = x_prompt, x_sample
    new_p, new_s = [], []
    for l in range(DEPTH):
        lw = (w_in[l], w_branch[l], w_out[l], lower_bounds[l], norm_hgrn[l], mlstm_i_bias[l], mlstm_f_bias[l],
              norm_mlstm[l], conv_short_w[l], conv_conformer_w[l], conv_conformer_b[l],
              ln_conformer_g[l], ln_conformer_b[l])
        zero_st = (jnp.zeros((bp, H_A, DK_A, DV_A), jnp.float32),
                   jnp.zeros((bp, H_B, DK_B, DV_B), jnp.float32),
                   jnp.zeros((bp, H_B, DK_B), jnp.float32),
                   jnp.zeros((bp, H_B), jnp.float32),
                   jnp.zeros((bp, CONV_C - 1, D_C), x_prompt.dtype),
                   jnp.zeros((bp, CONV_D - 1, D_D), x_prompt.dtype))
        past_st = (state_hgrn[l], state_mlstm_c[l], state_mlstm_n[l], state_mlstm_m[l],
                   state_conv_short[l], state_conv_conformer[l])
        xp, st_p = trunk_layer(xp, lw, norm_mix[l], norm_mlp[l], w_up[l], w_down[l], zero_st)
        xs, st_s = trunk_layer(xs, lw, norm_mix[l], norm_mlp[l], w_up[l], w_down[l], past_st)
        new_p.append(st_p)
        new_s.append(st_s)

    y_prompt = rms_norm(xp, norm_final)
    y_sample = rms_norm(xs, norm_final)
    hgrn_p = jnp.stack([s[0] for s in new_p])
    hgrn_s = jnp.stack([s[0] for s in new_s])
    mlstm_c_p = jnp.stack([s[1] for s in new_p])
    mlstm_c_s = jnp.stack([s[1] for s in new_s])
    mlstm_n_p = jnp.stack([s[2] for s in new_p])
    mlstm_n_s = jnp.stack([s[2] for s in new_s])
    mlstm_m_p = jnp.stack([s[3] for s in new_p])
    mlstm_m_s = jnp.stack([s[3] for s in new_s])
    conv_short_p = jnp.stack([s[4] for s in new_p])
    conv_short_s = jnp.stack([s[4] for s in new_s])
    conv_conf_p = jnp.stack([s[5] for s in new_p])
    conv_conf_s = jnp.stack([s[5] for s in new_s])
    return (y_prompt, y_sample, hgrn_p, hgrn_s, mlstm_c_p, mlstm_c_s, mlstm_n_p, mlstm_n_s,
            mlstm_m_p, mlstm_m_s, conv_short_p, conv_short_s, conv_conf_p, conv_conf_s)


_drawn_inputs = setup_inputs


def setup_inputs(seed=0):
    import zlib

    import numpy as np

    out = dict(_drawn_inputs(seed))
    spreads = {}
    factors = {'state_hgrn': 4.928, 'conv_conformer_b': 5.285, 'ln_conformer_b': 8.0}
    for name, (base, spread) in spreads.items():
        noise = np.random.default_rng([zlib.crc32(name.encode()), seed]).standard_normal(out[name].shape)
        drawn = base * np.exp(spread * noise) if base else spread * noise
        out[name] = __import__('jax').numpy.asarray(drawn.astype(out[name].dtype))
    for name, factor in factors.items():
        out[name] = (out[name] * factor).astype(out[name].dtype)
    return out
```

```python
from contextlib import ExitStack

import numpy as np

import concourse.bass as bass
from concourse import mybir

F32 = mybir.dt.float32
F32R = mybir.dt.float32r
U8 = mybir.dt.uint8
ALU = mybir.AluOpType
ACT = mybir.ActivationFunctionType
AX = mybir.AxisListType.X

P = 128
D = 1024
KT = D // P
TP = 1024
NS, LS = 8, 8
TS = NS * LS
T = TP + TS
NT = TP // P
W = 512
FT = W // P
H = 4
FF = 4 * D
EPS = 1e-6
QSCALE = float(P) ** -0.5
CD, CC = 31, 3
CH = [(0, 364), (364, 728), (728, T)]
TT_ = [(i * P, min(i * P + P, T)) for i in range(NT + 1)]

SPLITS = dict(qa=0, fa=512, ia=1024, ga=1536, qb=2048, kb=2560, vb=3072, ob=3584, ig=4096, fg=4100,
              bc=4104, cc=4616, xc=5128, ad=5640, gd=6152, gates=6664)

R_CDW, R_CDB, R_LNG, R_LNB, R_CCW, R_NH, R_NM, R_LB = 0, 31, 32, 33, 34, 37, 38, 39
NPAR = 40

UNIT = KT * P
SLOTS = 2


def constants():
    m = np.arange(P)
    lv = np.zeros((P, 7, 64), np.float32)
    for i in range(7):
        s = 1 << i
        blocks = P // (2 * s)
        one = np.zeros((P, blocks, s), np.float32)
        for b in range(blocks):
            one[2 * s * b:2 * s * b + s, b, :] = 1
        lv[:, i, :] = one.reshape(P, 64)
    neg = np.where(m[:, None] <= m[None, :], 0.0, -1e30).astype(np.float32)
    k = np.arange(TS)
    same = (k[:, None] // LS == k[None, :] // LS) & (k[:, None] <= k[None, :])
    negs = np.full((P, TS), -1e30, np.float32)
    negs[:TS] = np.where(same, 0.0, -1e30)
    bm = np.zeros((P, NS), np.float32)
    bm[:TS] = (k[:, None] // LS == np.arange(NS)[None, :])
    sel = np.zeros((P, H, P), np.float32)
    for h in range(H):
        sel[h, h] = 1.0
    keep = np.ones((P, T), np.float32)
    keep[:, 0:TP:P] = 0.0
    keep[:, TP::LS] = 0.0
    f = np.concatenate([np.eye(P, dtype=np.float32), neg, negs, bm, sel.reshape(P, H * P),
                        np.ones((P, P), np.float32)], axis=1)
    return lv.reshape(P, 7 * 64), np.ascontiguousarray(f), np.ascontiguousarray(keep[:4])


class Unit:
    def __init__(self, kind, idx, name):
        self.kind, self.idx, self.name = kind, idx, name


def plan():
    units = []

    def unit(kind, name, idx):
        units.append((kind, name, idx))
        return len(units) - 1

    def groups(u):
        kind = units[u][0]
        n = 9 if kind == "tok" else 3
        out = []
        for g in range(n):
            out += [("half", u, g, 0), ("half", u, g, 1)]
        return out

    conv = []
    for t in range(FT):
        conv += [("tap", t, j) for j in range(CD)]
    items = []
    seen_ad = 0
    count = [0]

    def pace(it, tiles):
        if it[3] == 1:
            count[0] += 1
            for _ in range(2 + count[0] % 2):
                if conv and conv[0][1] < tiles:
                    items.append(conv.pop(0))

    for t in range(FT):
        for nm in ("gd", "ad"):
            for it in groups(unit("feat", nm, t)):
                items.append(it)
                pace(it, seen_ad)
        seen_ad += 1
    for t in range(FT):
        for nm in ("cc", "xc", "bc"):
            for it in groups(unit("feat", nm, t)):
                items.append(it)
                pace(it, FT)
            if nm == "xc":
                items.append(("short", t))
    items += conv
    items.append(("states_cd",))
    items.append(("ln",))

    def merge(a, b):
        a, b, out = list(a), list(b), []
        na, nb, used = len(a), len(b), 0
        for i, item in enumerate(a):
            out.append(item)
            while used < nb and used * na <= i * nb:
                out.append(b[used])
                used += 1
        return out + b[used:]

    def branch(x, names, vname, stages):
        def heads(h):
            return [i for nm in names for i in groups(unit("feat", nm, h))]

        def value(p):
            return groups(unit("tok", vname, 2 * p)) + groups(unit("tok", vname, 2 * p + 1))

        def rec(h):
            return [("rec", x, s, h) for s in stages]
        out = value(0)
        if x == "B":
            out += [("rows_out",)]
        out += heads(0)
        out += [("rec", x, "prep", 0)] + merge(heads(1), rec(0))
        out += [("rec", x, "prep", 1)] + merge(heads(2), rec(1))
        out += value(1)
        out += [("rec", x, "prep", 2)] + merge(heads(3), rec(2))
        out += [("rec", x, "prep", 3)] + rec(3)
        return out

    items.append(("phase", 0))
    items += branch("A", ("qa", "fa", "ga"), "ia", ["lv%d" % i for i in range(8)] +
                    ["turn", "state", "out", "norm", "gate"])
    items.append(("phase", 1))
    items += groups(unit("if", "if", 0))
    items.append(("rows",))
    items += branch("B", ("qb", "kb", "ob"), "vb", ["decay", "score", "turn", "state", "out", "norm", "gate"])
    items.append(("phase", 2))
    return units, items


UNITS, ITEMS = plan()
NU = len(UNITS)
IF_U = [k for k, _, _ in UNITS].index("if")
FILLS = [0]
for _k, _n, _i in UNITS:
    FILLS.append(FILLS[-1] + (3 if _k == "tok" else 1))
GROUPS = [0]
for _k, _n, _i in UNITS:
    GROUPS.append(GROUPS[-1] + (9 if _k == "tok" else 3))
M_U, M_B, M_G = NU, FILLS[-1], GROUPS[-1]
M_UN, M_BN, M_GN = 12, 16, 48
M_IT = 4
O_U, O_B, O_G = M_U + M_IT * M_UN, M_B + M_IT * M_BN, M_G + M_IT * M_GN
O_UN, O_BN, O_GN, O_IT = 4, 12, 36, 2
L_U, L_B, L_G = O_U + O_IT * O_UN, O_B + O_IT * O_BN, O_G + O_IT * O_GN
L_UN, L_BN, L_GN, L_IT = 8, 16, 48, 8
ALL_U = L_U + L_IT * L_UN
C_ID, C_NEG, C_NEGS, C_BM, C_SEL, C_ONE = 0, 128, 256, 320, 328, 840
NCON = 968


def build(nc, a, o, scratch):
    with ExitStack() as top:
        top.enter_context(nc.allow_non_contiguous_dma(reason="a few columns of states and biases"))

        def sb(stack, name, shape, dt=F32):
            return stack.enter_context(nc.sbuf_tensor(name, shape, dt))

        sems = {}

        def sem(name):
            if name not in sems:
                sems[name] = top.enter_context(nc.semaphore(name))
            return sems[name]

        h_hi = sb(top, "h_hi", [P, KT, T], F32R)
        h_lo = sb(top, "h_lo", [P, KT, T], F32R)
        w_raw = sb(top, "w_raw", [P, SLOTS, UNIT])
        w_hi = sb(top, "w_hi", [P, SLOTS, UNIT], F32R)
        w_lo = sb(top, "w_lo", [P, SLOTS, UNIT], F32R)
        con = sb(top, "con", [P, NCON])
        lvm = sb(top, "lvm", [P, 7, 512], U8)
        par = sb(top, "par", [P, FT, NPAR])
        nrm = sb(top, "nrm", [P, 16])
        biases = sb(top, "biases", [H, 2])
        lbt = sb(top, "lbt", [P, 4, FT])
        ss = sb(top, "ss", [P, 16])
        rs = sb(top, "rs", [P, 16])
        mhalf = sb(top, "mhalf", [P, 16])
        acc = top.enter_context(nc.psum_tensor("acc", [P, 3, 512], F32))
        pz = top.enter_context(nc.psum_tensor("pz", [P, 5, 512], F32))
        ident = con[:, C_ID:C_ID + P]
        negm = con[:, C_NEG:C_NEG + P]
        negs = con[0:TS, C_NEGS:C_NEGS + TS]
        bmask = con[0:TS, C_BM:C_BM + NS]
        ones = con[:, C_ONE:C_ONE + P]

        def sel(h):
            return con[0:H, C_SEL + h * P:C_SEL + h * P + P]

        with ExitStack() as st:
            xin = sb(st, "xin", [P, NT + 1, D])
            xt = sb(st, "xt", [P, 2, D])
            junk0 = sb(st, "junk0", [P, 2, D])
            full0 = sb(st, "full0", [P, 4, 512])
            prow = sb(st, "prow", [NPAR, W])
            nrow = sb(st, "nrow", [16, P])
            lvf = sb(st, "lvf", [P, 7, 64])
        with ExitStack() as st:
            e_d = sb(st, "e_d", [P, FT, TP + CD - 1])
            e_ds = sb(st, "e_ds", [P, FT, NS, LS + CD - 1])
            y_d = sb(st, "y_d", [P, FT, T])
            sg_d = sb(st, "sg_d", [P, T])
            e_c = sb(st, "e_c", [P, TP + CC - 1])
            e_cs = sb(st, "e_cs", [P, NS, LS + CC - 1])
            e_cs_old = sb(st, "e_cs_old", [P, FT, NS, CC - 1])
            y_c = sb(st, "y_c", [P, T])
            o_c = sb(st, "o_c", [P, T])
            bufd = sb(st, "bufd", [120, 2, W])
            bufc = sb(st, "bufc", [16, W])
            taild = sb(st, "taild", [P, W])
            tailc = sb(st, "tailc", [P, W])
            endc = sb(st, "endc", [P, FT, P])
            endd = sb(st, "endd", [P, FT, P])
            ln_t = sb(st, "ln_t", [P, T])
            ln_r = sb(st, "ln_r", [P, T])
        with ExitStack() as st:
            va = sb(st, "va", [P, NT + 1, 256])
            qa = sb(st, "qa", [P, 2, T])
            ka = sb(st, "ka", [P, 2, T])
            fa = sb(st, "fa", [P, 2, T])
            ga = sb(st, "ga", [P, 2, T])
            sga = sb(st, "sga", [P, 2, T])
            tree = sb(st, "tree", [P, T])
            sa = sb(st, "sa", [P, (NT + 1) * P])
            kta = sb(st, "kta", [P, NT + 1, P])
            sta = sb(st, "sta", [P, NT, P])
            s0a = sb(st, "s0a", [P, NS, P])
            sna = sb(st, "sna", [P, NS, P])
            qza = sb(st, "qza", [P, NS * (TS + LS)])
            sqa = sb(st, "sqa", [P, NT + 1, P])
            vza = sb(st, "vza", [TS, NS, P])
            ota = sb(st, "ota", [P, NT + 1, P])
        with ExitStack() as st:
            vb = sb(st, "vb", [P, NT + 1, 2, P + 2])
            qb = sb(st, "qb", [P, 2, T])
            kb = sb(st, "kb", [P, 2, T])
            gb = sb(st, "gb", [P, 2, T])
            wb = sb(st, "wb", [P, (NT + 1) * P])
            qs = sb(st, "qs", [P, T])
            ktb = sb(st, "ktb", [P, NT + 1, P])
            cnb = sb(st, "cnb", [P, NT, P + 2])
            c0b = sb(st, "c0b", [P, NS, P + 2])
            cnew = sb(st, "cnew", [P, NS, P + 2])
            qzb = sb(st, "qzb", [P, NS * (TS + LS)])
            sqb = sb(st, "sqb", [P, NT + 1, P])
            mp = sb(st, "mp", [H, 16])
            nlast = sb(st, "nlast", [H, 16])
            vzb = sb(st, "vzb", [TS, NS, P])
            otb = sb(st, "otb", [P, NT + 1, P])
            den = sb(st, "den", [P, 16])
            nM = sb(st, "nM", [H, T])
            wint = sb(st, "wint", [H, T])
            cdr = sb(st, "cdr", [H, 16])
            cdc = sb(st, "cdc", [P, H, 16])
            cols = sb(st, "cols", [P, NT + 1, P])
            m0 = sb(st, "m0", [H, 16])
            mrow = sb(st, "mrow", [H, T])
            keepr = sb(st, "keepr", [H, T])
            irow = qb[0:H, 0, :]
            frow = qb[0:H, 1, :]
            brow = kb[0:H, 0, :]
            arow = kb[0:H, 1, :]
            trow = gb[0:H, 0, :]
            urow = gb[0:H, 1, :]
            rt = wb[:, 0:T]
        with ExitStack() as st:
            b_hi = sb(st, "b_hi", [P, FT, T], F32R)
            b_lo = sb(st, "b_lo", [P, FT, T], F32R)
            b_raw = sb(st, "b_raw", [P, 2, T])
            gsig = sb(st, "gsig", [P, 2, T])
            gtmp = sb(st, "gtmp", [P, 2, 364])
            merged = sb(st, "merged", [P, KT, T])
        with ExitStack() as st:
            x1 = sb(st, "x1", [P, NT + 1, D])
            u_hi = sb(st, "u_hi", [P, FT, T], F32R)
            u_lo = sb(st, "u_lo", [P, FT, T], F32R)
            ur = sb(st, "ur", [P, 2, 364])
            uu = sb(st, "uu", [P, 2, 364])
            full1 = sb(st, "full1", [P, 4, 512])
            xt1 = sb(st, "xt1", [P, 2, D])
            junk1 = sb(st, "junk1", [P, 2, D])
            gfin = sb(st, "gfin", [P, D])

        x_tiles = [a["x_prompt"][0, i * P:(i + 1) * P, :] for i in range(NT)] + \
                  [a["x_sample"].rearrange("b t d -> (b t) d")]
        y_tiles = [o["y_p"][0, i * P:(i + 1) * P, :] for i in range(NT)] + \
                  [o["y_s"].rearrange("b t d -> (b t) d")]
        rows_of = [P] * NT + [TS]
        w_in = a["w_in"][0]
        w_branch = a["w_branch"].rearrange("l n c d -> (l n c) d")
        w_down = a["w_down"].rearrange("l f d -> (l f) d")

        def unit_source(kind, name, idx):
            c = SPLITS[name] if name in SPLITS else 0
            if kind == "feat":
                return w_in[:, c + idx * P:c + (idx + 1) * P].rearrange("(k p) n -> p k n", p=P)
            p_, half = idx // 2, idx % 2
            return w_in[half * 512:half * 512 + 512, c + p_ * 256:c + p_ * 256 + 256] \
                .rearrange("(k p) n -> p k n", p=P)

        w_loaded = [sem(f"w_loaded{s}") for s in range(SLOTS)]
        hi_ready, w_ready = sem("hi_ready"), sem("w_ready")
        unit_used, group_ready = sem("unit_used"), sem("group_ready")
        acc_free = [sem(f"acc_free{b}") for b in range(3)]
        consts_in, params_in, x_in = sem("consts_in"), sem("params_in"), [sem(f"x_in{i}") for i in range(NT + 1)]

        def load_c0(sp, h):
            sp.dma_start(c0b[:, :, 0:P], a["state_mlstm_c"][0, :, h].rearrange("b d v -> d b v")) \
                .then_inc(sem("c0_in"), 16)
            sp.dma_start(c0b[:, :, P:P + 1], a["state_mlstm_n"][0, :, h].rearrange("b (d a) -> d b a", a=1)) \
                .then_inc(sem("c0_in"), 16)

        def full_of(full, i, hh):
            return full[:, 2 * (i % 2) + hh, :].rearrange("p (k n) -> p k n", k=4)[:, :, 0:rows_of[i]]

        block = top.enter_context(nc.Block())
        NAMES = ("pe", "act", "pool", "dve", "sp")

        def phase_end(eng, me, n):
            if me != "sp":
                eng.drain().then_inc(sem("phase_" + me), 1)
            else:
                eng.nop().then_inc(sem("phase_sp"), 1)
            for x in NAMES:
                if x != me and not (x == "sp" and n > 4):
                    eng.wait_ge(sem("phase_" + x), n)

        @block.sync
        def _(sp):
            def unit_load(u):
                kind, name, idx = UNITS[u]
                s = u % SLOTS
                if u >= SLOTS:
                    sp.wait_ge(w_ready, u - SLOTS + 1)
                dst = w_raw[:, s, :]
                if kind == "if":
                    d4 = dst.rearrange("p (k n) -> p k n", k=KT)
                    sp.dma_start(d4[:, :, 0:8], w_in[:, SPLITS["ig"]:SPLITS["ig"] + 8]
                                 .rearrange("(k p) n -> p k n", p=P)).then_inc(w_loaded[s], 16)
                else:
                    k = KT if kind == "feat" else 4
                    sp.dma_start(dst.rearrange("p (k n) -> p k n", k=k),
                                 unit_source(kind, name, idx)).then_inc(w_loaded[s], 16)

            for i in range(NT + 1):
                sp.dma_start(xin[0:rows_of[i], i, :], x_tiles[i]).then_inc(x_in[i], 16)
                if i == 0:
                    sp.dma_start(con[:, :], a["con"]).then_inc(consts_in, 16)
            unit_load(0)
            unit_load(1)
            phase_end(sp, "sp", 1)
            for j in range(2):
                sp.dma_start(bufd[:, j, :], a["state_conv_conformer"][0, 4 * j:4 * j + 4]
                             .rearrange("b t c -> (b t) c")).then_inc(sem("buf_in"), 16)
            sp.dma_start(bufc[:, :], a["state_conv_short"][0].rearrange("b t c -> (b t) c")).then_inc(sem("buf_in"), 16)
            out_sem = sem("stored")
            n_out = [0]

            def store(dst, src):
                sp.dma_start(dst, src).then_inc(out_sem, 16)
                n_out[0] += 16

            store(o["cd_s"][0, :, 0:CD - 1 - LS, :], a["state_conv_conformer"][0, :, LS:CD - 1, :])

            nxt = 2
            for it in ITEMS:
                if it[0] == "half" and it[2] == 0 and it[3] == 0 and nxt < NU and nxt <= it[1] + 2:
                    unit_load(nxt)
                    nxt += 1
                elif it[0] == "half" and it[3] == 1 and it[2] == 2 and UNITS[it[1]][1] == "bc":
                    t = UNITS[it[1]][2]
                    sp.wait_ge(sem("oc_done"), 3 * t + 3)
                    store(scratch[2, t], o_c[:, :])
                    sp.wait_ge(out_sem, n_out[0])
                    sp.nop().then_inc(sem("oc_stored"), 1)
                elif it[0] == "states_cd":
                    sp.wait_ge(sem("tails_done"), 2)
                    for b in range(NS):
                        store(o["cc_s"][0, b], tailc[64 + 8 * b + LS - CC + 1:64 + 8 * b + 8, :])
                        store(o["cd_s"][0, b, CD - 1 - LS:, :], taild[64 + 8 * b:64 + 8 * b + 8, :])
                    store(o["cc_p"][0, 0], tailc[64 - CC + 1:64, :])
                    store(o["cd_p"][0, 0], taild[64 - CD + 1:64, :])
                elif it[0] == "ln":
                    for t in range(FT):
                        sp.wait_ge(sem("od_done"), t + 1)
                        store(scratch[3, t], y_d[:, t, :])
                    sp.wait_ge(out_sem, n_out[0])
                    phase_end(sp, "sp", 2)
                    sp.dma_start(s0a[:, :, :], a["state_hgrn"][0, :, 0].rearrange("b d v -> d b v")) \
                        .then_inc(sem("s0_in"), 16)
                elif it[0] == "rec" and it[2] == "gate":
                    x, h = it[1], it[3]
                    if x == "A":
                        sp.wait_ge(sem("a_gated"), h + 1)
                        store(scratch[0, h], ga[:, h % 2, :])
                        store(o["hg_p"][0, 0, h], sta[:, NT - 1, :])
                        store(o["hg_s"][0, :, h].rearrange("b d v -> d b v"), sna[:, :, :])
                        if h + 1 < H:
                            sp.dma_start(s0a[:, :, :], a["state_hgrn"][0, :, h + 1].rearrange("b d v -> d b v")) \
                                .then_inc(sem("s0_in"), 16)
                        sp.wait_ge(out_sem, n_out[0])
                        sp.nop().then_inc(sem("a_stored"), 1)
                        if h == H - 1:
                            phase_end(sp, "sp", 3)
                            sp.dma_start(m0[:, 0:NS], a["state_mlstm_m"][0].rearrange("b h -> h b")) \
                                .then_inc(sem("m0_in"), 16)
                            sp.dma_start(keepr[:, :], a["keep"]).then_inc(sem("m0_in"), 16)
                            load_c0(sp, 0)
                    else:
                        sp.wait_ge(sem("b_gated"), h + 1)
                        store(scratch[1, h], gb[:, h % 2, :])
                        store(o["mc_p"][0, 0, h], cnb[:, NT - 1, 0:P])
                        store(o["mn_p"][0, 0, h].rearrange("(d a) -> d a", a=1), cnb[:, NT - 1, P:P + 1])
                        store(o["mc_s"][0, :, h].rearrange("b d v -> d b v"), cnew[:, :, 0:P])
                        store(o["mn_s"][0, :, h].rearrange("b (d a) -> d b a", a=1), cnew[:, :, P:P + 1])
                        if h + 1 < H:
                            load_c0(sp, h + 1)
                        sp.wait_ge(out_sem, n_out[0])
                        sp.nop().then_inc(sem("b_stored"), 1)
                elif it[0] == "rows":
                    sp.wait_ge(sem("m_done"), 1)
                    store(o["mm_p"][0].rearrange("a h -> h a"), mrow[:, TP - 1:TP])
                    store(o["mm_s"][0].rearrange("b h -> h b"),
                          mrow[:, TP:T].rearrange("h (b t) -> h b t", t=LS)[:, :, LS - 1])
            sp.wait_ge(out_sem, n_out[0])
            sp.nop().then_inc(sem("phase_sp"), 1)

            def loop_load(base, i, n, s, dst, src):
                sp.wait_ge(w_ready, base + i * n + s - SLOTS + 1)
                sp.dma_start(dst, src).then_inc(w_loaded[(base + s) % SLOTS], 16)

            def raw(u, k):
                return w_raw[:, u % SLOTS, :].rearrange("p (k n) -> p k n", k=k)

            with sp.Fori(0, M_IT) as i:
                for s in range(M_UN):
                    pair, j = s // 3, s % 3
                    if j < 2:
                        loop_load(M_U, i, M_UN, s, raw(M_U + s, KT),
                                  w_in[:, bass.ds(i * D + SPLITS["gates"] + (2 * pair + j) * P, P)]
                                  .rearrange("(k p) n -> p k n", p=P))
                    else:
                        loop_load(M_U, i, M_UN, s, raw(M_U + s, FT),
                                  w_branch[bass.ds(i * W, W), pair * 256:(pair + 1) * 256]
                                  .rearrange("(k p) n -> p k n", p=P))
            with sp.Fori(0, O_IT) as i:
                for s in range(O_UN):
                    loop_load(O_U, i, O_UN, s, raw(O_U + s, 2),
                              a["w_out"][0, s * 256:(s + 1) * 256, bass.ds(i * 512, 512)]
                              .rearrange("(k p) n -> p k n", p=P))
            with sp.Fori(0, L_IT) as i:
                for s in range(4):
                    loop_load(L_U, i, L_UN, s, raw(L_U + s, KT),
                              a["w_up"][0, :, bass.ds(i * 512 + s * P, P)].rearrange("(k p) n -> p k n", p=P))
                for s in range(4):
                    loop_load(L_U, i, L_UN, 4 + s, raw(L_U + s, 2),
                              w_down[bass.ds(i * 512 + (s // 2) * 256, 256), (s % 2) * 512:(s % 2 + 1) * 512]
                              .rearrange("(k p) n -> p k n", p=P))
            sp.wait_ge(w_ready, ALL_U - SLOTS + 1)
            sp.dma_start(raw(ALL_U, KT), a["w_up"][0, :, 0:P].rearrange("(k p) n -> p k n", p=P)) \
                .then_inc(w_loaded[ALL_U % SLOTS], 16)
            for i in range(NT + 1):
                sp.wait_ge(sem("y_done"), i + 1)
                store(y_tiles[i], x1[0:rows_of[i], i, :])
            sp.wait_ge(out_sem, n_out[0])

        @block.tensor
        def _(pe):
            def product(out, lh, ll, rh, rl, first, last):
                pe.matmul(out, lh, rh, start=first, stop=False)
                pe.matmul(out, lh, rl, start=False, stop=False)
                return pe.matmul(out, ll, rh, start=False, stop=last)

            def w_tile(w, s, k, c0, c1, nk=KT):
                return w[:, s, :].rearrange("p (k n) -> p k n", k=nk)[:, k, c0:c1]

            def feat_mm(s, g, ks, src_hi, src_lo, nk=KT, col=0):
                c0, c1 = CH[g]
                for k in ks:
                    mm = product(acc[:, g, 0:c1 - c0], w_tile(w_hi, s, k, col, col + P, nk),
                                 w_tile(w_lo, s, k, col, col + P, nk),
                                 src_hi[:, k, c0:c1], src_lo[:, k, c0:c1], k == 0, k == nk - 1)
                return mm

            def wide_mm(s, i, src_hi, src_lo, k0):
                t0, t1 = TT_[i]
                for k in range(2):
                    mm = product(acc[0:t1 - t0, i % 3, :], src_hi[:, k0 + k, t0:t1], src_lo[:, k0 + k, t0:t1],
                                 w_tile(w_hi, s, k, 0, 512, 2), w_tile(w_lo, s, k, 0, 512, 2), k == 0, k == 1)
                return mm

            def tok_mm(s, i, ks, src_hi, src_lo, k0=0):
                t0, t1 = TT_[i]
                for k in ks:
                    mm = product(acc[0:t1 - t0, i % 3, 0:256], src_hi[:, k0 + k, t0:t1], src_lo[:, k0 + k, t0:t1],
                                 w_tile(w_hi, s, k, 0, 256, 4), w_tile(w_lo, s, k, 0, 256, 4), k == 0, k == 3)
                return mm

            pe.wait_ge(params_in, 16 * 10)
            pe.wait_ge(consts_in, 16 * 4)
            for t in range(FT):
                pe.transpose(pz[:, 0, t * NPAR:(t + 1) * NPAR], prow[:, t * P:(t + 1) * P], ident[0:NPAR, 0:NPAR])
            pe.transpose(pz[:, 0, FT * NPAR:FT * NPAR + 16], nrow[:, :], ident[0:16, 0:16]) \
                .then_inc(sem("params_turned"), 1)

            def turn_tokens(src, pre, scaled, base):
                for i in range(NT + 1):
                    n = rows_of[i]
                    pe.wait_ge(sem(scaled), i + 1)
                    for hh in range(2):
                        if i >= 2:
                            pe.wait_ge(sem(pre + "_full"), 2 * i + hh - 3)
                        for k in range(4):
                            tr = pe.transpose(pz[:, 1 + 2 * (i % 2) + hh, k * P:k * P + n],
                                              src[0:n, i % 2, (4 * hh + k) * P:(4 * hh + k + 1) * P],
                                              ident[0:n, 0:n])
                        tr.then_inc(sem(pre + "_turned"), 1)

            turn_tokens(xt, "x", "x_scaled", 0)
            phase_end(pe, "pe", 1)
            pe.wait_ge(sem("buf_in"), 16 * 3)
            for j in range(2):
                for t in range(FT):
                    pe.transpose(pz[:, j, t * 120:t * 120 + 120], bufd[:, j, t * P:(t + 1) * P], ident[0:120, 0:120])
            for t in range(FT):
                tr = pe.transpose(pz[:, 2, t * 16:t * 16 + 16], bufc[:, t * P:(t + 1) * P], ident[0:16, 0:16])
            tr.then_inc(sem("bufs_turned"), 1)

            def rec_a(s, h):
                b2 = h % 2
                q, k = qa[:, b2, :], ka[:, b2, :]
                hc = (h % 2) * P
                if s == "prep":
                    return
                if s.startswith("lv"):
                    lv = int(s[2:])
                    if lv == 0:
                        pe.wait_ge(sem("a_prep"), h + 1)
                        if h >= 1:
                            pe.wait_ge(sem("a_gated"), h)
                        for c in range(NT):
                            pe.matmul(pz[:, c // 4, (c % 4) * P:(c % 4 + 1) * P], k[:, c * P:(c + 1) * P],
                                      q[:, c * P:(c + 1) * P], start=True, stop=True)
                        pe.matmul(pz[0:TS, 2, 0:TS], k[:, TP:T], q[:, TP:T], start=True, stop=True) \
                            .then_inc(sem("a_scored"), 1)
                        return
                    sz = 1 << (lv - 1)
                    if lv == 1:
                        pe.wait_ge(sem("a_q1"), h + 1)
                    else:
                        pe.wait_ge(sem("a_lv"), 7 * h + lv - 1)
                    q = sga[:, b2, :]
                    if lv >= 2:
                        pe.wait_ge(sem("a_masked"), 8 * h + lv - 1)
                    bank, sbank = (3, 4) if lv % 2 else (0, 2)
                    for c in range(NT):
                        qo = q[:, c * P:(c + 1) * P].rearrange("p (b two s) -> p b two s", two=2, s=sz)[:, :, 1, :]
                        mm = pe.matmul(pz[:, bank, c * 64:(c + 1) * 64].rearrange("p (b s) -> p b s", s=sz),
                                       k[:, c * P:(c + 1) * P], qo, start=True, stop=True)
                    if lv <= 3:
                        qo = q[:, TP:T].rearrange("p (b two s) -> p b two s", two=2, s=sz)[:, :, 1, :]
                        mm = pe.matmul(pz[0:TS, sbank, 0:32].rearrange("p (b s) -> p b s", s=sz),
                                       k[:, TP:T], qo, start=True, stop=True)
                    mm.then_inc(sem("a_scored"), 1)
                elif s == "turn":
                    pe.wait_ge(sem("a_lv"), 7 * h + 7)
                    pe.wait_ge(sem("a_masked"), 8 * h + 8)
                    for c in range(NT):
                        pe.transpose(pz[:, c // 4, (c % 4) * P:(c % 4 + 1) * P], k[:, c * P:(c + 1) * P], ident)
                    pe.transpose(pz[0:TS, 2, 0:P], k[:, TP:T], ident).then_inc(sem("a_kturned"), 1)
                elif s == "state":
                    pe.wait_ge(sem("a_kt"), h + 1)
                    for c in range(NT):
                        pe.matmul(pz[:, 3 + c // 4, (c % 4) * P:(c % 4 + 1) * P], kta[:, c, :],
                                  va[:, c, hc:hc + P], start=True, stop=True)
                    pe.wait_ge(sem("a_vz"), h + 1)
                    for j in range(2):
                        mm = pe.matmul(pz[:, j, :], kta[0:TS, NT, :],
                                       vza[:, 4 * j:4 * j + 4, :].rearrange("p b v -> p (b v)"),
                                       start=True, stop=True)
                    mm.then_inc(sem("a_updates"), 1)
                elif s == "out":
                    pe.wait_ge(sem("a_states"), h + 1)
                    q = sga[:, b2, :]
                    pe.wait_ge(sem("a_qz"), h + 1)
                    for c in range(NT):
                        bk = 2 if c < 4 else 3
                        ov = pz[:, bk, (c % 4) * P:(c % 4 + 1) * P]
                        pe.matmul(ov, sa[:, c * P:(c + 1) * P], va[:, c, hc:hc + P], start=True, stop=c == 0)
                        if c:
                            pe.matmul(ov, q[:, c * P:(c + 1) * P], sta[:, c - 1, :], start=False, stop=True)
                    pe.matmul(pz[0:TS, 4, 0:P], sa[0:TS, TP:T], va[0:TS, NT, hc:hc + P], start=True, stop=False)
                    for b in range(NS):
                        mm = pe.matmul(pz[0:TS, 4, 0:P], qza[:, b * TS:(b + 1) * TS], s0a[:, b, :], start=False, stop=b == NS - 1)
                    mm.then_inc(sem("a_out"), 1)
                elif s == "norm":
                    return
                elif s == "gate":
                    turn_out("a", ota, h)

            def turn_out(x, ot, h):
                pe.wait_ge(sem(x + "_normed"), h + 1)
                for c in range(NT + 1):
                    n = rows_of[c]
                    tr = pe.transpose(pz[:, c // 4, (c % 4) * P:(c % 4) * P + n], ot[0:n, c, :], ident[0:n, 0:n])
                tr.then_inc(sem(x + "_turned"), 1)

            def rec_b(s, h):
                b2 = h % 2
                q, k = qb[:, b2, :], kb[:, b2, :]
                v1 = vb[:, :, h % 2, :]
                if s == "prep":
                    return
                if s == "decay":
                    if h >= 1:
                        pe.wait_ge(sem("b_gated"), h)
                    pe.wait_ge(sem("b_rows"), 1)
                    for j, (c0, c1) in enumerate(((0, 512), (512, 1024), (1024, T))):
                        pe.matmul(pz[:, j, 0:c1 - c0], sel(h), nM[:, c0:c1], start=True, stop=True)
                    for j, (c0, c1) in enumerate(((0, 512), (512, 1024))):
                        pe.matmul(pz[:, 3 + j, :], sel(h), wint[:, c0:c1], start=True, stop=True)
                    pe.matmul(pz[:, 2, 64:128], sel(h), wint[:, TP:T], start=True, stop=True) \
                        .then_inc(sem("b_spread"), 1)
                elif s == "score":
                    pe.wait_ge(sem("b_decayed"), h + 1)
                    pe.wait_ge(sem("b_proj"), 9 * h + 9)
                    for c in range(NT):
                        pe.matmul(pz[:, c // 4, (c % 4) * P:(c % 4 + 1) * P], k[:, c * P:(c + 1) * P],
                                  q[:, c * P:(c + 1) * P], start=True, stop=True)
                    pe.matmul(pz[0:TS, 2, 0:TS], k[:, TP:T], q[:, TP:T], start=True, stop=True) \
                        .then_inc(sem("b_scored"), 1)
                elif s == "turn":
                    for c in range(NT):
                        pe.transpose(pz[:, 3 + c // 4, (c % 4) * P:(c % 4 + 1) * P], k[:, c * P:(c + 1) * P], ident)
                    pe.wait_ge(sem("b_weighted"), h + 1)
                    pe.transpose(pz[0:TS, 2, 128:128 + P], k[:, TP:T], ident).then_inc(sem("b_kturned"), 1)
                elif s == "state":
                    pe.wait_ge(sem("b_kt"), h + 1)
                    for c in range(NT):
                        pe.matmul(pz[:, (0, 1, 3)[c // 3], (c % 3) * 129:(c % 3) * 129 + 129], ktb[:, c, :],
                                  v1[:, c, 0:P + 1], start=True, stop=True)
                    pe.wait_ge(sem("b_vz"), h + 1)
                    for j, bk in enumerate((2, 4)):
                        pe.matmul(pz[:, bk, :], ktb[0:TS, NT, :],
                                  vzb[:, 4 * j:4 * j + 4, :].rearrange("p b v -> p (b v)"), start=True, stop=True)
                    pe.matmul(pz[:, 3, 400:400 + NS], ktb[0:TS, NT, :], bmask, start=True, stop=True) \
                        .then_inc(sem("b_updates"), 1)
                elif s == "out":
                    pe.wait_ge(sem("b_states"), h + 1)
                    pe.wait_ge(sem("b_qz"), h + 1)
                    for c in range(NT):
                        ov = pz[:, (0, 1, 3)[c // 3], (c % 3) * 129:(c % 3) * 129 + 129]
                        pe.matmul(ov, wb[:, c * P:(c + 1) * P], v1[:, c, 0:P + 1], start=True, stop=c == 0)
                        if c:
                            pe.matmul(ov, qs[:, c * P:(c + 1) * P], cnb[:, c - 1, 0:P + 1], start=False, stop=True)
                    ov = pz[0:TS, 3, 258:258 + 129]
                    pe.matmul(ov, wb[0:TS, TP:T], v1[0:TS, NT, 0:P + 1], start=True, stop=False)
                    for b in range(NS):
                        mm = pe.matmul(ov, qzb[:, b * TS:(b + 1) * TS], c0b[:, b, 0:P + 1], start=False, stop=b == NS - 1)
                    mm.then_inc(sem("b_out"), 1)
                elif s == "gate":
                    turn_out("b", otb, h)

            for it in ITEMS:
                if it[0] == "half":
                    _, u, g, hf = it
                    kind, name, idx = UNITS[u]
                    if g == 0 and hf == 0:
                        pe.wait_ge(w_ready, u + 1)
                    fill = FILLS[u] + (g // 3 if kind == "tok" else 0)
                    if hf == 0 and fill:
                        pe.wait_ge(acc_free[g % 3], fill)
                    if kind == "tok":
                        mm = tok_mm(u % 2, g, (0, 1) if hf == 0 else (2, 3), h_hi, h_lo, 4 * (idx % 2))
                    else:
                        mm = feat_mm(u % 2, g, range(0, 4) if hf == 0 else range(4, 8), h_hi, h_lo)
                    if hf == 1:
                        mm.then_inc(group_ready, 1)
                elif it[0] == "states_cd":
                    pe.wait_ge(sem("ends_ready"), 8)
                    for t in range(FT):
                        pe.transpose(pz[:, 0, t * P:(t + 1) * P], endd[:, t, :], ident)
                        tr = pe.transpose(pz[:, 1, t * P:(t + 1) * P], endc[:, t, :], ident)
                    tr.then_inc(sem("ends_turned"), 1)
                elif it[0] == "ln":
                    pe.wait_ge(sem("tails_done"), 2)
                    pe.wait_ge(sem("conv_done"), FT)
                    for rnd in range(2):
                        if rnd:
                            pe.wait_ge(sem("ln_centred"), FT)
                        for t in range(FT):
                            if rnd:
                                pe.wait_ge(sem("ln_squared"), t + 1)
                            for j, (c0, c1) in enumerate(((0, 512), (512, 1024), (1024, T))):
                                src = (ln_t[:, c0:c1] if t % 2 == 0 else ln_r[:, c0:c1]) if rnd else y_d[:, t, c0:c1]
                                mm = pe.matmul(pz[:, j, 0:c1 - c0], ones, src, start=t == 0, stop=t == FT - 1)
                            if rnd:
                                mm.then_inc(sem("ln_var"), 1)
                        if not rnd:
                            mm.then_inc(sem("ln_mean"), 1)
                    phase_end(pe, "pe", 2)
                elif it[0] == "phase":
                    if it[1]:
                        phase_end(pe, "pe", it[1] + 2)
                elif it[0] == "rows_out":
                    pe.wait_ge(sem("rows_ready"), 1)
                    for c in range(NT + 1):
                        n = rows_of[c]
                        tr = pe.transpose(pz[0:n, c // 4, (c % 4) * P:(c % 4 + 1) * P], rt[:, c * P:c * P + n], ident)
                    for h in range(H):
                        mm = pe.matmul(pz[:, 3, h * 16:h * 16 + 16], sel(h), cdr[:, :], start=True, stop=True)
                    mm.then_inc(sem("rows_turned"), 1)
                elif it[0] == "rec":
                    (rec_a if it[1] == "A" else rec_b)(it[2], it[3])

            with pe.Fori(0, M_IT) as i:
                for s in range(M_UN):
                    pair, j = s // 3, s % 3
                    pe.wait_ge(w_ready, M_U + 1 + s + i * M_UN)
                    if s == 2:
                        pe.wait_ge(sem("branch_ready"), i * FT + FT)
                    for r in range(2 if j == 2 else 1):
                        for g in range(3):
                            pe.wait_ge(acc_free[g], M_B + 4 * pair + j + r + i * M_BN)
                            if j < 2:
                                mm = feat_mm((M_U + s) % 2, g, range(KT), h_hi, h_lo)
                            else:
                                mm = feat_mm((M_U + s) % 2, g, range(FT), b_hi, b_lo, FT, r * P)
                            mm.then_inc(group_ready, 1)
            phase_end(pe, "pe", 5)
            with pe.Fori(0, O_IT) as i:
                for s in range(O_UN):
                    pe.wait_ge(w_ready, O_U + 1 + s + i * O_UN)
                    pe.wait_ge(sem("merged_low_a"), (2, 3, 4, 6)[s])
                    if s:
                        pe.wait_ge(sem("merged_low_b"), (0, 1, 2, 2)[s])
                    for c in range(NT + 1):
                        pe.wait_ge(acc_free[c % 3], O_B + s * 3 + c // 3 + i * O_BN)
                        wide_mm((O_U + s) % 2, c, h_hi, h_lo, 2 * s).then_inc(group_ready, 1)
            turn_tokens(xt1, "m", "m_scaled", 0)
            phase_end(pe, "pe", 6)
            with pe.Fori(0, L_IT) as i:
                for s in range(4):
                    pe.wait_ge(w_ready, L_U + 1 + s + i * L_UN)
                    for g in range(3):
                        pe.wait_ge(acc_free[g], L_B + s + i * L_BN)
                        feat_mm((L_U + s) % 2, g, range(KT), h_hi, h_lo).then_inc(group_ready, 1)
                for s in range(4):
                    pe.wait_ge(w_ready, L_U + 5 + s + i * L_UN)
                    if s % 2 == 0:
                        pe.wait_ge(sem("u_ready"), i * 12 + 3 * s + 8)
                    for c in range(NT + 1):
                        pe.wait_ge(acc_free[c % 3], L_B + 4 + s * 3 + c // 3 + i * L_BN)
                        wide_mm((L_U + s) % 2, c, u_hi, u_lo, 2 * (s // 2)).then_inc(group_ready, 1)


        @block.scalar
        def _(act):
            def copy(out, in_, **k):
                return act.activation(out, in_, ACT.Copy, **k)

            def split_hi(u):
                s = u % SLOTS
                act.wait_ge(w_loaded[s], 16 * (u // SLOTS + 1))
                if u >= SLOTS:
                    act.wait_ge(group_ready, GROUPS[u - 1])
                if u < NU and UNITS[u][0] == "if":
                    act.wait_ge(sem("if_zero"), 1)
                    raw4 = w_raw[:, s, :].rearrange("p (k n) -> p k n", k=KT)
                    hi4 = w_hi[:, s, :].rearrange("p (k n) -> p k n", k=KT)
                    copy(hi4[:, :, 0:4], raw4[:, :, 0:4])
                    copy(hi4[:, :, 32:36], raw4[:, :, 4:8]).then_inc(hi_ready, 1)
                else:
                    copy(w_hi[:, s, :], w_raw[:, s, :]).then_inc(hi_ready, 1)

            def split_hi_loop(base, gbase, i, n, gn, s, g_before):
                sl = (base + s) % SLOTS
                act.wait_ge(w_loaded[sl], 16 * ((base + s) // SLOTS + 1) + i * (16 * n // SLOTS))
                act.wait_ge(group_ready, gbase + g_before + i * gn)
                copy(w_hi[:, sl, :], w_raw[:, sl, :]).then_inc(hi_ready, 1)

            def norm_all(pre, src, junk, full, wait_in):
                for i in range(NT + 3):
                    if i <= NT:
                        n = rows_of[i]
                        wait_in(i)
                        if i >= 2:
                            act.wait_ge(sem(pre + "_sq"), i - 1)
                        act.activation(junk[0:n, i % 2, :], src(i), ACT.Square, accum_out=ss[0:n, i:i + 1]) \
                            .then_inc(sem(pre + "_sq"), 1)
                    if i >= 2:
                        t0, t1 = TT_[i - 2]
                        for hh in range(2):
                            act.wait_ge(sem(pre + "_full"), 2 * (i - 2) + hh + 1)
                            copy(h_hi[:, 4 * hh:4 * hh + 4, t0:t1], full_of(full, i - 2, hh)) \
                                .then_inc(sem(pre + "_hi"), 1)

            for nm, r0, n in (("conv_conformer_w", R_CDW, CD), ("conv_conformer_b", R_CDB, 1),
                              ("ln_conformer_g", R_LNG, 1), ("ln_conformer_b", R_LNB, 1),
                              ("conv_short_w", R_CCW, CC), ("norm_hgrn", R_NH, 1),
                              ("norm_mlstm", R_NM, 1), ("lb_logits", R_LB, 1)):
                act.dma_start(prow[r0:r0 + n, :], a[nm][0] if n > 1 else a[nm]).then_inc(params_in, 16)
            act.dma_start(nrow[0:8, :], a["norm_mix"][0].rearrange("(a b) -> a b", b=P)).then_inc(params_in, 16)
            act.dma_start(nrow[8:16, :], a["norm_mlp"][0].rearrange("(a b) -> a b", b=P)).then_inc(params_in, 16)
            act.dma_start(lvf[:, :, :].rearrange("p a b -> p (a b)"), a["lvm"]).then_inc(consts_in, 16)
            act.dma_start(biases[:, 0:1], a["mlstm_i_bias"].rearrange("a b -> b a")).then_inc(consts_in, 16)
            act.dma_start(biases[:, 1:2], a["mlstm_f_bias"].rearrange("a b -> b a")).then_inc(consts_in, 16)
            norm_all("x", lambda i: xin[0:rows_of[i], i, :], junk0, full0, lambda i: act.wait_ge(x_in[i], 16))
            act.wait_ge(sem("lb_diff"), 1)
            act.activation(lbt[:, 1, :], lbt[:, 0, :], ACT.Exp).then_inc(sem("lb_exp"), 1)
            split_hi(0)
            phase_end(act, "act", 1)

            def evac(u, g):
                kind, name, idx = UNITS[u]
                act.wait_ge(group_ready, GROUPS[u] + g + 1)
                if kind == "feat":
                    c0, c1 = CH[g]
                    src = acc[:, g, 0:c1 - c0]
                    if name == "gd":
                        if idx:
                            act.wait_ge(sem("glu_done"), 3 * (idx - 1) + g + 1)
                        act.activation(sg_d[:, c0:c1], src, ACT.Sigmoid).then_inc(acc_free[g], 1)
                        return
                    if name == "cc":
                        if idx and g == 0:
                            act.wait_ge(sem("short_done"), idx)
                            act.wait_ge(sem("ends_ready"), 4 + idx)
                        if g < 2:
                            copy(e_c[:, CC - 1 + c0:CC - 1 + c1], src).then_inc(acc_free[g], 1)
                        else:
                            copy(e_c[:, CC - 1 + c0:], acc[:, g, 0:TP - c0])
                            copy(e_cs[:, :, CC - 1:], acc[:, g, TP - c0:T - c0]
                                 .rearrange("p (b t) -> p b t", t=LS)).then_inc(acc_free[g], 1)
                        return
                    if name in ("xc", "bc", "ad"):
                        return
                    b2, bank = idx % 2, acc_free[g]
                    if g == 0 and name in ("qa", "qb"):
                        if idx >= 2:
                            act.wait_ge(sem(("a" if name == "qa" else "b") + "_stored"), idx - 1)
                        if name == "qb" and idx == 0:
                            act.wait_ge(sem("b_rows"), 1)
                    if name == "qa":
                        act.activation(ka[:, b2, c0:c1], src, ACT.Sigmoid)
                        copy(qa[:, b2, c0:c1], src).then_inc(bank, 1)
                    elif name == "fa":
                        act.activation(fa[:, b2, c0:c1], src, ACT.Sigmoid).then_inc(bank, 1)
                    elif name == "ga":
                        act.activation(sga[:, b2, c0:c1], src, ACT.Sigmoid)
                        copy(ga[:, b2, c0:c1], src).then_inc(bank, 1)
                    elif name == "qb":
                        copy(qb[:, b2, c0:c1], src, scale=QSCALE).then_inc(bank, 1)
                    elif name == "kb":
                        copy(kb[:, b2, c0:c1], src).then_inc(bank, 1)
                    elif name == "ob":
                        act.activation(gb[:, b2, c0:c1], src, ACT.Sigmoid).then_inc(bank, 1)
                    act.wait_ge(bank, FILLS[u] + 1)
                    act.nop().then_inc(sem("a_proj" if name[1] == "a" else "b_proj"), 1)
                elif kind == "if":
                    c0, c1 = CH[g]
                    copy(irow[:, c0:c1], acc[0:H, g, 0:c1 - c0])
                    copy(frow[:, c0:c1], acc[32:32 + H, g, 0:c1 - c0]).then_inc(acc_free[g], 1)
                elif idx % 2 == 0:
                    n = rows_of[g]
                    x = "a" if name == "ia" else "b"
                    if idx == 2 and g == 0:
                        act.wait_ge(sem(x + "_out"), 2)
                    dst = va[0:n, g, :] if x == "a" else vb[0:n, g, :, 0:P]
                    src = acc[0:n, g % 3, 0:256]
                    if x == "b":
                        src = src.rearrange("p (h v) -> p h v", h=2)
                    copy(dst, src).then_inc(acc_free[g % 3], 1)

            def out_evac(x, h, ot):
                act.wait_ge(sem(x + "_out"), h + 1)
                if h:
                    act.wait_ge(sem(x + "_gated"), h)
                copy(ot[:, 0:4, :], pz[:, 2, :].rearrange("p (c v) -> p c v", v=P))
                copy(ot[:, 4:8, :], pz[:, 3, :].rearrange("p (c v) -> p c v", v=P))
                copy(ot[0:TS, NT, :], pz[0:TS, 4, 0:P]).then_inc(sem(x + "_oevac"), 1)

            for it in ITEMS:
                if it[0] == "half":
                    _, u, g, hf = it
                    if g == 0 and hf == 0 and u + 1 < NU:
                        split_hi(u + 1)
                    if hf == 1:
                        evac(u, g)
                elif it[0] == "states_cd":
                    act.wait_ge(sem("ends_turned"), 1)
                    copy(taild[:, :], pz[:, 0, :]).then_inc(sem("tails_done"), 1)
                    copy(tailc[:, :], pz[:, 1, :]).then_inc(sem("tails_done"), 1)
                elif it[0] == "ln":
                    act.wait_ge(sem("ln_centred"), FT)
                    for t in range(FT):
                        if t >= 2:
                            act.wait_ge(sem("ln_var"), t - 1)
                        act.activation((ln_t, ln_r)[t % 2][:, :], y_d[:, t, :], ACT.Square) \
                            .then_inc(sem("ln_squared"), 1)
                    act.wait_ge(sem("ln_eps"), 1)
                    act.activation(ln_t[:, :], ln_t[:, :], ACT.Sqrt).then_inc(sem("ln_sqrt"), 1)
                    for t in range(FT):
                        act.wait_ge(sem("ln_affine"), t + 1)
                        if t >= 2:
                            act.wait_ge(sem("od_done"), t - 1)
                        act.activation((sg_d, y_c)[t % 2][:, :], y_d[:, t, :], ACT.Sigmoid) \
                            .then_inc(sem("ln_sig"), 1)
                    phase_end(act, "act", 2)
                elif it[0] == "phase" and it[1]:
                    phase_end(act, "act", it[1] + 2)
                elif it[0] == "rows":
                    act.wait_ge(sem("f_biased"), 1)
                    act.activation(trow, frow, ACT.Abs).then_inc(sem("row_act"), 1)
                    act.wait_ge(sem("row_act"), 1)
                    act.activation(urow, trow, ACT.Exp, scale=-1.0).then_inc(sem("row_act"), 1)
                    act.wait_ge(sem("row_act"), 2)
                    act.activation(trow, urow, ACT.Ln, bias=1.0).then_inc(sem("row_act"), 1)
                    act.wait_ge(sem("row_exps"), 1)
                    act.activation(wint[:, :], trow, ACT.Exp).then_inc(sem("row_done"), 1)
                    act.activation(cdr[:, :], nlast[:, :], ACT.Exp).then_inc(sem("row_done"), 1)
                    act.wait_ge(sem("rt_zero"), 1)
                    copy(rt[0:H, :], arow)
                    act.activation(rt[32:32 + H, :], mrow[:, :], ACT.Exp, scale=-1.0)
                    act.activation(rt[64:64 + H, :], urow, ACT.Exp).then_inc(sem("rows_ready"), 1)
                elif it[0] == "rec":
                    _, x, s, h = it
                    if x == "A":
                        if s == "turn":
                            act.wait_ge(sem("a_kturned"), h + 1)
                            copy(kta[:, 0:4, :], pz[:, 0, :].rearrange("p (c v) -> p c v", v=P))
                            copy(kta[:, 4:8, :], pz[:, 1, :].rearrange("p (c v) -> p c v", v=P))
                            copy(kta[0:TS, NT, :], pz[0:TS, 2, 0:P]).then_inc(sem("a_kt"), 1)
                        elif s == "out":
                            out_evac("a", h, ota)
                    else:
                        if s == "score":
                            act.wait_ge(sem("b_decayed"), h + 1)
                            act.activation(wb[:, 0:TP], wb[:, 0:TP], ACT.Exp)
                            act.activation(wb[0:TS, TP:T], wb[0:TS, TP:T], ACT.Exp).then_inc(sem("b_exp"), 1)
                        elif s == "out":
                            act.wait_ge(sem("b_out"), h + 1)
                            for j, (bk, nc_) in enumerate(((0, 3), (1, 3), (3, 2))):
                                act.activation(den[:, 3 * j:3 * j + nc_],
                                               pz[:, bk, 0:129 * nc_].rearrange("p (c n) -> p c n", n=129)[:, :, 128],
                                               ACT.Abs)
                            act.activation(den[0:TS, NT:NT + 1], pz[0:TS, 3, 386:387], ACT.Abs) \
                                .then_inc(sem("b_absden"), 1)

            split_hi(NU)
            with act.Fori(0, M_IT) as i:
                for s in range(M_UN):
                    pair, j = s // 3, s % 3
                    done = 12 * pair + 3 * j
                    split_hi_loop(M_U, M_G, i, M_UN, M_GN, s + 1, done)
                    if j < 2:
                        for g in range(3):
                            if s < 2 and g >= 1:
                                t = 2 * s + g - 1
                                act.wait_ge(sem(f"b_in{t % 2}"), i * 32 + 16 * (t // 2) + 16)
                                copy(b_hi[:, t, :], b_raw[:, t % 2, :]).then_inc(sem("b_hi_ready"), 1)
                            act.wait_ge(group_ready, M_G + done + g + 1 + i * M_GN)
                            if j == 0 and g == 0:
                                act.wait_ge(sem("m_gated"), i * 24 + pair * 6 + 1)
                            c0, c1 = CH[g]
                            act.activation(gsig[:, j, c0:c1], acc[:, g, 0:c1 - c0], ACT.Sigmoid) \
                                .then_inc(acc_free[g], 1)
            phase_end(act, "act", 5)
            for i in range(NT + 1):
                act.dma_start(x1[0:rows_of[i], i, :], x_tiles[i]).then_inc(sem("xres_in"), 16)
            for k in range(KT):
                copy(h_hi[:, k, :], merged[:, k, :]).then_inc(sem("mh_ready"), 1)
            act.dma_start(gfin[:, :], a["norm_final"].rearrange("(a d) -> a d", a=1).broadcast_to([P, D])) \
                .then_inc(sem("gfin_in"), 16)
            with act.Fori(0, O_IT) as i:
                for s in range(O_UN):
                    split_hi_loop(O_U, O_G, i, O_UN, O_GN, s + 1, 9 * s)
            norm_all("m", lambda i: x1[0:rows_of[i], i, :], junk1, full1,
                     lambda i: act.wait_ge(sem("o_added"), O_IT * O_GN) if i == 0 else None)
            phase_end(act, "act", 6)
            with act.Fori(0, L_IT) as i:
                for s in range(L_UN):
                    done = 3 * s if s < 4 else 12 + 9 * (s - 4)
                    split_hi_loop(L_U, L_G, i, L_UN, L_GN, s + 1, done)
                    if s >= 4:
                        continue
                    for g in range(3):
                        c0, c1 = CH[g]
                        e = 3 * s + g
                        act.wait_ge(group_ready, L_G + e + 1 + i * L_GN)
                        act.activation(ur[:, e % 2, 0:c1 - c0], acc[:, g, 0:c1 - c0], ACT.Relu) \
                            .then_inc(sem("u_relu"), 1)
                        act.wait_ge(sem("u_squared"), e + 1 + i * 12)
                        copy(u_hi[:, s, c0:c1], uu[:, e % 2, 0:c1 - c0]).then_inc(sem("u_high"), 1)
            for i in range(NT + 1):
                n = rows_of[i]
                act.wait_ge(sem("l_added"), L_IT * 36 + 1 - NT + i)
                if i >= 2:
                    act.wait_ge(sem("f_sq"), i - 1)
                act.activation(xt1[0:n, i % 2, :], x1[0:n, i, :], ACT.Square, accum_out=ss[0:n, i:i + 1]) \
                    .then_inc(sem("f_sq"), 1)

        @block.gpsimd
        def _(pool):
            links = [0]

            def link(ins):
                links[0] += 1
                ins.then_inc(sem("pool_link"), 1)
                pool.wait_ge(sem("pool_link"), links[0])

            def tt(out, x, y, op):
                return pool.tensor_tensor(out, x, y, op)

            def split_lo(u):
                s = u % SLOTS
                if u < NU and UNITS[u][0] == "if":
                    pool.wait_ge(group_ready, GROUPS[u - 1])
                    pool.memset(w_hi[:, s, :].bitcast(F32), 0.0)
                    link(pool.memset(w_lo[:, s, :].bitcast(F32), 0.0))
                    pool.nop().then_inc(sem("if_zero"), 1)
                    pool.wait_ge(hi_ready, u + 1)
                    raw4 = w_raw[:, s, :].rearrange("p (k n) -> p k n", k=KT)
                    hi4 = w_hi[:, s, :].rearrange("p (k n) -> p k n", k=KT).bitcast(F32)
                    lo4 = w_lo[:, s, :].rearrange("p (k n) -> p k n", k=KT)
                    tt(lo4[:, :, 0:4], raw4[:, :, 0:4], hi4[:, :, 0:4], ALU.subtract)
                    tt(lo4[:, :, 32:36], raw4[:, :, 4:8], hi4[:, :, 32:36], ALU.subtract).then_inc(w_ready, 1)
                    return
                pool.wait_ge(hi_ready, u + 1)
                if u >= SLOTS:
                    pool.wait_ge(group_ready, GROUPS[u - 1])
                tt(w_lo[:, s, :], w_raw[:, s, :], w_hi[:, s, :].bitcast(F32), ALU.subtract).then_inc(w_ready, 1)

            def split_lo_loop(base, gbase, i, n, gn, s, g_before):
                sl = (base + s) % SLOTS
                pool.wait_ge(group_ready, gbase + g_before + i * gn)
                pool.wait_ge(hi_ready, base + s + 1 + i * n)
                tt(w_lo[:, sl, :], w_raw[:, sl, :], w_hi[:, sl, :].bitcast(F32), ALU.subtract).then_inc(w_ready, 1)

            def power(pre, i, n):
                pool.wait_ge(sem(pre + "_ms"), i + 1)
                tt(rs[0:n, i:i + 1], ss[0:n, i:i + 1], mhalf[0:n, i:i + 1], ALU.pow).then_inc(sem(pre + "_rs"), 1)

            def norm_all(pre, full):
                for i in range(NT + 3):
                    if i <= NT:
                        power(pre, i, rows_of[i])
                    if i >= 2:
                        t0, t1 = TT_[i - 2]
                        pool.wait_ge(sem(pre + "_hi"), 2 * (i - 2) + 1)
                        tt(h_lo[:, 0:4, t0:t1], full_of(full, i - 2, 0), h_hi[:, 0:4, t0:t1].bitcast(F32),
                           ALU.subtract).then_inc(sem(pre + "_lo_a"), 1)

            link(pool.memset(mhalf[:, :], -0.5))
            norm_all("x", full0)
            split_lo(0)
            phase_end(pool, "pool", 1)
            pool.memset(e_d[:, :, 0:CD - 1], 0.0)
            pool.memset(e_c[:, 0:CC - 1], 0.0).then_inc(sem("pads_zero"), 1)

            def bs_view(f, s):
                if s == 1:
                    return f
                off, n = {2: (0, 544), 4: (544, 272), 8: (816, 136), 16: (952, 64), 32: (1016, 32),
                          64: (1048, 16), 128: (1064, 8)}[s]
                return tree[:, off:off + n]

            def spread_v(x, vz, v, h):
                vv = v.rearrange("p (o v) -> p o v", o=1).broadcast_to([TS, NS, P])
                bb = bmask.rearrange("p (b o) -> p b o", o=1).broadcast_to([TS, NS, P])
                tt(vz[:, :, :], vv, bb, ALU.mult).then_inc(sem(x + "_vz"), 1)

            def diag_q(x, qz, q):
                pool.tensor_copy(qz[:, :].rearrange("p (b n) -> p b n", n=TS + LS)[:, :, 0:LS],
                                 q.rearrange("p (b t) -> p b t", t=LS)).then_inc(sem(x + "_qz"), 1)

            for it in ITEMS:
                if it[0] == "half":
                    _, u, g, hf = it
                    kind, name, idx = UNITS[u]
                    if g == 0 and hf == 0 and u + 1 < NU:
                        split_lo(u + 1)
                    if hf == 1 and g == 2 and name == "ad":
                        pool.wait_ge(sem("glu_done"), 3 * idx + 3)
                        pool.tensor_copy(endd[:, idx, 0:64], e_d[:, idx, CD - 1 + TP - 64:])
                        pool.tensor_copy(endd[:, idx, 64:128].rearrange("p (b t) -> p b t", t=LS),
                                         e_ds[:, idx, :, CD - 1:]).then_inc(sem("ends_ready"), 1)
                elif it[0] == "short":
                    t = it[1]
                    pool.wait_ge(sem("short_in"), 3 * t + 3)
                    pool.tensor_copy(endc[:, t, 0:64], e_c[:, CC - 1 + TP - 64:])
                    pool.tensor_copy(endc[:, t, 64:128].rearrange("p (b t) -> p b t", t=LS),
                                     e_cs[:, :, CC - 1:]).then_inc(sem("ends_ready"), 1)
                elif it[0] == "ln":
                    for t in range(FT):
                        pool.wait_ge(sem("ln_scaled"), t + 1)
                        pool.tensor_scalar(y_d[:, t, :], y_d[:, t, :], par[:, t, R_LNG:R_LNG + 1],
                                           par[:, t, R_LNB:R_LNB + 1], ALU.mult, ALU.add) \
                            .then_inc(sem("ln_affine"), 1)
                    phase_end(pool, "pool", 2)
                    pool.memset(qza[:, :], 0.0)
                    pool.memset(sqa[:, :, :], 0.0)
                    pool.memset(ota[:, :, :], 0.0).then_inc(sem("a_cleared"), 1)
                elif it[0] == "phase" and it[1]:
                    phase_end(pool, "pool", it[1] + 2)
                    if it[1] == 1:
                        pool.memset(qzb[:, :], 0.0)
                        pool.memset(vb[:, :, :, P:P + 1], 1.0)
                        pool.memset(den[:, :], 1.0)
                        pool.memset(cols[:, :, :], 0.0)
                        pool.memset(otb[:, :, :], 0.0).then_inc(sem("b_cleared"), 1)
                        pool.memset(rt, 0.0).then_inc(sem("rt_zero"), 1)
                elif it[0] == "rec":
                    _, x, s, h = it
                    b2 = h % 2
                    if x == "A" and s == "prep":
                        q, k, f, g_ = qa[:, b2, :], ka[:, b2, :], fa[:, b2, :], ga[:, b2, :]
                        pool.wait_ge(sem("a_proj"), 9 * h + 9)
                        tt(q, q, k, ALU.mult)
                        link(pool.tensor_scalar(f, f, lbt[:, 3, h:h + 1], lbt[:, 2, h:h + 1], ALU.mult, ALU.add))
                        pool.tensor_scalar(k, f, -1.0, 1.0, ALU.mult, ALU.add).then_inc(sem("a_prep"), 1)
                        link(tt(g_, g_, sga[:, b2, :], ALU.mult))
                        tt(sga[:, b2, :], q, f, ALU.mult).then_inc(sem("a_q1"), 1)
                        if h:
                            pool.wait_ge(sem("a_states"), h)
                        for i in range(7):
                            s_ = 1 << i
                            n = (T if s_ <= 4 else TP) // s_
                            pv = bs_view(f, s_)[:, 0:n].rearrange("p (b two) -> p b two", two=2)
                            out = bs_view(f, 2 * s_)
                            ins = tt(out[:, 0:n // 2], pv[:, :, 0], pv[:, :, 1], ALU.mult)
                            if i < 6:
                                link(ins)
                            else:
                                ins.then_inc(sem("a_tree"), 1)
                        pool.wait_ge(sem("va_ready"), 9 * (h // 2) + 9)
                        spread_v("a", vza, va[0:TS, NT, (h % 2) * P:(h % 2 + 1) * P], h)
                    elif x == "A" and s.startswith("lv"):
                        if s == "lv4":
                            pool.wait_ge(sem("a_lv"), 7 * h + 3)
                            if h:
                                pool.wait_ge(sem("a_out"), h)
                            diag_q("a", qza, sga[:, b2, TP:T])
                    elif x == "B" and s == "prep":
                        if h == 0:
                            pool.wait_ge(sem("b_rows"), 1)
                        if h:
                            pool.wait_ge(sem("b_out"), h)
                        pool.wait_ge(sem("vb_ready"), 9 * (h // 2) + 9)
                        spread_v("b", vzb, vb[0:TS, NT, h % 2, 0:P], h)
                    elif x == "B" and s == "decay":
                        pool.wait_ge(sem("b_decayed"), h + 1)
                        diag_q("b", qzb, qs[:, TP:T])
                    elif s == "norm":
                        x_ = x.lower()
                        pool.wait_ge(sem(x_ + "_ms"), h + 1)
                        tt(rs[:, 0:NT + 1], ss[:, 0:NT + 1], mhalf[:, 0:NT + 1], ALU.pow) \
                            .then_inc(sem(x_ + "_rs"), 1)

            def branch_load(n_i, t):
                pool.dma_start(b_raw[:, t % 2, :], scratch[bass.ds(n_i, 1), t].rearrange("a p n -> (a p) n")) \
                    .then_inc(sem(f"b_in{t % 2}"), 16)

            split_lo(NU)
            with pool.Fori(0, M_IT) as i:
                branch_load(i, 0)
                branch_load(i, 1)
                for s in range(M_UN):
                    pair, j = s // 3, s % 3
                    split_lo_loop(M_U, M_G, i, M_UN, M_GN, s + 1, 12 * pair + 3 * j)
                    if s < 2:
                        for t in (2 * s, 2 * s + 1):
                            pool.wait_ge(sem("b_hi_ready"), i * 4 + t + 1)
                            tt(b_lo[:, t, :], b_raw[:, t % 2, :], b_hi[:, t, :].bitcast(F32), ALU.subtract) \
                                .then_inc(sem("branch_ready"), 1)
                            if t < 2:
                                pool.wait_ge(sem("branch_ready"), i * 4 + t + 1)
                                branch_load(i, t + 2)
            phase_end(pool, "pool", 5)
            for k in (2, 5):
                pool.wait_ge(sem("mh_ready"), k + 1)
                tt(h_lo[:, k, :], merged[:, k, :], h_hi[:, k, :].bitcast(F32), ALU.subtract) \
                    .then_inc(sem("merged_low_b"), 1)
            with pool.Fori(0, O_IT) as i:
                for s in range(O_UN):
                    split_lo_loop(O_U, O_G, i, O_UN, O_GN, s + 1, 9 * s)
            norm_all("m", full1)
            pool.sem_inc(sem("u_ready"), 2)
            phase_end(pool, "pool", 6)
            with pool.Fori(0, L_IT) as i:
                for s in range(L_UN):
                    split_lo_loop(L_U, L_G, i, L_UN, L_GN, s + 1, 3 * s if s < 4 else 12 + 9 * (s - 4))
                    if s >= 4:
                        continue
                    for g in range(3):
                        c0, c1 = CH[g]
                        e = 3 * s + g
                        pool.wait_ge(sem("u_high"), e + 1 + i * 12)
                        tt(u_lo[:, s, c0:c1], uu[:, e % 2, 0:c1 - c0], u_hi[:, s, c0:c1].bitcast(F32),
                           ALU.subtract).then_inc(sem("u_ready"), 1)
            pool.wait_ge(sem("f_ms"), 1)
            tt(rs[:, 0:NT + 1], ss[:, 0:NT + 1], mhalf[:, 0:NT + 1], ALU.pow).then_inc(sem("f_rs"), 1)

        @block.vector
        def _(dve):
            links = [0]

            def link(ins):
                links[0] += 1
                ins.then_inc(sem("dve_link"), 1)
                dve.wait_ge(sem("dve_link"), links[0])

            def tt(out, x, y, op):
                return dve.tensor_tensor(out, x, y, op)

            def stt(out, x, sc, y, op0, op1):
                return dve.scalar_tensor_tensor(out, x, sc, y, op0, op1)

            def norm_all(pre, src, dst, full, col):
                for i in range(NT + 4):
                    if i <= NT:
                        n = rows_of[i]
                        dve.wait_ge(sem(pre + "_sq"), i + 1)
                        dve.tensor_scalar(ss[0:n, i:i + 1], ss[0:n, i:i + 1], 1.0 / D, EPS, ALU.mult, ALU.add) \
                            .then_inc(sem(pre + "_ms"), 1)
                    if 1 <= i <= NT + 1:
                        k = i - 1
                        n = rows_of[k]
                        dve.wait_ge(sem(pre + "_rs"), k + 1)
                        if k >= 2:
                            dve.wait_ge(sem(pre + "_turned"), 2 * k - 2)
                        dve.tensor_scalar(dst[0:n, k % 2, :], src(k), rs[0:n, k:k + 1], None, ALU.mult) \
                            .then_inc(sem(pre + "_scaled"), 1)
                    if i >= 3:
                        t0, t1 = TT_[i - 3]
                        dve.wait_ge(sem(pre + "_hi"), 2 * (i - 3) + 2)
                        tt(h_lo[:, 4:8, t0:t1], full_of(full, i - 3, 1), h_hi[:, 4:8, t0:t1].bitcast(F32),
                           ALU.subtract).then_inc(sem(pre + "_lo_b"), 1)
                    if 2 <= i <= NT + 2:
                        k = i - 2
                        n = rows_of[k]
                        if k >= 2:
                            dve.wait_ge(sem(pre + "_lo_a"), k - 1)
                            dve.wait_ge(sem(pre + "_lo_b"), k - 1)
                        for hh in range(2):
                            dve.wait_ge(sem(pre + "_turned"), 2 * k + hh + 1)
                            gain = nrm[:, col + 4 * hh:col + 4 * hh + 4].rearrange("p (k o) -> p k o", o=1) \
                                .broadcast_to([P, 4, n])
                            tt(full_of(full, k, hh), pz[:, 1 + 2 * (k % 2) + hh, :]
                               .rearrange("p (k n) -> p k n", k=4)[:, :, 0:n], gain, ALU.mult) \
                                .then_inc(sem(pre + "_full"), 1)

            dve.wait_ge(sem("params_turned"), 1)
            dve.tensor_copy(par[:, :, :], pz[:, 0, 0:FT * NPAR].rearrange("p (t n) -> p t n", t=FT))
            link(dve.tensor_copy(nrm[:, :], pz[:, 0, FT * NPAR:FT * NPAR + 16]))
            lbl = par[:, :, R_LB]
            tt(lbt[:, 0, :], lbl, lbl, ALU.subtract).then_inc(sem("lb_diff"), 1)
            norm_all("x", lambda i: xin[0:rows_of[i], i, :], xt, full0, 0)
            dve.wait_ge(consts_in, 64)
            for i in range(7):
                dve.tensor_copy(lvm[:, i, :].rearrange("p (c n) -> p c n", c=NT),
                                lvf[:, i:i + 1, :].broadcast_to([P, NT, 64]))
            dve.wait_ge(sem("lb_exp"), 1)
            link(dve.reciprocal(lbt[:, 2, :], lbt[:, 1, :]))
            link(tt(lbt[:, 3, :], lbt[:, 1, :], lbt[:, 2, :], ALU.mult))
            link(tt(lbt[:, 2, :], lbt[:, 3, :], lbt[:, 3, :], ALU.subtract))
            dve.tensor_scalar(lbt[:, 3, :], lbt[:, 2, :], -1.0, 1.0, ALU.mult, ALU.add)
            phase_end(dve, "dve", 1)

            def convs_in():
                dve.wait_ge(sem("bufs_turned"), 1)
                for j in range(2):
                    dve.tensor_copy(e_ds[:, :, 4 * j:4 * j + 4, 0:CD - 1],
                                    pz[:, j, 0:480].rearrange("p (t b n) -> p t b n", t=FT, b=4))
                dve.tensor_copy(e_cs_old[:, :, :, :],
                                pz[:, 2, 0:64].rearrange("p (t b n) -> p t b n", t=FT, b=NS)) \
                    .then_inc(sem("bufs_in"), 1)

            def evac(u, g):
                kind, name, idx = UNITS[u]
                if kind == "feat":
                    c0, c1 = CH[g]
                    src = acc[:, g, 0:c1 - c0]
                    if name == "ad":
                        dve.wait_ge(group_ready, GROUPS[u] + g + 1)
                        ed = e_d[:, idx, CD - 1:]
                        if g < 2:
                            tt(ed[:, c0:c1], src, sg_d[:, c0:c1], ALU.mult).then_inc(acc_free[g], 1)
                        else:
                            tt(ed[:, c0:TP], src[:, 0:TP - c0], sg_d[:, c0:TP], ALU.mult)
                            tt(e_ds[:, idx, :, CD - 1:], src[:, TP - c0:T - c0].rearrange("p (b t) -> p b t", t=LS),
                               sg_d[:, TP:T].rearrange("p (b t) -> p b t", t=LS), ALU.mult).then_inc(acc_free[g], 1)
                        dve.wait_ge(acc_free[g], FILLS[u] + 1)
                        dve.nop().then_inc(sem("glu_done"), 1)
                    elif name == "xc":
                        dve.wait_ge(group_ready, GROUPS[u] + g + 1)
                        dve.wait_ge(acc_free[g], FILLS[u])
                        if g == 0:
                            if idx:
                                dve.wait_ge(sem("short_done"), idx)
                            dve.tensor_copy(e_cs[:, :, 0:CC - 1], e_cs_old[:, idx, :, :])
                        ec = e_c[:, CC - 1:]
                        if g < 2:
                            tt(ec[:, c0:c1], src, ec[:, c0:c1], ALU.mult).then_inc(acc_free[g], 1)
                        else:
                            tt(ec[:, c0:TP], src[:, 0:TP - c0], ec[:, c0:TP], ALU.mult)
                            sv = e_cs[:, :, CC - 1:]
                            tt(sv, src[:, TP - c0:T - c0].rearrange("p (b t) -> p b t", t=LS), sv, ALU.mult) \
                                .then_inc(acc_free[g], 1)
                        dve.wait_ge(acc_free[g], FILLS[u] + 1)
                        dve.nop().then_inc(sem("short_in"), 1)
                    elif name == "bc":
                        dve.wait_ge(group_ready, GROUPS[u] + g + 1)
                        dve.wait_ge(sem("short_done"), idx + 1)
                        if idx and g == 0:
                            dve.wait_ge(sem("oc_stored"), idx)
                        tt(o_c[:, c0:c1], src, y_c[:, c0:c1], ALU.mult).then_inc(acc_free[g], 1)
                        dve.wait_ge(acc_free[g], FILLS[u] + 1)
                        dve.nop().then_inc(sem("oc_done"), 1)
                elif kind == "tok" and idx % 2 == 1:
                    n = rows_of[g]
                    a_ = name == "ia"
                    dve.wait_ge(group_ready, GROUPS[u] + g + 1)
                    dve.wait_ge(acc_free[g % 3], FILLS[u] - 2 + g // 3)
                    dst = va[0:n, g, :] if a_ else vb[0:n, g, :, 0:P]
                    src = acc[0:n, g % 3, 0:256]
                    if not a_:
                        src = src.rearrange("p (h v) -> p h v", h=2)
                    tt(dst, src, dst, ALU.add).then_inc(acc_free[g % 3], 1)
                    if g == 8:
                        for b in range(3):
                            dve.wait_ge(acc_free[b], FILLS[u] + 3)
                        dve.nop().then_inc(sem("va_ready" if a_ else "vb_ready"), 9)

            def tap(t, j):
                w = par[:, t, R_CDW + j:R_CDW + j + 1]
                yp, ys = y_d[:, t, 0:TP], y_d[:, t, TP:T].rearrange("p (b t) -> p b t", t=LS)
                xp, xs_ = e_d[:, t, j:j + TP], e_ds[:, t, :, j:j + LS]
                if j == 0:
                    b = par[:, t, R_CDB:R_CDB + 1]
                    if t == 0:
                        dve.wait_ge(sem("pads_zero"), 1)
                        dve.wait_ge(sem("bufs_in"), 1)
                    dve.wait_ge(sem("glu_done"), 3 * t + 3)
                    dve.tensor_scalar(yp, xp, w, b, ALU.mult, ALU.add)
                    dve.tensor_scalar(ys, xs_, w, b, ALU.mult, ALU.add).then_inc(sem("tap_done"), 1)
                else:
                    dve.wait_ge(sem("tap_done"), CD * t + j)
                    stt(yp, xp, w, yp, ALU.mult, ALU.add)
                    stt(ys, xs_, w, ys, ALU.mult, ALU.add).then_inc(sem("tap_done"), 1)
                if j == CD - 1:
                    dve.wait_ge(sem("tap_done"), CD * (t + 1))
                    dve.nop().then_inc(sem("conv_done"), 1)

            def short(t):
                yp, ys = y_c[:, 0:TP], y_c[:, TP:T].rearrange("p (b t) -> p b t", t=LS)
                dve.wait_ge(sem("short_in"), 3 * t + 3)
                if t:
                    dve.wait_ge(sem("oc_done"), 3 * t)
                for j in range(CC):
                    w = par[:, t, R_CCW + j:R_CCW + j + 1]
                    xp, xs_ = e_c[:, j:j + TP], e_cs[:, :, j:j + LS]
                    if j == 0:
                        dve.tensor_scalar(yp, xp, w, None, ALU.mult)
                        link(dve.tensor_scalar(ys, xs_, w, None, ALU.mult))
                    else:
                        stt(yp, xp, w, yp, ALU.mult, ALU.add)
                        ins = stt(ys, xs_, w, ys, ALU.mult, ALU.add)
                        if j < CC - 1:
                            link(ins)
                ins.then_inc(sem("short_done"), 1)

            def rms(x, h, ot, sq):
                link(tt(sq[:, :, :], ot[:, :, :], ot[:, :, :], ALU.mult))
                link(dve.tensor_reduce(ss[:, 0:NT + 1], sq[:, :, :], AX, ALU.add))
                dve.tensor_scalar(ss[:, 0:NT + 1], ss[:, 0:NT + 1], 1.0 / P, EPS, ALU.mult, ALU.add) \
                    .then_inc(sem(x + "_ms"), 1)
                dve.wait_ge(sem(x + "_rs"), h + 1)
                tt(ot[:, :, :], ot[:, :, :], rs[:, 0:NT + 1].rearrange("p (c o) -> p c o", o=1)
                   .broadcast_to([P, NT + 1, P]), ALU.mult).then_inc(sem(x + "_normed"), 1)

            def gate_out(x, h, g_, row):
                dve.wait_ge(sem(x + "_turned"), h + 1)
                gain = par[:, h, row:row + 1]
                stt(g_[:, 0:512], pz[:, 0, :], gain, g_[:, 0:512], ALU.mult, ALU.mult)
                stt(g_[:, 512:TP], pz[:, 1, :], gain, g_[:, 512:TP], ALU.mult, ALU.mult)
                stt(g_[:, TP:T], pz[:, 2, 0:TS], gain, g_[:, TP:T], ALU.mult, ALU.mult).then_inc(sem(x + "_gated"), 1)

            def rec_a(s, h):
                b2 = h % 2
                k, f = ka[:, b2, :], fa[:, b2, :]
                if s == "lv0":
                    dve.wait_ge(sem("a_scored"), 8 * h + 1)
                    idb = ident.rearrange("p (o n) -> p o n", o=1).broadcast_to([P, 4, P])
                    for j in range(2):
                        tt(sa[:, 512 * j:512 * j + 512].rearrange("p (c n) -> p c n", n=P),
                           pz[:, j, :].rearrange("p (c n) -> p c n", n=P), idb, ALU.mult)
                    tt(sa[0:TS, TP:T], pz[0:TS, 2, 0:TS], ident[0:TS, 0:TS], ALU.mult).then_inc(sem("a_masked"), 1)
                elif s.startswith("lv"):
                    i = int(s[2:])
                    sz = 1 << (i - 1)
                    bank, sbank = (3, 4) if i % 2 else (0, 2)
                    dve.wait_ge(sem("a_scored"), 8 * h + i + 1)
                    n = T if sz <= 4 else TP
                    if i == 1:
                        dve.wait_ge(sem("a_tree"), h + 1)
                        dve.wait_ge(sem("a_q1"), h + 1)
                    else:
                        dve.wait_ge(sem("a_lv"), 7 * h + i - 1)
                    kv = k[:, 0:n].rearrange("p (b two s) -> p b two s", two=2, s=sz)[:, :, 0, :]
                    bv = bs_of(f, sz)[:, 0:n // sz].rearrange("p (b two) -> p b two", two=2)[:, :, 1:2] \
                        .broadcast_to([P, n // (2 * sz), sz])
                    q = sga[:, b2, :]
                    qv = q[:, 0:n].rearrange("p (b two s) -> p b two s", two=2, s=sz)[:, :, 1, :]
                    bq = bs_of(f, sz)[:, 0:n // sz].rearrange("p (b two) -> p b two", two=2)[:, :, 0:1] \
                        .broadcast_to([P, n // (2 * sz), sz])
                    tt(kv, kv, bv, ALU.mult)
                    tt(qv, qv, bq, ALU.mult).then_inc(sem("a_lv"), 1)
                    dve.wait_ge(sem("a_masked"), 8 * h + i)
                    mask = lvm[:, i - 1, :]
                    so = sa[:, 0:TP].rearrange("p (b two s) -> p b two s", two=2, s=sz)[:, :, 1, :]
                    ins = dve.copy_predicated(so, mask.rearrange("p (b s) -> p b s", s=sz),
                                              pz[:, bank, :].rearrange("p (b s) -> p b s", s=sz))
                    if i <= 3:
                        so = sa[0:TS, TP:T].rearrange("p (b two s) -> p b two s", two=2, s=sz)[:, :, 1, :]
                        ins = dve.copy_predicated(so, mask[0:TS, 0:32].rearrange("p (b s) -> p b s", s=sz),
                                                  pz[0:TS, sbank, 0:32].rearrange("p (b s) -> p b s", s=sz))
                    ins.then_inc(sem("a_masked"), 1)
                elif s == "state":
                    dve.wait_ge(sem("a_updates"), h + 1)
                    if h:
                        dve.wait_ge(sem("a_stored"), h)
                    link(dve.tensor_copy(sta[:, 0, :], pz[:, 3, 0:P]))
                    b128, b8 = bs_of(f, 128), bs_of(f, 8)
                    for c in range(1, NT):
                        link(stt(sta[:, c, :], sta[:, c - 1, :], b128[:, c:c + 1],
                                 pz[:, 3 + c // 4, (c % 4) * P:(c % 4 + 1) * P], ALU.mult, ALU.add))
                    dve.wait_ge(sem("s0_in"), 16 * (h + 1))
                    link(tt(sna[:, :, :], s0a[:, :, :], b8[:, 128:136].rearrange("p (b o) -> p b o", o=1)
                            .broadcast_to([P, NS, P]), ALU.mult))
                    for j in range(2):
                        ins = tt(sna[:, 4 * j:4 * j + 4, :], pz[:, j, :].rearrange("p (b v) -> p b v", v=P),
                                 sna[:, 4 * j:4 * j + 4, :], ALU.add)
                    ins.then_inc(sem("a_states"), 1)
                elif s == "norm":
                    dve.wait_ge(sem("a_oevac"), h + 1)
                    rms("a", h, ota, sqa)
                elif s == "gate":
                    dve.wait_ge(sem("a_q1"), h + 1)
                    gate_out("a", h, ga[:, b2, :], R_NH)

            def rows():
                dve.wait_ge(acc_free[2], FILLS[IF_U] + 1)
                dve.wait_ge(acc_free[1], FILLS[IF_U] + 1)
                dve.wait_ge(acc_free[0], FILLS[IF_U] + 1)
                dve.wait_ge(sem("m0_in"), 32)
                dve.tensor_scalar(irow, irow, biases[:, 0:1], None, ALU.add)
                dve.tensor_scalar(frow, frow, biases[:, 1:2], None, ALU.add).then_inc(sem("f_biased"), 1)
                dve.wait_ge(sem("f_biased"), 1)
                dve.wait_ge(sem("row_act"), 3)
                link(stt(frow, frow, 0.0, trow, ALU.min, ALU.subtract))
                dve.tensor_tensor_scan(mrow[:, 0:TP], frow[:, 0:TP], irow[:, 0:TP], 0.0, ALU.add, ALU.max)
                for b in range(NS):
                    t0 = TP + LS * b
                    dve.tensor_tensor_scan(mrow[:, t0:t0 + LS], frow[:, t0:t0 + LS], irow[:, t0:t0 + LS],
                                           m0[:, b:b + 1], ALU.add, ALU.max)
                link(dve.tensor_tensor_scan(brow, keepr[:, :], frow, 0.0, ALU.mult, ALU.add))
                dve.nop().then_inc(sem("m_done"), 1)
                tt(nM[:, :], brow, mrow[:, :], ALU.subtract)
                tt(arow, irow, brow, ALU.subtract)
                dve.memset(mp[:, 0:1], 0.0)
                dve.tensor_copy(mp[:, 1:NT], mrow[:, P - 1:TP - P:P])
                link(dve.tensor_copy(mp[:, NT:16], m0[:, 0:NS]))
                dve.tensor_copy(nlast[:, 0:NT], nM[:, P - 1:TP:P])
                link(dve.tensor_copy(nlast[:, NT:16], nM[:, TP + LS - 1:T:LS]))

                def spread(v, j):
                    return (v[:, 0:NT].rearrange("p (c o) -> p c o", o=1).broadcast_to([H, NT, P]) if j == 0 else
                            v[:, NT:16].rearrange("p (c o) -> p c o", o=1).broadcast_to([H, NS, LS]))

                def view(r, j):
                    return r[:, 0:TP].rearrange("p (c n) -> p c n", n=P) if j == 0 else \
                        r[:, TP:T].rearrange("p (c n) -> p c n", n=LS)
                for j in range(2):
                    tt(view(trow, j), view(nM, j), spread(mp, j), ALU.add)
                    ins = tt(view(urow, j), view(arow, j), spread(nlast, j), ALU.add)
                link(ins)
                tt(nlast[:, :], nlast[:, :], mp[:, :], ALU.add).then_inc(sem("row_exps"), 1)

            def rows_out():
                dve.wait_ge(sem("rows_turned"), 1)
                dve.tensor_copy(cols[:, 0:4, :], pz[:, 0, :].rearrange("p (c n) -> p c n", n=P))
                dve.tensor_copy(cols[:, 4:8, :], pz[:, 1, :].rearrange("p (c n) -> p c n", n=P))
                dve.tensor_copy(cols[0:TS, NT, :], pz[0:TS, 2, 0:P])
                dve.tensor_copy(cdc[:, :, :], pz[:, 3, 0:64].rearrange("p (h c) -> p h c", h=H)) \
                    .then_inc(sem("b_rows"), 1)

            def rec_b(s, h):
                b2 = h % 2
                q = qb[:, b2, :]
                if s == "decay":
                    dve.wait_ge(sem("b_spread"), h + 1)
                    if h == 0:
                        dve.wait_ge(sem("b_rows"), 1)
                    for c in range(NT):
                        stt(wb[:, c * P:(c + 1) * P], pz[:, c // 4, (c % 4) * P:(c % 4 + 1) * P],
                            cols[:, c, h:h + 1], negm, ALU.add, ALU.min)
                    stt(wb[0:TS, TP:T], pz[0:TS, 2, 0:TS], cols[0:TS, NT, h:h + 1], negs, ALU.add, ALU.min)
                    dve.wait_ge(sem("b_proj"), 9 * h + 9)
                    tt(qs[:, 0:512], pz[:, 3, :], q[:, 0:512], ALU.mult)
                    tt(qs[:, 512:TP], pz[:, 4, :], q[:, 512:TP], ALU.mult)
                    tt(qs[:, TP:T], pz[:, 2, 64:128], q[:, TP:T], ALU.mult).then_inc(sem("b_decayed"), 1)
                elif s == "score":
                    dve.wait_ge(sem("b_exp"), h + 1)
                    dve.wait_ge(sem("b_scored"), h + 1)
                    tt(wb[:, 0:512], pz[:, 0, :], wb[:, 0:512], ALU.mult)
                    tt(wb[:, 512:TP], pz[:, 1, :], wb[:, 512:TP], ALU.mult)
                    tt(wb[0:TS, TP:T], pz[0:TS, 2, 0:TS], wb[0:TS, TP:T], ALU.mult).then_inc(sem("b_weighted"), 1)
                elif s == "turn":
                    dve.wait_ge(sem("b_kturned"), h + 1)

                    def ws(c0, c1, n=P):
                        return cols[0:n, c0:c1, 64 + h:65 + h].broadcast_to([n, c1 - c0, P])
                    tt(ktb[:, 0:4, :], pz[:, 3, :].rearrange("p (c n) -> p c n", n=P), ws(0, 4), ALU.mult)
                    tt(ktb[:, 4:8, :], pz[:, 4, :].rearrange("p (c n) -> p c n", n=P), ws(4, 8), ALU.mult)
                    dve.tensor_scalar(ktb[0:TS, NT, :], pz[0:TS, 2, 128:256], cols[0:TS, NT, 64 + h:65 + h], None,
                                      ALU.mult).then_inc(sem("b_kt"), 1)
                elif s == "state":
                    dve.wait_ge(sem("b_updates"), h + 1)
                    if h:
                        dve.wait_ge(sem("b_stored"), h)
                    link(dve.tensor_copy(cnb[:, 0, 0:P + 1], pz[:, 0, 0:P + 1]))
                    for c in range(1, NT):
                        link(stt(cnb[:, c, 0:P + 1], cnb[:, c - 1, 0:P + 1], cdc[:, h, c:c + 1],
                                 pz[:, (0, 1, 3)[c // 3], (c % 3) * 129:(c % 3) * 129 + 129], ALU.mult, ALU.add))
                    dve.wait_ge(sem("c0_in"), 32 * (h + 1))
                    link(tt(cnew[:, :, 0:P + 1], c0b[:, :, 0:P + 1],
                            cdc[:, h, NT:16].rearrange("p (b o) -> p b o", o=1).broadcast_to([P, NS, P + 1]),
                            ALU.mult))
                    for j, bk in enumerate((2, 4)):
                        tt(cnew[:, 4 * j:4 * j + 4, 0:P], pz[:, bk, :].rearrange("p (b v) -> p b v", v=P),
                           cnew[:, 4 * j:4 * j + 4, 0:P], ALU.add)
                    tt(cnew[:, :, P], pz[:, 3, 400:408], cnew[:, :, P], ALU.add).then_inc(sem("b_states"), 1)
                elif s == "norm":
                    dve.wait_ge(sem("b_absden"), h + 1)
                    link(tt(den[:, 0:NT + 1], den[:, 0:NT + 1], cols[:, :, 32 + h], ALU.max))
                    link(dve.reciprocal(den[:, 0:NT + 1], den[:, 0:NT + 1]))
                    for c0, c1, bk in ((0, 3, 0), (3, 6, 1), (6, 8, 3)):
                        n = c1 - c0
                        tt(otb[:, c0:c1, :], pz[:, bk, 0:129 * n].rearrange("p (c n) -> p c n", n=129)[:, :, 0:P],
                           den[:, c0:c1].rearrange("p (c o) -> p c o", o=1).broadcast_to([P, n, P]), ALU.mult)
                    link(dve.tensor_scalar(otb[0:TS, NT, :], pz[0:TS, 3, 258:386], den[0:TS, NT:NT + 1], None,
                                           ALU.mult))
                    rms("b", h, otb, sqb)
                elif s == "gate":
                    gate_out("b", h, gb[:, b2, :], R_NM)

            def bs_of(f, s):
                if s == 1:
                    return f
                off, n = {2: (0, 544), 4: (544, 272), 8: (816, 136), 16: (952, 64), 32: (1016, 32),
                          64: (1048, 16), 128: (1064, 8)}[s]
                return tree[:, off:off + n]

            convs_in()
            for it in ITEMS:
                if it[0] == "half":
                    if it[3] == 1:
                        evac(it[1], it[2])
                elif it[0] == "tap":
                    tap(it[1], it[2])
                elif it[0] == "short":
                    short(it[1])
                elif it[0] == "ln":
                    dve.wait_ge(sem("ln_mean"), 1)
                    for t in range(FT):
                        for j, (c0, c1) in enumerate(((0, 512), (512, 1024), (1024, T))):
                            ins = stt(y_d[:, t, c0:c1], pz[:, j, 0:c1 - c0], -1.0 / W, y_d[:, t, c0:c1],
                                      ALU.mult, ALU.add)
                        ins.then_inc(sem("ln_centred"), 1)
                    dve.wait_ge(sem("ln_var"), FT)
                    for j, (c0, c1) in enumerate(((0, 512), (512, 1024), (1024, T))):
                        ins = dve.tensor_scalar(ln_t[:, c0:c1], pz[:, j, 0:c1 - c0], 1.0 / W, EPS, ALU.mult, ALU.add)
                    ins.then_inc(sem("ln_eps"), 1)
                    dve.wait_ge(sem("ln_sqrt"), 1)
                    link(dve.reciprocal(ln_r[:, :], ln_t[:, :]))
                    for t in range(FT):
                        tt(y_d[:, t, :], y_d[:, t, :], ln_r[:, :], ALU.mult).then_inc(sem("ln_scaled"), 1)
                    for t in range(FT):
                        dve.wait_ge(sem("ln_sig"), t + 1)
                        tt(y_d[:, t, :], y_d[:, t, :], (sg_d, y_c)[t % 2][:, :], ALU.mult).then_inc(sem("od_done"), 1)
                    phase_end(dve, "dve", 2)
                elif it[0] == "phase" and it[1]:
                    phase_end(dve, "dve", it[1] + 2)
                elif it[0] == "rows":
                    rows()
                elif it[0] == "rows_out":
                    rows_out()
                elif it[0] == "rec":
                    (rec_a if it[1] == "A" else rec_b)(it[2], it[3])

            dve.memset(merged[:, :, :], 0.0).then_inc(sem("m_gated"), 1)
            with dve.Fori(0, M_IT) as i:
                for pair in range(4):
                    for r in range(2):
                        for g in range(3):
                            c0, c1 = CH[g]
                            e = 6 * pair + 3 * r + g
                            dve.wait_ge(group_ready, M_G + 12 * pair + 6 + 3 * r + g + 1 + i * M_GN)
                            tt(gtmp[:, e % 2, 0:c1 - c0], acc[:, g, 0:c1 - c0], gsig[:, r, c0:c1], ALU.mult) \
                                .then_inc(acc_free[g], 1)
                            dve.wait_ge(acc_free[g], M_B + 4 * pair + 2 + r + 1 + i * M_BN)
                            mv = merged[:, 2 * pair + r, c0:c1]
                            tt(mv, gtmp[:, e % 2, 0:c1 - c0], mv, ALU.add).then_inc(sem("m_gated"), 1)
            phase_end(dve, "dve", 5)
            for k in (0, 1, 3, 4, 6, 7):
                dve.wait_ge(sem("mh_ready"), k + 1)
                tt(h_lo[:, k, :], merged[:, k, :], h_hi[:, k, :].bitcast(F32), ALU.subtract) \
                    .then_inc(sem("merged_low_a"), 1)
            dve.wait_ge(sem("xres_in"), 16 * (NT + 1))
            with dve.Fori(0, O_IT) as i:
                for s in range(O_UN):
                    for c in range(NT + 1):
                        n = rows_of[c]
                        dve.wait_ge(group_ready, O_G + 9 * s + c + 1 + i * O_GN)
                        if s:
                            dve.wait_ge(sem("o_added"), i * O_GN + 9 * (s - 1) + c + 1)
                        xv = x1[0:n, c, bass.ds(i * 512, 512)]
                        tt(xv, acc[0:n, c % 3, :], xv, ALU.add).then_inc(acc_free[c % 3], 1)
                        dve.wait_ge(acc_free[c % 3], O_B + 3 * s + c // 3 + 1 + i * O_BN)
                        dve.nop().then_inc(sem("o_added"), 1)
            norm_all("m", lambda i: x1[0:rows_of[i], i, :], xt1, full1, 8)
            dve.sem_inc(sem("l_added"), 1)
            phase_end(dve, "dve", 6)
            with dve.Fori(0, L_IT) as i:
                for s in range(4):
                    for g in range(3):
                        c0, c1 = CH[g]
                        e = 3 * s + g
                        dve.wait_ge(sem("u_relu"), e + 1 + i * 12)
                        dve.wait_ge(sem("u_ready"), e + 1 + i * 12)
                        tt(uu[:, e % 2, 0:c1 - c0], acc[:, g, 0:c1 - c0], ur[:, e % 2, 0:c1 - c0], ALU.mult) \
                            .then_inc(acc_free[g], 1)
                        dve.wait_ge(acc_free[g], L_B + s + 1 + i * L_BN)
                        dve.nop().then_inc(sem("u_squared"), 1)
                for s in range(4):
                    for c in range(NT + 1):
                        n = rows_of[c]
                        dve.wait_ge(group_ready, L_G + 12 + 9 * s + c + 1 + i * L_GN)
                        if s == 0 and c == 0:
                            dve.wait_ge(sem("l_added"), i * 36 + 1)
                        if s >= 2:
                            dve.wait_ge(sem("l_added"), i * 36 + 9 * (s - 2) + c + 2)
                        xv = x1[0:n, c, (s % 2) * 512:(s % 2 + 1) * 512]
                        tt(xv, acc[0:n, c % 3, :], xv, ALU.add).then_inc(acc_free[c % 3], 1)
                        dve.wait_ge(acc_free[c % 3], L_B + 4 + 3 * s + c // 3 + 1 + i * L_BN)
                        dve.nop().then_inc(sem("l_added"), 1)
            dve.wait_ge(sem("gfin_in"), 16)
            dve.wait_ge(sem("f_sq"), NT + 1)
            dve.tensor_scalar(ss[:, 0:NT + 1], ss[:, 0:NT + 1], 1.0 / D, EPS, ALU.mult, ALU.add) \
                .then_inc(sem("f_ms"), 1)
            dve.wait_ge(sem("f_rs"), 1)
            for i in range(NT + 1):
                n = rows_of[i]
                stt(x1[0:n, i, :], x1[0:n, i, :], rs[0:n, i:i + 1], gfin[0:n, :], ALU.mult, ALU.mult) \
                    .then_inc(sem("y_done"), 1)


INS = ["x_prompt", "x_sample", "state_hgrn", "state_mlstm_c", "state_mlstm_n", "state_mlstm_m",
       "state_conv_short", "state_conv_conformer", "w_in", "w_branch", "w_out", "lb_logits", "norm_hgrn",
       "mlstm_i_bias", "mlstm_f_bias", "norm_mlstm", "conv_short_w", "conv_conformer_w", "conv_conformer_b",
       "ln_conformer_g", "ln_conformer_b", "norm_mix", "norm_mlp", "w_up", "w_down", "norm_final"]
OUTS = [("y_p", (1, TP, D)), ("y_s", (NS, LS, D)), ("hg_p", (1, 1, H, P, P)), ("hg_s", (1, NS, H, P, P)),
        ("mc_p", (1, 1, H, P, P)), ("mc_s", (1, NS, H, P, P)), ("mn_p", (1, 1, H, P)), ("mn_s", (1, NS, H, P)),
        ("mm_p", (1, 1, H)), ("mm_s", (1, NS, H)), ("cc_p", (1, 1, CC - 1, W)), ("cc_s", (1, NS, CC - 1, W)),
        ("cd_p", (1, 1, CD - 1, W)), ("cd_s", (1, NS, CD - 1, W))]


def kernel(**inputs):
    import concourse.bacc as bacc
    from concourse.bass_utils import run_bass_kernel_spmd

    nc = bacc.Bacc("TRN2", target_bir_lowering=False, num_devices=1)
    arrays, a, o = {}, {}, {}
    lvm, con, keep = constants()
    given = {n: np.ascontiguousarray(inputs[n]) for n in INS}
    given.update(lvm=lvm, con=con, keep=keep)
    for name, v in given.items():
        arrays["in_" + name] = v
        a[name] = nc.dram_tensor("in_" + name, v.shape, mybir.dt.from_np(v.dtype), kind="ExternalInput").ap()
    for name, shape in OUTS:
        o[name] = nc.dram_tensor("out_" + name, shape, F32, kind="ExternalOutput").ap()
    scratch = nc.dram_tensor("branch_outputs", (4, FT, P, T), F32, kind="Internal").ap()
    build(nc, a, o, scratch)
    r = run_bass_kernel_spmd(nc, [arrays], core_ids=[0])
    return tuple(r.results[0]["out_" + name] for name, _ in OUTS)
```

```python
from contextlib import ExitStack

import numpy as np

import concourse.bass as bass
from concourse import mybir

F32 = mybir.dt.float32
F32R = mybir.dt.float32r
U8 = mybir.dt.uint8
ALU = mybir.AluOpType
ACT = mybir.ActivationFunctionType
AX = mybir.AxisListType.X

P = 128
D = 1024
KT = D // P
TP = 1024
NS, LS = 8, 8
TS = NS * LS
T = TP + TS
NT = TP // P
W = 512
FT = W // P
H = 4
FF = 4 * D
EPS = 1e-6
QSCALE = float(P) ** -0.5
CD, CC = 31, 3
CH = [(0, 364), (364, 728), (728, T)]
TT_ = [(i * P, min(i * P + P, T)) for i in range(NT + 1)]

SPLITS = dict(qa=0, fa=512, ia=1024, ga=1536, qb=2048, kb=2560, vb=3072, ob=3584, ig=4096, fg=4100,
              bc=4104, cc=4616, xc=5128, ad=5640, gd=6152, gates=6664)

R_CDW, R_CDB, R_LNG, R_LNB, R_CCW, R_NH, R_NM, R_LB = 0, 31, 32, 33, 34, 37, 38, 39
NPAR = 40

PARAMS = (("conv_conformer_w", R_CDW, CD), ("conv_conformer_b", R_CDB, 1), ("ln_conformer_g", R_LNG, 1),
          ("ln_conformer_b", R_LNB, 1), ("conv_short_w", R_CCW, CC), ("norm_hgrn", R_NH, 1),
          ("norm_mlstm", R_NM, 1), ("lb_logits", R_LB, 1))

UNIT = KT * P
SLOTS = 2


def constants():
    m = np.arange(P)
    lv = np.zeros((P, 7, 64), np.float32)
    for i in range(7):
        s = 1 << i
        blocks = P // (2 * s)
        one = np.zeros((P, blocks, s), np.float32)
        for b in range(blocks):
            one[2 * s * b:2 * s * b + s, b, :] = 1
        lv[:, i, :] = one.reshape(P, 64)
    neg = np.where(m[:, None] <= m[None, :], 0.0, -1e30).astype(np.float32)
    k = np.arange(TS)
    same = (k[:, None] // LS == k[None, :] // LS) & (k[:, None] <= k[None, :])
    negs = np.full((P, TS), -1e30, np.float32)
    negs[:TS] = np.where(same, 0.0, -1e30)
    bm = np.zeros((P, NS), np.float32)
    bm[:TS] = (k[:, None] // LS == np.arange(NS)[None, :])
    sel = np.zeros((P, H, P), np.float32)
    for h in range(H):
        sel[h, h] = 1.0
    keep = np.ones((P, T), np.float32)
    keep[:, 0:TP:P] = 0.0
    keep[:, TP::LS] = 0.0
    f = np.concatenate([np.eye(P, dtype=np.float32), neg, negs, bm, sel.reshape(P, H * P),
                        np.ones((P, P), np.float32)], axis=1)
    return lv.reshape(P, 7 * 64), np.ascontiguousarray(f), np.ascontiguousarray(keep[:4])


def plan():
    units = []

    def unit(kind, name, idx):
        units.append((kind, name, idx))
        return len(units) - 1

    def groups(u):
        kind = units[u][0]
        n = 9 if kind == "tok" else 3
        out = []
        for g in range(n):
            out += [("half", u, g, 0), ("half", u, g, 1)]
        return out

    pool_conv = [("pool_tap", 0, j) for j in range(CD)]
    conv = [("tap", t, j) for t in range(1, FT) for j in range(CD)]
    items = []
    seen_ad = 0
    count = [0]

    def pace(it, tiles):
        if it[3] == 1:
            count[0] += 1
            if pool_conv and tiles and count[0] % 3:
                items.append(pool_conv.pop(0))
            for _ in range(2):
                if conv and conv[0][1] < tiles:
                    items.append(conv.pop(0))

    for t in range(FT):
        for nm in ("gd", "ad"):
            for it in groups(unit("feat", nm, t)):
                items.append(it)
                pace(it, seen_ad)
        seen_ad += 1
    for t in range(FT):
        for nm in ("cc", "xc", "bc"):
            for it in groups(unit("feat", nm, t)):
                items.append(it)
                pace(it, FT)
            if nm == "xc":
                items.append(("short", t))
    items += pool_conv + conv
    items.append(("states_cd",))

    def merge(a, b, at):
        def length(item):
            return 0 if item[0] != "half" else 1 if units[item[1]][0] == "tok" else 2.7
        total, past, used, out = sum(length(i) for i in a), 0, 0, []
        for item in a:
            out.append(item)
            past += length(item)
            while used < len(b) and past >= at[used] * total:
                out.append(b[used])
                used += 1
        return out + b[used:]

    a_names, b_names = ("qa", "fa", "ga"), ("qb", "kb", "ob")
    a_stages = ["lv%d" % i for i in range(8)] + ["turn", "state", "out", "norm", "scale", "gate"]
    b_stages = ["decay", "score", "turn", "state", "out", "norm", "scale", "gate"]
    a_at = [0.03 + 0.066 * i for i in range(8)] + [0.57, 0.63, 0.74, 0.76, 0.84, 1]
    b_at = [0.03, 0.25, 0.38, 0.5, 0.7, 0.72, 0.8, 1]
    b_third = [0, 0.2, 0.3, 0.42, 0.6, 0.62, 0.75, 1]
    b_last = [0, 0.3, 0.35, 0.5, 0.8, 0.8, 0.9, 1]

    def heads(names, h):
        out = []
        for nm in names:
            if nm == "ga":
                out.append(("rec", "A", "prepq", h))
            out += groups(unit("feat", nm, h))
        return out

    def value(name, p):
        return groups(unit("tok", name, 2 * p)) + groups(unit("tok", name, 2 * p + 1))

    def rec(x, h, stages):
        return [("rec", x, s, h) for s in stages]

    first = value("ia", 0) + heads(a_names, 0)
    norm = [(4, "mean", 0), (6, "centre", 0)] + [(at, "square", t) for t, at in enumerate((9, 10, 15, 18))] + \
           [(at, "var", t) for t, at in enumerate((14, 17, 20, 23))] + [(26, "root", 0)] + \
           [(28 + 2 * j, "invert", j) for j in range(4)] + [(36 + t, "scale", t) for t in range(FT)] + \
           [(40 + 2 * t, "gate", t) for t in range(FT)] + [(48, "store", 0), (51, "stored", 0)]
    first = [item for item in first if item[0] == "half"]
    for i, item in enumerate(first):
        items += [("ln", stage, t) for at, stage, t in norm if at == i]
        items.append(item)
    items.append(("rec", "A", "prepq", 0))
    items += [("rec", "A", "prep", 0)] + merge(heads(a_names, 1), rec("A", 0, a_stages), a_at)
    items += [("rec", "A", "prep", 1)] + merge(heads(a_names, 2), rec("A", 1, a_stages), a_at)
    items += value("ia", 1)
    items += [("rec", "A", "prep", 2)] + merge(heads(a_names, 3), rec("A", 2, a_stages), a_at)
    items += [("rec", "A", "prep", 3)] + \
        merge(groups(unit("if", "if", 0)) + value("vb", 0), rec("A", 3, a_stages), a_at)
    items += [("phase", 2), ("rows",)]
    first = heads(b_names, 0)
    items += first[:12] + [("rows_exps",)] + first[12:] + [("rows_out",)]
    items += [("rec", "B", "prep", 0)] + merge(heads(b_names, 1), rec("B", 0, b_stages), b_at)
    items += [("rec", "B", "prep", 1)] + merge(heads(b_names, 2), rec("B", 1, b_stages), b_at)
    items += value("vb", 1)
    items += [("rec", "B", "prep", 2)] + merge(heads(b_names[:2], 3), rec("B", 2, b_stages), b_third)
    items += [("rec", "B", "prep", 3)] + merge(heads(b_names[2:], 3), rec("B", 3, b_stages), b_last)
    items.append(("phase", 3))
    return units, items


UNITS, ITEMS = plan()
NU = len(UNITS)
IF_U = [k for k, _, _ in UNITS].index("if")
FILLS = [0]
for _k, _n, _i in UNITS:
    FILLS.append(FILLS[-1] + (3 if _k == "tok" else 1))
GROUPS = [0]
for _k, _n, _i in UNITS:
    GROUPS.append(GROUPS[-1] + (9 if _k == "tok" else 3))
M_U, M_B, M_G = NU, FILLS[-1], GROUPS[-1]
M_UN, M_BN, M_GN = 12, 16, 48
M_IT = 4
O_U, O_B, O_G = M_U + M_IT * M_UN, M_B + M_IT * M_BN, M_G + M_IT * M_GN
O_UN, O_BN, O_GN, O_IT = 4, 12, 36, 2
MERGED_PARTS = [(0, 0, 3 * P), (1, 0, 3 * P), (0, 3 * P, T), (1, 3 * P, T)] + [(k, 0, T) for k in range(2, KT)]
L_U, L_B, L_G = O_U + O_IT * O_UN, O_B + O_IT * O_BN, O_G + O_IT * O_GN
L_UN, L_BN, L_GN, L_IT = 8, 16, 48, 8
ALL_U = L_U + L_IT * L_UN
C_ID, C_NEG, C_NEGS, C_BM, C_SEL, C_ONE = 0, 128, 256, 320, 328, 840
NCON = 968


def build(nc, a, o, scratch):
    with ExitStack() as top:
        top.enter_context(nc.allow_non_contiguous_dma(reason="a few columns of states and biases"))

        def sb(stack, name, shape, dt=F32):
            return stack.enter_context(nc.sbuf_tensor(name, shape, dt))

        sems = {}

        def sem(name):
            if name not in sems:
                sems[name] = top.enter_context(nc.semaphore(name))
            return sems[name]

        h_hi = sb(top, "h_hi", [P, KT, T], F32R)
        h_lo = sb(top, "h_lo", [P, KT, T], F32R)
        w_raw = sb(top, "w_raw", [P, SLOTS, UNIT])
        w_hi = sb(top, "w_hi", [P, SLOTS, UNIT], F32R)
        w_lo = sb(top, "w_lo", [P, SLOTS, UNIT], F32R)
        con = sb(top, "con", [P, NCON])
        lvm = sb(top, "lvm", [P, 7, 512], U8)
        par = sb(top, "par", [P, FT, NPAR])
        nrm = sb(top, "nrm", [P, 16])
        biases = sb(top, "biases", [H, 2])
        lbt = sb(top, "lbt", [P, 4, FT])
        ss = sb(top, "ss", [P, 16])
        rs = sb(top, "rs", [P, 16])
        mhalf = sb(top, "mhalf", [P, 16])
        acc = top.enter_context(nc.psum_tensor("acc", [P, 3, 512], F32))
        pz = top.enter_context(nc.psum_tensor("pz", [P, 5, 512], F32))
        ident = con[:, C_ID:C_ID + P]
        negm = con[:, C_NEG:C_NEG + P]
        negs = con[0:TS, C_NEGS:C_NEGS + TS]
        bmask = con[0:TS, C_BM:C_BM + NS]
        ones = con[:, C_ONE:C_ONE + P]

        def sel(h):
            return con[0:H, C_SEL + h * P:C_SEL + h * P + P]

        with ExitStack() as st:
            xin = sb(st, "xin", [P, NT + 1, D])
            xt = sb(st, "xt", [P, 2, D])
            junk0 = sb(st, "junk0", [P, 2, D])
            full0 = sb(st, "full0", [P, 4, 512])
            prow = sb(st, "prow", [NPAR, W])
            nrow = sb(st, "nrow", [16, P])
        with ExitStack() as st:
            y_d = sb(st, "y_d", [P, FT, T])
            sg_d = sb(st, "sg_d", [P, T])
            y_c = sb(st, "y_c", [P, T])
            ln_t = sb(st, "ln_t", [P, T])
            ln_r = sb(st, "ln_r", [P, T])
            taild = sb(st, "taild", [P, W])
            tailc = sb(st, "tailc", [P, W])
            e_d = sb(st, "e_d", [P, FT, TP + CD - 1])
            e_ds = sb(st, "e_ds", [P, FT, NS, LS + CD - 1])
            e_c = sb(st, "e_c", [P, TP + CC - 1])
            e_cs = sb(st, "e_cs", [P, NS, LS + CC - 1])
            e_cs_old = sb(st, "e_cs_old", [P, FT, NS, CC - 1])
            o_c = sb(st, "o_c", [P, T])
            bufd = sb(st, "bufd", [120, 2, W])
            bufc = sb(st, "bufc", [16, W])
            lvf = sb(st, "lvf", [P, 7, 64])
            tap_prod = sb(st, "tap_prod", [P, 2, T])
            endc = sb(st, "endc", [P, FT, P])
            endd = sb(st, "endd", [P, FT, P])
        with ExitStack() as st:
            tree = sb(st, "tree", [P, T])
            sa = sb(st, "sa", [P, (NT + 1) * P])
            kta = sb(st, "kta", [P, NT + 1, P])
            s0a = sb(st, "s0a", [P, NS, P])
            qza = sb(st, "qza", [P, NS * (TS + LS)])
            sqa = sb(st, "sqa", [P, NT + 1, P])
            vza = sb(st, "vza", [TS, NS, P])
            ota = sb(st, "ota", [P, NT + 1, P])
            sta = sb(st, "sta", [P, NT, P])
            sna = sb(st, "sna", [P, NS, P])
            va = sb(st, "va", [P, NT + 1, 256])
            proj_a = sb(st, "proj_a", [P, 2, 5, T])
            ga, qa, ka, fa, sga = [proj_a[:, :, j, :] for j in range(5)]
        with ExitStack() as st:
            kb = sb(st, "kb", [P, 2, T])
            gb = sb(st, "gb", [P, 2, T])
            qb = sb(st, "qb", [P, 2, T])
            qs = sb(st, "qs", [P, T])
            wb = sb(st, "wb", [P, (NT + 1) * P])
            cnb = sb(st, "cnb", [P, NT, P + 2])
            c0b = sb(st, "c0b", [P, NS, P + 2])
            cnew = sb(st, "cnew", [P, NS, P + 2])
            vzb = sb(st, "vzb", [TS, NS, P])
            mp = sb(st, "mp", [H, 16])
            nlast = sb(st, "nlast", [H, 16])
            den = sb(st, "den", [P, 16])
            cdr = sb(st, "cdr", [H, 16])
            cdc = sb(st, "cdc", [P, H, 16])
            m0 = sb(st, "m0", [H, 16])
            nup = sb(st, "nup", [P, NS])
            vb = sb(st, "vb", [P, NT + 1, 2, P + 2])
            ktb = sb(st, "ktb", [P, NT + 1, P])
            sqb = sb(st, "sqb", [P, NT + 1, P])
            otb = sb(st, "otb", [P, NT + 1, P])
            qzb = sb(st, "qzb", [P, NS * (TS + LS)])
            nM = sb(st, "nM", [H, T])
            wint = sb(st, "wint", [H, T])
            cols = sb(st, "cols", [P, NT + 1, P])
            mrow = sb(st, "mrow", [H, T])
            keepr = sb(st, "keepr", [H, T])
            irow = ktb[:, :, :].rearrange("p c n -> p (c n)")[0:H, 0:T]
            frow = sqb[:, :, :].rearrange("p c n -> p (c n)")[0:H, 0:T]
            brow = kb[0:H, 1, :]
            arow = gb[0:H, 1, :]
            trow = qb[0:H, 1, :]
            urow = qs[0:H, :]
            rt = wb[:, 0:T]
        with ExitStack() as st:
            gsig = sb(st, "gsig", [P, 2, T])
            gtmp = sb(st, "gtmp", [P, 2, 364])
            b_hi = sb(st, "b_hi", [P, FT, T], F32R)
            b_lo = sb(st, "b_lo", [P, FT, T], F32R)
            merged = sb(st, "merged", [P, KT, T])
            b_raw = sb(st, "b_raw", [P, 2, T])
        with ExitStack() as st:
            x1 = sb(st, "x1", [P, NT + 1, D])
            u_hi = sb(st, "u_hi", [P, FT, T], F32R)
            u_lo = sb(st, "u_lo", [P, FT, T], F32R)
            ur = sb(st, "ur", [P, 2, 364])
            uu = sb(st, "uu", [P, 2, 364])
            full1 = sb(st, "full1", [P, 4, 512])
            xt1 = sb(st, "xt1", [P, 2, D])
            junk1 = sb(st, "junk1", [P, 2, D])
            gfin = sb(st, "gfin", [P, D])

        x_tiles = [a["x_prompt"][0, i * P:(i + 1) * P, :] for i in range(NT)] + \
                  [a["x_sample"].rearrange("b t d -> (b t) d")]
        y_tiles = [o["y_p"][0, i * P:(i + 1) * P, :] for i in range(NT)] + \
                  [o["y_s"].rearrange("b t d -> (b t) d")]
        rows_of = [P] * NT + [TS]
        w_in = a["w_in"][0]
        w_branch = a["w_branch"].rearrange("l n c d -> (l n c) d")
        w_down = a["w_down"].rearrange("l f d -> (l f) d")

        def unit_source(kind, name, idx):
            c = SPLITS[name] if name in SPLITS else 0
            if kind == "feat":
                return w_in[:, c + idx * P:c + (idx + 1) * P].rearrange("(k p) n -> p k n", p=P)
            p_, half = idx // 2, idx % 2
            return w_in[half * 512:half * 512 + 512, c + p_ * 256:c + p_ * 256 + 256] \
                .rearrange("(k p) n -> p k n", p=P)

        w_loaded = [sem(f"w_loaded{s}") for s in range(SLOTS)]
        hi_ready, w_ready = sem("hi_ready"), sem("w_ready")
        unit_used, group_ready = sem("unit_used"), sem("group_ready")
        acc_free = [sem(f"acc_free{b}") for b in range(3)]
        con_in, consts_in, params_in = sem("con_in"), sem("consts_in"), sem("params_in")
        x_in = [sem(f"x_in{i}") for i in range(NT + 1)]

        def load_params(eng, some):
            for nm, r0, n in some:
                eng.dma_start(prow[r0:r0 + n, :], a[nm][0] if n > 1 else a[nm]).then_inc(params_in, 16)

        def load_c0(sp, h):
            sp.dma_start(c0b[:, :, 0:P], a["state_mlstm_c"][0, :, h].rearrange("b d v -> d b v")) \
                .then_inc(sem("c0_in"), 16)
            sp.dma_start(c0b[:, :, P:P + 1], a["state_mlstm_n"][0, :, h].rearrange("b (d a) -> d b a", a=1)) \
                .then_inc(sem("c0_in"), 16)

        def full_of(full, i, hh):
            return full[:, 2 * (i % 2) + hh, :].rearrange("p (k n) -> p k n", k=4)[:, :, 0:rows_of[i]]

        n_branches = []

        block = top.enter_context(nc.Block())
        NAMES = ("pe", "act", "pool", "dve", "sp")

        def phase_end(eng, me, n, wait=True):
            if me != "sp":
                eng.drain().then_inc(sem("phase_" + me), 1)
            elif n < 3:
                eng.nop().then_inc(sem("phase_sp"), 1)
            for x in NAMES:
                if wait and x != me and not (x == "sp" and n > 1):
                    eng.wait_ge(sem("phase_" + x), n)

        @block.sync
        def _(sp):
            def unit_load(u):
                kind, name, idx = UNITS[u]
                s = u % SLOTS
                if u >= SLOTS:
                    sp.wait_ge(w_ready, u - SLOTS + 1)
                dst = w_raw[:, s, :]
                if kind == "if":
                    d4 = dst.rearrange("p (k n) -> p k n", k=KT)
                    sp.dma_start(d4[:, :, 0:8], w_in[:, SPLITS["ig"]:SPLITS["ig"] + 8]
                                 .rearrange("(k p) n -> p k n", p=P)).then_inc(w_loaded[s], 16)
                else:
                    k = KT if kind == "feat" else 4
                    sp.dma_start(dst.rearrange("p (k n) -> p k n", k=k),
                                 unit_source(kind, name, idx)).then_inc(w_loaded[s], 16)

            for i in range(NT + 1):
                sp.dma_start(xin[0:rows_of[i], i, :], x_tiles[i]).then_inc(x_in[i], 16)
                if i == 0:
                    sp.dma_start(ident, a["con"][:, C_ID:C_ID + P]).then_inc(con_in, 16)
                if i == 1:
                    load_params(sp, PARAMS[3:])
                    sp.dma_start(nrow[0:8, :], a["norm_mix"][0].rearrange("(a b) -> a b", b=P)).then_inc(params_in, 16)
                    sp.dma_start(nrow[8:16, :], a["norm_mlp"][0].rearrange("(a b) -> a b", b=P)).then_inc(params_in, 16)
            unit_load(0)
            sp.dma_start(con[:, C_ID + P:], a["con"][:, C_ID + P:]).then_inc(consts_in, 16)
            sp.dma_start(biases[:, 0:1], a["mlstm_i_bias"].rearrange("a b -> b a")).then_inc(consts_in, 16)
            sp.dma_start(biases[:, 1:2], a["mlstm_f_bias"].rearrange("a b -> b a")).then_inc(consts_in, 16)
            unit_load(1)
            phase_end(sp, "sp", 1)
            sp.dma_start(lvf[:, :, :].rearrange("p a b -> p (a b)"), a["lvm"]).then_inc(consts_in, 16)
            for j in range(2):
                sp.dma_start(bufd[:, j, :], a["state_conv_conformer"][0, 4 * j:4 * j + 4]
                             .rearrange("b t c -> (b t) c")).then_inc(sem("buf_in"), 16)
            sp.dma_start(bufc[:, :], a["state_conv_short"][0].rearrange("b t c -> (b t) c")).then_inc(sem("buf_in"), 16)
            out_sem = sem("stored")
            n_out = [0]

            def store(dst, src):
                sp.dma_start(dst, src).then_inc(out_sem, 16)
                n_out[0] += 16

            store(o["cd_s"][0, :, 0:CD - 1 - LS, :], a["state_conv_conformer"][0, :, LS:CD - 1, :])

            def loop_load(base, i, n, s, dst, src):
                sp.wait_ge(w_ready, base + i * n + s - SLOTS + 1)
                sp.dma_start(dst, src).then_inc(w_loaded[(base + s) % SLOTS], 16)

            def raw(u, k):
                return w_raw[:, u % SLOTS, :].rearrange("p (k n) -> p k n", k=k)

            def merge_load(i, s):
                i2, s2 = i + s // M_UN, s % M_UN
                pair, j = s2 // 3, s2 % 3
                if j < 2:
                    loop_load(M_U, i, M_UN, s, raw(M_U + s, KT),
                              w_in[:, bass.ds(i2 * D + SPLITS["gates"] + (2 * pair + j) * P, P)]
                              .rearrange("(k p) n -> p k n", p=P))
                else:
                    loop_load(M_U, i, M_UN, s, raw(M_U + s, FT),
                              w_branch[bass.ds(i2 * W, W), pair * 256:(pair + 1) * 256]
                              .rearrange("(k p) n -> p k n", p=P))

            nxt = 2
            for it in ITEMS:
                if it[0] == "half" and it[2] == 0 and it[3] == 0 and nxt < NU and nxt <= it[1] + 2:
                    unit_load(nxt)
                    nxt += 1
                elif it == ("half", NU - 1, 0, 0):
                    merge_load(0, 0)
                elif it[0] == "half" and it[3] == 1 and it[2] == 2 and UNITS[it[1]][1] == "bc":
                    t = UNITS[it[1]][2]
                    sp.wait_ge(sem("oc_done"), 3 * t + 3)
                    store(scratch[2, t], o_c[:, :])
                    sp.wait_ge(out_sem, n_out[0])
                    sp.nop().then_inc(sem("oc_stored"), 1)
                elif it[0] == "states_cd":
                    sp.wait_ge(sem("tails_done"), 2)
                    for b in range(NS):
                        store(o["cc_s"][0, b], tailc[64 + 8 * b + LS - CC + 1:64 + 8 * b + 8, :])
                        store(o["cd_s"][0, b, CD - 1 - LS:, :], taild[64 + 8 * b:64 + 8 * b + 8, :])
                    store(o["cc_p"][0, 0], tailc[64 - CC + 1:64, :])
                    store(o["cd_p"][0, 0], taild[64 - CD + 1:64, :])
                elif it[0] == "ln" and it[1] == "store":
                    for t in range(FT):
                        sp.wait_ge(sem("od_done"), t + 1)
                        store(scratch[3, t], y_d[:, t, :])
                elif it[0] == "ln" and it[1] == "stored":
                    sp.wait_ge(out_sem, n_out[0])
                    sp.nop().then_inc(sem("od_stored"), 1)
                    sp.dma_start(s0a[:, :, :], a["state_hgrn"][0, :, 0].rearrange("b d v -> d b v")) \
                        .then_inc(sem("s0_in"), 16)
                elif it[0] == "rec" and it[2] == "norm":
                    x, h = it[1], it[3]
                    if x == "A":
                        sp.wait_ge(sem("a_ms"), h + 1)
                        store(o["hg_p"][0, 0, h], sta[:, NT - 1, :])
                        store(o["hg_s"][0, :, h].rearrange("b d v -> d b v"), sna[:, :, :])
                    else:
                        if h == H - 1:
                            merge_load(0, 1)
                        sp.wait_ge(sem("b_ms"), h + 1)
                        store(o["mc_p"][0, 0, h], cnb[:, NT - 1, 0:P])
                        store(o["mn_p"][0, 0, h].rearrange("(d a) -> d a", a=1), cnb[:, NT - 1, P:P + 1])
                        store(o["mc_s"][0, :, h].rearrange("b d v -> d b v"), cnew[:, :, 0:P])
                        store(o["mn_s"][0, :, h].rearrange("b (d a) -> d b a", a=1), cnew[:, :, P:P + 1])
                elif it[0] == "rec" and it[2] == "gate":
                    x, h = it[1], it[3]
                    if x == "A":
                        sp.wait_ge(sem("a_gated"), h + 1)
                        store(scratch[0, h], ga[:, h % 2, :])
                        if h + 1 < H:
                            sp.dma_start(s0a[:, :, :], a["state_hgrn"][0, :, h + 1].rearrange("b d v -> d b v")) \
                                .then_inc(sem("s0_in"), 16)
                        sp.wait_ge(out_sem, n_out[0])
                        sp.nop().then_inc(sem("a_stored"), 1)
                        if h == H - 1:
                            phase_end(sp, "sp", 2)
                            sp.dma_start(m0[:, 0:NS], a["state_mlstm_m"][0].rearrange("b h -> h b")) \
                                .then_inc(sem("m0_in"), 16)
                            sp.dma_start(keepr[:, :], a["keep"]).then_inc(sem("m0_in"), 16)
                            load_c0(sp, 0)
                    else:
                        sp.wait_ge(sem("b_gated"), h + 1)
                        store(scratch[1, h], gb[:, h % 2, :])
                        if h + 1 < H:
                            load_c0(sp, h + 1)
                        if h < H - 1:
                            sp.wait_ge(out_sem, n_out[0])
                            sp.nop().then_inc(sem("b_stored"), 1)
                elif it[0] == "rows":
                    sp.wait_ge(sem("m_done"), 1)
                    store(o["mm_p"][0].rearrange("a h -> h a"), mrow[:, TP - 1:TP])
                    store(o["mm_s"][0].rearrange("b h -> h b"),
                          mrow[:, TP:T].rearrange("h (b t) -> h b t", t=LS)[:, :, LS - 1])
            n_branches.append(n_out[0])

            with sp.Fori(0, M_IT - 1) as i:
                for s in range(SLOTS, M_UN + SLOTS):
                    merge_load(i, s)
            for s in range(SLOTS, M_UN):
                merge_load(M_IT - 1, s)
            for j in range(O_IT * O_UN):
                if j == SLOTS:
                    phase_end(sp, "sp", 4)
                    for hh in range(2):
                        for i in range(NT + 1):
                            sp.dma_start(x1[0:rows_of[i], i, hh * 512:(hh + 1) * 512],
                                         x_tiles[i][:, hh * 512:(hh + 1) * 512]) \
                                .then_inc(sem("xres_in") if hh else x_in[i], 16)
                sp.wait_ge(w_ready, O_U + j - SLOTS + 1)
                k0, c0 = j % O_UN * 256, j // O_UN * 512
                sp.dma_start(raw(O_U + j, 2), a["w_out"][0, k0:k0 + 256, c0:c0 + 512]
                             .rearrange("(k p) n -> p k n", p=P)).then_inc(w_loaded[(O_U + j) % SLOTS], 16)
            with sp.Fori(0, L_IT) as i:
                for s in range(4):
                    loop_load(L_U, i, L_UN, s, raw(L_U + s, KT),
                              a["w_up"][0, :, bass.ds(i * 512 + s * P, P)].rearrange("(k p) n -> p k n", p=P))
                for s in range(4):
                    loop_load(L_U, i, L_UN, 4 + s, raw(L_U + s, 2),
                              w_down[bass.ds(i * 512 + (s // 2) * 256, 256), (s % 2) * 512:(s % 2 + 1) * 512]
                              .rearrange("(k p) n -> p k n", p=P))
            sp.wait_ge(w_ready, ALL_U - SLOTS + 1)
            sp.dma_start(raw(ALL_U, KT), a["w_up"][0, :, 0:P].rearrange("(k p) n -> p k n", p=P)) \
                .then_inc(w_loaded[ALL_U % SLOTS], 16)
            for i in (0, 2, 3, 1, 4, 5, 6, 7, NT):
                sp.wait_ge(sem("y_done" if i >= 2 else "y_done_pool"), i - 1 if i >= 2 else i + 1)
                store(y_tiles[i], x1[0:rows_of[i], i, :])
            sp.wait_ge(out_sem, n_out[0])

        @block.tensor
        def _(pe):
            def product(out, lh, ll, rh, rl, first, last):
                pe.matmul(out, lh, rh, start=first, stop=False)
                pe.matmul(out, lh, rl, start=False, stop=False)
                return pe.matmul(out, ll, rh, start=False, stop=last)

            def w_tile(w, s, k, c0, c1, nk=KT):
                return w[:, s, :].rearrange("p (k n) -> p k n", k=nk)[:, k, c0:c1]

            def feat_mm(s, g, ks, src_hi, src_lo, nk=KT, col=0):
                c0, c1 = CH[g]
                for k in ks:
                    mm = product(acc[:, g, 0:c1 - c0], w_tile(w_hi, s, k, col, col + P, nk),
                                 w_tile(w_lo, s, k, col, col + P, nk),
                                 src_hi[:, k, c0:c1], src_lo[:, k, c0:c1], k == 0, k == nk - 1)
                return mm

            def wide_mm(s, i, src_hi, src_lo, k0):
                t0, t1 = TT_[i]
                for k in range(2):
                    mm = product(acc[0:t1 - t0, i % 3, :], src_hi[:, k0 + k, t0:t1], src_lo[:, k0 + k, t0:t1],
                                 w_tile(w_hi, s, k, 0, 512, 2), w_tile(w_lo, s, k, 0, 512, 2), k == 0, k == 1)
                return mm

            def tok_mm(s, i, ks, src_hi, src_lo, k0=0):
                t0, t1 = TT_[i]
                for k in ks:
                    mm = product(acc[0:t1 - t0, i % 3, 0:256], src_hi[:, k0 + k, t0:t1], src_lo[:, k0 + k, t0:t1],
                                 w_tile(w_hi, s, k, 0, 256, 4), w_tile(w_lo, s, k, 0, 256, 4), k == 0, k == 3)
                return mm

            def turn_params():
                pe.wait_ge(params_in, 16 * 10)
                for t in range(FT):
                    pe.transpose(pz[:, 0, t * NPAR:(t + 1) * NPAR], prow[:, t * P:(t + 1) * P],
                                 ident[0:NPAR, 0:NPAR])
                pe.transpose(pz[:, 0, FT * NPAR:FT * NPAR + 16], nrow[:, :], ident[0:16, 0:16]) \
                    .then_inc(sem("params_turned"), 1)

            def turn_tokens(src, pre, scaled):
                for i in range(NT + 1):
                    n = rows_of[i]
                    pe.wait_ge(sem(scaled), i + 1)
                    for hh in range(2):
                        if i >= 2:
                            pe.wait_ge(sem(pre + "_full"), 2 * i + hh - 3)
                        for k in range(4):
                            tr = pe.transpose(pz[:, 1 + 2 * (i % 2) + hh, k * P:k * P + n],
                                              src[0:n, i % 2, (4 * hh + k) * P:(4 * hh + k + 1) * P],
                                              ident[0:n, 0:n])
                        tr.then_inc(sem(pre + "_turned"), 1)
                    if i == 0 and pre == "x":
                        turn_params()

            pe.wait_ge(con_in, 16)
            def tokens_in(pre, g):
                n = (3, 6, NT + 1)[g]
                pe.wait_ge(sem(pre + "_hi"), 2 * n)
                pe.wait_ge(sem(pre + "_lo_a"), n)
                pe.wait_ge(sem(pre + "_lo_b"), n)

            turn_tokens(xt, "x", "x_scaled")
            phase_end(pe, "pe", 1, wait=False)

            def convs_in():
                pe.wait_ge(sem("buf_in"), 16 * 3)
                for j in range(2):
                    for t in range(FT):
                        pe.transpose(pz[:, j, t * 120:t * 120 + 120], bufd[:, j, t * P:(t + 1) * P],
                                     ident[0:120, 0:120])
                for t in range(FT):
                    tr = pe.transpose(pz[:, 2, t * 16:t * 16 + 16], bufc[:, t * P:(t + 1) * P], ident[0:16, 0:16])
                tr.then_inc(sem("bufs_turned"), 1)

            def rec_a(s, h):
                b2 = h % 2
                q, k = qa[:, b2, :], ka[:, b2, :]
                hc = (h % 2) * P
                if s == "prep":
                    return
                if s.startswith("lv"):
                    lv = int(s[2:])
                    if lv == 0:
                        pe.wait_ge(sem("a_prep"), h + 1)
                        if h >= 1:
                            pe.wait_ge(sem("a_gated"), h)
                        for c in range(NT):
                            pe.matmul(pz[:, c // 4, (c % 4) * P:(c % 4 + 1) * P], k[:, c * P:(c + 1) * P],
                                      q[:, c * P:(c + 1) * P], start=True, stop=True)
                        pe.matmul(pz[0:TS, 2, 0:TS], k[:, TP:T], q[:, TP:T], start=True, stop=True) \
                            .then_inc(sem("a_scored"), 1)
                        return
                    sz = 1 << (lv - 1)
                    if lv == 1:
                        pe.wait_ge(sem("a_q1"), h + 1)
                    else:
                        pe.wait_ge(sem("a_lv"), 7 * h + lv - 1)
                    q = sga[:, b2, :]
                    if lv >= 2:
                        pe.wait_ge(sem("a_masked"), 8 * h + lv - 1)
                    bank, sbank = (3, 4) if lv % 2 else (0, 2)
                    for c in range(NT):
                        qo = q[:, c * P:(c + 1) * P].rearrange("p (b two s) -> p b two s", two=2, s=sz)[:, :, 1, :]
                        mm = pe.matmul(pz[:, bank, c * 64:(c + 1) * 64].rearrange("p (b s) -> p b s", s=sz),
                                       k[:, c * P:(c + 1) * P], qo, start=True, stop=True)
                    if lv <= 3:
                        qo = q[:, TP:T].rearrange("p (b two s) -> p b two s", two=2, s=sz)[:, :, 1, :]
                        mm = pe.matmul(pz[0:TS, sbank, 0:32].rearrange("p (b s) -> p b s", s=sz),
                                       k[:, TP:T], qo, start=True, stop=True)
                    mm.then_inc(sem("a_scored"), 1)
                elif s == "turn":
                    pe.wait_ge(sem("a_lv"), 7 * h + 7)
                    pe.wait_ge(sem("a_masked"), 8 * h + 8)
                    for c in range(NT):
                        pe.transpose(pz[:, c // 4, (c % 4) * P:(c % 4 + 1) * P], k[:, c * P:(c + 1) * P], ident)
                    pe.transpose(pz[0:TS, 2, 0:P], k[:, TP:T], ident).then_inc(sem("a_kturned"), 1)
                elif s == "state":
                    pe.wait_ge(sem("a_kt"), h + 1)
                    for c in range(NT):
                        pe.matmul(pz[:, 3 + c // 4, (c % 4) * P:(c % 4 + 1) * P], kta[:, c, :],
                                  va[:, c, hc:hc + P], start=True, stop=True)
                    pe.wait_ge(sem("a_vz"), h + 1)
                    for j in range(2):
                        mm = pe.matmul(pz[:, j, :], kta[0:TS, NT, :],
                                       vza[:, 4 * j:4 * j + 4, :].rearrange("p b v -> p (b v)"),
                                       start=True, stop=True)
                    mm.then_inc(sem("a_updates"), 1)
                elif s == "out":
                    pe.wait_ge(sem("a_states"), h + 1)
                    q = sga[:, b2, :]
                    pe.wait_ge(sem("a_qz"), h + 1)
                    for c in range(NT):
                        bk = 2 if c < 4 else 3
                        ov = pz[:, bk, (c % 4) * P:(c % 4 + 1) * P]
                        pe.matmul(ov, sa[:, c * P:(c + 1) * P], va[:, c, hc:hc + P], start=True, stop=c == 0)
                        if c:
                            pe.matmul(ov, q[:, c * P:(c + 1) * P], sta[:, c - 1, :], start=False, stop=True)
                    pe.matmul(pz[0:TS, 4, 0:P], sa[0:TS, TP:T], va[0:TS, NT, hc:hc + P], start=True, stop=False)
                    pe.wait_ge(sem("s0_in"), 16 * (h + 1))
                    for b in range(NS):
                        mm = pe.matmul(pz[0:TS, 4, 0:P], qza[:, b * TS:(b + 1) * TS], s0a[:, b, :], start=False,
                                       stop=b == NS - 1)
                    mm.then_inc(sem("a_out"), 1)
                elif s == "norm":
                    return
                elif s == "gate":
                    turn_out("a", ota, h)

            def turn_out(x, ot, h):
                pe.wait_ge(sem(x + "_normed"), h + 1)
                for c in range(NT + 1):
                    n = rows_of[c]
                    tr = pe.transpose(pz[:, c // 4, (c % 4) * P:(c % 4) * P + n], ot[0:n, c, :], ident[0:n, 0:n])
                tr.then_inc(sem(x + "_turned"), 1)

            def rec_b(s, h):
                b2 = h % 2
                q, k = qb[:, b2, :], kb[:, b2, :]
                v1 = vb[:, :, h % 2, :]
                if s == "prep":
                    return
                if s == "decay":
                    if h >= 1:
                        pe.wait_ge(sem("b_gated"), h)
                    pe.wait_ge(sem("b_rows"), 1)
                    for j, (c0, c1) in enumerate(((0, 512), (512, 1024), (1024, T))):
                        pe.matmul(pz[:, j, 0:c1 - c0], sel(h), nM[:, c0:c1], start=True, stop=True)
                    for j, (c0, c1) in enumerate(((0, 512), (512, 1024))):
                        pe.matmul(pz[:, 3 + j, :], sel(h), wint[:, c0:c1], start=True, stop=True)
                    pe.matmul(pz[:, 2, 64:128], sel(h), wint[:, TP:T], start=True, stop=True) \
                        .then_inc(sem("b_spread"), 1)
                elif s == "score":
                    pe.wait_ge(sem("b_decayed"), h + 1)
                    pe.wait_ge(sem("b_proj"), 9 * h + 6)
                    for c in range(NT):
                        pe.matmul(pz[:, c // 4, (c % 4) * P:(c % 4 + 1) * P], k[:, c * P:(c + 1) * P],
                                  q[:, c * P:(c + 1) * P], start=True, stop=True)
                    pe.matmul(pz[0:TS, 2, 0:TS], k[:, TP:T], q[:, TP:T], start=True, stop=True) \
                        .then_inc(sem("b_scored"), 1)
                elif s == "turn":
                    for c in range(NT):
                        pe.transpose(pz[:, 3 + c // 4, (c % 4) * P:(c % 4 + 1) * P], k[:, c * P:(c + 1) * P], ident)
                    pe.wait_ge(sem("b_weighted"), h + 1)
                    pe.transpose(pz[0:TS, 2, 128:128 + P], k[:, TP:T], ident).then_inc(sem("b_kturned"), 1)
                elif s == "state":
                    pe.wait_ge(sem("b_kt"), h + 1)
                    for c in range(NT):
                        pe.matmul(pz[:, (0, 1, 3)[c // 3], (c % 3) * 129:(c % 3) * 129 + 129], ktb[:, c, :],
                                  v1[:, c, 0:P + 1], start=True, stop=True)
                    pe.wait_ge(sem("b_vz"), h + 1)
                    for j, bk in enumerate((2, 4)):
                        pe.matmul(pz[:, bk, :], ktb[0:TS, NT, :],
                                  vzb[:, 4 * j:4 * j + 4, :].rearrange("p b v -> p (b v)"), start=True, stop=True)
                    pe.matmul(pz[:, 3, 400:400 + NS], ktb[0:TS, NT, :], bmask, start=True, stop=True) \
                        .then_inc(sem("b_updates"), 1)
                elif s == "out":
                    pe.wait_ge(sem("b_states"), h + 1)
                    pe.wait_ge(sem("b_qz"), h + 1)
                    for c in range(NT):
                        ov = pz[:, (0, 1, 3)[c // 3], (c % 3) * 129:(c % 3) * 129 + 129]
                        pe.matmul(ov, wb[:, c * P:(c + 1) * P], v1[:, c, 0:P + 1], start=True, stop=c == 0)
                        if c:
                            pe.matmul(ov, qs[:, c * P:(c + 1) * P], cnb[:, c - 1, 0:P + 1], start=False, stop=True)
                    pe.wait_ge(sem("c0_in"), 32 * (h + 1))
                    ov = pz[0:TS, 3, 258:258 + 129]
                    pe.matmul(ov, wb[0:TS, TP:T], v1[0:TS, NT, 0:P + 1], start=True, stop=False)
                    for b in range(NS):
                        mm = pe.matmul(ov, qzb[:, b * TS:(b + 1) * TS], c0b[:, b, 0:P + 1], start=False,
                                       stop=b == NS - 1)
                    mm.then_inc(sem("b_out"), 1)
                elif s == "gate":
                    turn_out("b", otb, h)

            for it in ITEMS:
                if it[0] == "half":
                    _, u, g, hf = it
                    kind, name, idx = UNITS[u]
                    if it == ("half", 1, 0, 0):
                        convs_in()
                    if g == 0 and hf == 0:
                        pe.wait_ge(w_ready, u + 1)
                    if u == 0 and hf == 0:
                        tokens_in("x", g)
                    fill = FILLS[u] + (g // 3 if kind == "tok" else 0)
                    if hf == 0 and fill:
                        pe.wait_ge(acc_free[g % 3], fill)
                    if kind == "tok":
                        mm = tok_mm(u % 2, g, (0, 1) if hf == 0 else (2, 3), h_hi, h_lo, 4 * (idx % 2))
                    else:
                        mm = feat_mm(u % 2, g, range(0, 4) if hf == 0 else range(4, 8), h_hi, h_lo)
                    if hf == 1:
                        mm.then_inc(group_ready, 1)
                elif it[0] == "states_cd":
                    pe.wait_ge(sem("ends_ready"), 8)
                    for t in range(FT):
                        pe.transpose(pz[:, 0, t * P:(t + 1) * P], endd[:, t, :], ident)
                        tr = pe.transpose(pz[:, 1, t * P:(t + 1) * P], endc[:, t, :], ident)
                    tr.then_inc(sem("ends_turned"), 1)
                elif it[0] == "ln":
                    _, stage, t = it
                    cuts = ((0, 512), (512, 1024), (1024, T))
                    if stage == "mean":
                        pe.wait_ge(sem("tails_done"), 2)
                        pe.wait_ge(sem("conv_done"), FT)
                        for k in range(FT):
                            for j, (c0, c1) in enumerate(cuts):
                                mm = pe.matmul(pz[:, j, 0:c1 - c0], ones, y_d[:, k, c0:c1], start=k == 0,
                                               stop=k == FT - 1)
                        mm.then_inc(sem("ln_mean"), 1)
                    elif stage == "var":
                        if t == 0:
                            pe.wait_ge(sem("ln_centred"), FT)
                        pe.wait_ge(sem("ln_squared"), t + 1)
                        for j, (c0, c1) in enumerate(cuts):
                            mm = pe.matmul(pz[:, j, 0:c1 - c0], ones, (ln_t, ln_r)[t % 2][:, c0:c1], start=t == 0,
                                           stop=t == FT - 1)
                        mm.then_inc(sem("ln_var"), 1)
                elif it[0] == "phase":
                    phase_end(pe, "pe", it[1], wait=False)
                elif it[0] == "rows_out":
                    pe.wait_ge(sem("rows_ready"), 1)
                    for c in range(NT + 1):
                        n = rows_of[c]
                        tr = pe.transpose(pz[0:n, c // 4, (c % 4) * P:(c % 4 + 1) * P], rt[:, c * P:c * P + n], ident)
                    for h in range(H):
                        mm = pe.matmul(pz[:, 3, h * 16:h * 16 + 16], sel(h), cdr[:, :], start=True, stop=True)
                    mm.then_inc(sem("rows_turned"), 1)
                elif it[0] == "rec":
                    (rec_a if it[1] == "A" else rec_b)(it[2], it[3])

            with pe.Fori(0, M_IT) as i:
                for s in range(M_UN):
                    pair, j = s // 3, s % 3
                    pe.wait_ge(w_ready, M_U + 1 + s + i * M_UN)
                    if s == 2:
                        pe.wait_ge(sem("branch_ready"), i * FT + FT)
                    for r in range(2 if j == 2 else 1):
                        for g in range(3):
                            pe.wait_ge(acc_free[g], M_B + 4 * pair + j + r + i * M_BN)
                            if j < 2:
                                mm = feat_mm((M_U + s) % 2, g, range(KT), h_hi, h_lo)
                            else:
                                mm = feat_mm((M_U + s) % 2, g, range(FT), b_hi, b_lo, FT, r * P)
                            mm.then_inc(group_ready, 1)
            phase_end(pe, "pe", 4, wait=False)
            with pe.Fori(0, O_IT) as i:
                for s in range(O_UN):
                    pe.wait_ge(w_ready, O_U + 1 + s + i * O_UN)
                    pe.wait_ge(sem("merged_low_a"), (2, 5, 6, 8)[s])
                    if s:
                        pe.wait_ge(sem("merged_low_b"), (0, 1, 2, 2)[s])
                    for c in range(NT + 1):
                        if s == 0 and c == 3:
                            pe.wait_ge(sem("merged_low_a"), 4)
                        pe.wait_ge(acc_free[c % 3], O_B + s * 3 + c // 3 + i * O_BN)
                        wide_mm((O_U + s) % 2, c, h_hi, h_lo, 2 * s).then_inc(group_ready, 1)
            turn_tokens(xt1, "m", "m_scaled")
            phase_end(pe, "pe", 5, wait=False)
            with pe.Fori(0, L_IT) as i:
                for s in range(4):
                    pe.wait_ge(w_ready, L_U + 1 + s + i * L_UN)
                    for g in range(3):
                        if s == 0:
                            tokens_in("m", g)
                        pe.wait_ge(acc_free[g], L_B + s + i * L_BN)
                        feat_mm((L_U + s) % 2, g, range(KT), h_hi, h_lo).then_inc(group_ready, 1)
                for s in range(4):
                    pe.wait_ge(w_ready, L_U + 5 + s + i * L_UN)
                    if s % 2 == 0:
                        pe.wait_ge(sem("u_ready"), i * 12 + 3 * s + 8)
                    for c in range(NT + 1):
                        pe.wait_ge(acc_free[c % 3], L_B + 4 + s * 3 + c // 3 + i * L_BN)
                        wide_mm((L_U + s) % 2, c, u_hi, u_lo, 2 * (s // 2)).then_inc(group_ready, 1)


        @block.scalar
        def _(act):
            def copy(out, in_, **k):
                return act.activation(out, in_, ACT.Copy, **k)

            def split_hi(u):
                s = u % SLOTS
                act.wait_ge(w_loaded[s], 16 * (u // SLOTS + 1))
                if u >= SLOTS:
                    act.wait_ge(group_ready, GROUPS[u - 1])
                if u < NU and UNITS[u][0] == "if":
                    act.wait_ge(sem("if_zero"), 1)
                    raw4 = w_raw[:, s, :].rearrange("p (k n) -> p k n", k=KT)
                    hi4 = w_hi[:, s, :].rearrange("p (k n) -> p k n", k=KT)
                    copy(hi4[:, :, 0:4], raw4[:, :, 0:4])
                    copy(hi4[:, :, 32:36], raw4[:, :, 4:8]).then_inc(hi_ready, 1)
                else:
                    copy(w_hi[:, s, :], w_raw[:, s, :]).then_inc(hi_ready, 1)

            def split_hi_loop(base, gbase, i, n, gn, s, g_before):
                sl = (base + s) % SLOTS
                act.wait_ge(w_loaded[sl], 16 * ((base + s) // SLOTS + 1) + i * (16 * n // SLOTS))
                act.wait_ge(group_ready, gbase + g_before + i * gn)
                copy(w_hi[:, sl, :], w_raw[:, sl, :]).then_inc(hi_ready, 1)

            def norm_all(pre, src, junk, full, wait_in):
                for i in range(NT + 4):
                    if pre == "x" and i == NT - 2:
                        split_hi(0)
                    if i <= NT:
                        n = rows_of[i]
                        wait_in(i)
                        if i >= 2:
                            act.wait_ge(sem(pre + "_sq"), i - 1)
                        act.activation(junk[0:n, i % 2, :], src(i), ACT.Square, accum_out=ss[0:n, i:i + 1]) \
                            .then_inc(sem(pre + "_sq"), 1)
                    if i >= 3:
                        t0, t1 = TT_[i - 3]
                        for hh in range(2):
                            act.wait_ge(sem(pre + "_full"), 2 * (i - 3) + hh + 1)
                            copy(h_hi[:, 4 * hh:4 * hh + 4, t0:t1], full_of(full, i - 3, hh)) \
                                .then_inc(sem(pre + "_hi"), 1)

            load_params(act, PARAMS[:3])
            norm_all("x", lambda i: xin[0:rows_of[i], i, :], junk0, full0, lambda i: act.wait_ge(x_in[i], 16))
            act.wait_ge(sem("lb_diff"), 1)
            act.activation(lbt[:, 1, :], lbt[:, 0, :], ACT.Exp).then_inc(sem("lb_exp"), 1)
            phase_end(act, "act", 1)

            def evac(u, g):
                kind, name, idx = UNITS[u]
                act.wait_ge(group_ready, GROUPS[u] + g + 1)
                if kind == "feat":
                    c0, c1 = CH[g]
                    src = acc[:, g, 0:c1 - c0]
                    if name == "gd":
                        if idx:
                            act.wait_ge(sem("glu_done"), 3 * (idx - 1) + g + 1)
                        act.activation(sg_d[:, c0:c1], src, ACT.Sigmoid).then_inc(acc_free[g], 1)
                        return
                    if name == "cc":
                        if idx and g == 0:
                            act.wait_ge(sem("short_done"), idx)
                            act.wait_ge(sem("ends_ready"), 4 + idx)
                        if g < 2:
                            copy(e_c[:, CC - 1 + c0:CC - 1 + c1], src).then_inc(acc_free[g], 1)
                        else:
                            copy(e_c[:, CC - 1 + c0:], acc[:, g, 0:TP - c0])
                            copy(e_cs[:, :, CC - 1:], acc[:, g, TP - c0:T - c0]
                                 .rearrange("p (b t) -> p b t", t=LS)).then_inc(acc_free[g], 1)
                        return
                    if name == "bc":
                        if idx and g == 0:
                            act.wait_ge(sem("oc_stored"), idx)
                        copy(o_c[:, c0:c1], src).then_inc(acc_free[g], 1)
                        return
                    if name in ("xc", "ad"):
                        return
                    b2, bank = idx % 2, acc_free[g]
                    if g == 0 and name in ("qa", "qb"):
                        if idx >= 2:
                            act.wait_ge(sem(("a" if name == "qa" else "b") + "_stored"), idx - 1)
                        if name == "qb" and idx == 1:
                            act.wait_ge(sem("b_rows"), 1)
                    if name == "qa":
                        act.activation(ka[:, b2, c0:c1], src, ACT.Sigmoid)
                        copy(qa[:, b2, c0:c1], src).then_inc(bank, 1)
                    elif name == "fa":
                        act.activation(fa[:, b2, c0:c1], src, ACT.Sigmoid).then_inc(bank, 1)
                    elif name == "ga":
                        act.activation(sga[:, b2, c0:c1], src, ACT.Sigmoid)
                        copy(ga[:, b2, c0:c1], src).then_inc(bank, 1)
                    elif name == "qb":
                        copy(qb[:, b2, c0:c1], src, scale=QSCALE).then_inc(bank, 1)
                    elif name == "kb":
                        copy(kb[:, b2, c0:c1], src).then_inc(bank, 1)
                    elif name == "ob":
                        act.activation(gb[:, b2, c0:c1], src, ACT.Sigmoid).then_inc(bank, 1)
                    act.wait_ge(bank, FILLS[u] + 1)
                    act.nop().then_inc(sem("a_proj" if name[1] == "a" else "b_proj"), 1)
                elif kind == "if":
                    c0, c1 = CH[g]
                    if g == 0:
                        act.wait_ge(sem("a_gated"), 3)
                    copy(irow[:, c0:c1], acc[0:H, g, 0:c1 - c0])
                    copy(frow[:, c0:c1], acc[32:32 + H, g, 0:c1 - c0]).then_inc(acc_free[g], 1)
                elif idx % 2 == 0:
                    n = rows_of[g]
                    x = "a" if name == "ia" else "b"
                    if x == "a" and idx == 0 and g == 0:
                        act.wait_ge(sem("conv_done"), FT)
                        act.wait_ge(sem("ends_turned"), 1)
                        act.wait_ge(sem("oc_stored"), FT)
                    if x == "b" and idx == 0 and g == 0:
                        act.wait_ge(sem("a_stored"), 3)
                    if idx == 2 and g == 0:
                        act.wait_ge(sem(x + "_out"), 2)
                    dst = va[0:n, g, :] if x == "a" else vb[0:n, g, :, 0:P]
                    src = acc[0:n, g % 3, 0:256]
                    if x == "b":
                        src = src.rearrange("p (h v) -> p h v", h=2)
                    copy(dst, src).then_inc(acc_free[g % 3], 1)

            def out_evac(x, h, ot):
                act.wait_ge(sem(x + "_out"), h + 1)
                if h:
                    act.wait_ge(sem(x + "_gated"), h)
                copy(ot[:, 0:4, :], pz[:, 2, :].rearrange("p (c v) -> p c v", v=P))
                copy(ot[:, 4:8, :], pz[:, 3, :].rearrange("p (c v) -> p c v", v=P))
                copy(ot[0:TS, NT, :], pz[0:TS, 4, 0:P]).then_inc(sem(x + "_oevac"), 1)

            for it in ITEMS:
                if it[0] == "half":
                    _, u, g, hf = it
                    if g == 0 and hf == 0:
                        split_hi(u + 1)
                    if hf == 1:
                        evac(u, g)
                elif it[0] == "states_cd":
                    act.wait_ge(sem("ends_turned"), 1)
                    copy(taild[:, :], pz[:, 0, :]).then_inc(sem("tails_done"), 1)
                    copy(tailc[:, :], pz[:, 1, :]).then_inc(sem("tails_done"), 1)
                elif it[0] == "pool_tap" and it[2]:
                    j = it[2]
                    w = par[:, 0, R_CDW + j:R_CDW + j + 1]
                    if j == 1:
                        act.wait_ge(sem("bufs_in"), 1)
                        act.wait_ge(sem("glu_done"), 3)
                        act.wait_ge(sem("pads_zero"), 1)
                    if j >= 3:
                        act.wait_ge(sem("prod_used"), j - 1)
                    copy(tap_prod[:, j % 2, 0:TP], e_d[:, 0, j:j + TP], scale=w)
                    copy(tap_prod[:, j % 2, TP:T].rearrange("p (b t) -> p b t", t=LS), e_ds[:, 0, :, j:j + LS],
                         scale=w).then_inc(sem("prod_ready"), 1)
                elif it[0] == "ln":
                    _, stage, t = it
                    if stage == "square":
                        act.wait_ge(sem("ln_centred"), t + 1)
                        if t >= 2:
                            act.wait_ge(sem("ln_var"), t - 1)
                        act.activation((ln_t, ln_r)[t % 2][:, :], y_d[:, t, :], ACT.Square) \
                            .then_inc(sem("ln_squared"), 1)
                    elif stage == "root":
                        act.wait_ge(sem("ln_eps"), 1)
                        act.activation(ln_t[:, :], ln_t[:, :], ACT.Sqrt).then_inc(sem("ln_sqrt"), 1)
                    elif stage == "gate":
                        act.wait_ge(sem("ln_affine"), t + 1)
                        if t >= 2:
                            act.wait_ge(sem("od_done"), t - 1)
                        act.activation((sg_d, y_c)[t % 2][:, :], y_d[:, t, :], ACT.Sigmoid) \
                            .then_inc(sem("ln_sig"), 1)
                elif it[0] == "phase":
                    phase_end(act, "act", it[1])
                elif it[0] == "rows":
                    act.wait_ge(sem("f_biased"), 1)
                    act.activation(trow, frow, ACT.Abs).then_inc(sem("row_act"), 1)
                    act.wait_ge(sem("row_act"), 1)
                    act.activation(urow, trow, ACT.Exp, scale=-1.0).then_inc(sem("row_act"), 1)
                    act.wait_ge(sem("row_act"), 2)
                    act.activation(trow, urow, ACT.Ln, bias=1.0).then_inc(sem("row_act"), 1)
                elif it[0] == "rows_exps":
                    act.wait_ge(sem("row_exps"), 1)
                    act.activation(wint[:, :], trow, ACT.Exp).then_inc(sem("row_done"), 1)
                    act.activation(cdr[:, :], nlast[:, :], ACT.Exp).then_inc(sem("row_done"), 1)
                    act.wait_ge(sem("rt_zero"), 1)
                    copy(rt[0:H, :], arow)
                    act.activation(rt[32:32 + H, :], mrow[:, :], ACT.Exp, scale=-1.0)
                    act.activation(rt[64:64 + H, :], urow, ACT.Exp).then_inc(sem("rows_ready"), 1)
                elif it[0] == "rec":
                    _, x, s, h = it
                    if x == "A":
                        if s == "turn":
                            act.wait_ge(sem("a_kturned"), h + 1)
                            copy(kta[:, 0:4, :], pz[:, 0, :].rearrange("p (c v) -> p c v", v=P))
                            copy(kta[:, 4:8, :], pz[:, 1, :].rearrange("p (c v) -> p c v", v=P))
                            copy(kta[0:TS, NT, :], pz[0:TS, 2, 0:P]).then_inc(sem("a_kt"), 1)
                        elif s == "out":
                            out_evac("a", h, ota)
                    else:
                        if s == "score":
                            act.wait_ge(sem("b_decayed"), h + 1)
                            act.activation(wb[:, 0:TP], wb[:, 0:TP], ACT.Exp)
                            act.activation(wb[0:TS, TP:T], wb[0:TS, TP:T], ACT.Exp).then_inc(sem("b_exp"), 1)
                        elif s == "out":
                            act.wait_ge(sem("b_out"), h + 1)
                            for j, (bk, nc_) in enumerate(((0, 3), (1, 3), (3, 2))):
                                act.activation(den[:, 3 * j:3 * j + nc_],
                                               pz[:, bk, 0:129 * nc_].rearrange("p (c n) -> p c n", n=129)[:, :, 128],
                                               ACT.Abs)
                            act.activation(den[0:TS, NT:NT + 1], pz[0:TS, 3, 386:387], ACT.Abs) \
                                .then_inc(sem("b_absden"), 1)

            with act.Fori(0, M_IT) as i:
                for s in range(M_UN):
                    pair, j = s // 3, s % 3
                    done = 12 * pair + 3 * j
                    split_hi_loop(M_U, M_G, i, M_UN, M_GN, s + 1, done)
                    if j < 2:
                        for g in range(3):
                            if s < 2 and g >= 1:
                                t = 2 * s + g - 1
                                act.wait_ge(sem("stored"), n_branches[0])
                                act.wait_ge(sem(f"b_in{t % 2}"), i * 32 + 16 * (t // 2) + 16)
                                copy(b_hi[:, t, :], b_raw[:, t % 2, :]).then_inc(sem("b_hi_ready"), 1)
                            act.wait_ge(group_ready, M_G + done + g + 1 + i * M_GN)
                            if j == 0 and g == 0:
                                act.wait_ge(sem("m_gated"), i * 24 + pair * 6 + 1)
                            c0, c1 = CH[g]
                            act.activation(gsig[:, j, c0:c1], acc[:, g, 0:c1 - c0], ACT.Sigmoid) \
                                .then_inc(acc_free[g], 1)
            phase_end(act, "act", 4)
            for k, t0, t1 in MERGED_PARTS:
                copy(h_hi[:, k, t0:t1], merged[:, k, t0:t1]).then_inc(sem("mh_ready"), 1)
            act.dma_start(gfin[:, :], a["norm_final"].rearrange("(a d) -> a d", a=1).broadcast_to([P, D])) \
                .then_inc(sem("gfin_in"), 16)
            with act.Fori(0, O_IT) as i:
                for s in range(O_UN):
                    split_hi_loop(O_U, O_G, i, O_UN, O_GN, s + 1, 9 * s)
            norm_all("m", lambda i: x1[0:rows_of[i], i, :], junk1, full1,
                     lambda i: act.wait_ge(sem("o_added"), O_IT * O_GN - NT + i))
            phase_end(act, "act", 5)
            with act.Fori(0, L_IT) as i:
                for s in range(L_UN):
                    done = 3 * s if s < 4 else 12 + 9 * (s - 4)
                    split_hi_loop(L_U, L_G, i, L_UN, L_GN, s + 1, done)
                    if s >= 4:
                        continue
                    for g in range(3):
                        c0, c1 = CH[g]
                        e = 3 * s + g
                        act.wait_ge(group_ready, L_G + e + 1 + i * L_GN)
                        act.activation(ur[:, e % 2, 0:c1 - c0], acc[:, g, 0:c1 - c0], ACT.Relu) \
                            .then_inc(sem("u_relu"), 1)
                        act.wait_ge(sem("u_squared"), e + 1 + i * 12)
                        copy(u_hi[:, s, c0:c1], uu[:, e % 2, 0:c1 - c0]).then_inc(sem("u_high"), 1)
            for i in range(NT + 1):
                n = rows_of[i]
                act.wait_ge(sem("l_added"), L_IT * 36 + 1 - NT + i)
                if i >= 2:
                    act.wait_ge(sem("f_sq"), i - 1)
                act.activation(xt1[0:n, i % 2, :], x1[0:n, i, :], ACT.Square, accum_out=ss[0:n, i:i + 1]) \
                    .then_inc(sem("f_sq"), 1)

        @block.gpsimd
        def _(pool):
            links = [0]

            def link(ins):
                links[0] += 1
                ins.then_inc(sem("pool_link"), 1)
                pool.wait_ge(sem("pool_link"), links[0])

            def tt(out, x, y, op):
                return pool.tensor_tensor(out, x, y, op)

            def split_lo(u):
                s = u % SLOTS
                if u < NU and UNITS[u][0] == "if":
                    pool.wait_ge(group_ready, GROUPS[u - 1])
                    pool.memset(w_hi[:, s, :].bitcast(F32), 0.0)
                    link(pool.memset(w_lo[:, s, :].bitcast(F32), 0.0))
                    pool.nop().then_inc(sem("if_zero"), 1)
                    pool.wait_ge(hi_ready, u + 1)
                    raw4 = w_raw[:, s, :].rearrange("p (k n) -> p k n", k=KT)
                    hi4 = w_hi[:, s, :].rearrange("p (k n) -> p k n", k=KT).bitcast(F32)
                    lo4 = w_lo[:, s, :].rearrange("p (k n) -> p k n", k=KT)
                    tt(lo4[:, :, 0:4], raw4[:, :, 0:4], hi4[:, :, 0:4], ALU.subtract)
                    tt(lo4[:, :, 32:36], raw4[:, :, 4:8], hi4[:, :, 32:36], ALU.subtract).then_inc(w_ready, 1)
                    return
                pool.wait_ge(hi_ready, u + 1)
                if u >= SLOTS:
                    pool.wait_ge(group_ready, GROUPS[u - 1])
                tt(w_lo[:, s, :], w_raw[:, s, :], w_hi[:, s, :].bitcast(F32), ALU.subtract).then_inc(w_ready, 1)

            def split_lo_loop(base, gbase, i, n, gn, s, g_before):
                sl = (base + s) % SLOTS
                pool.wait_ge(group_ready, gbase + g_before + i * gn)
                pool.wait_ge(hi_ready, base + s + 1 + i * n)
                tt(w_lo[:, sl, :], w_raw[:, sl, :], w_hi[:, sl, :].bitcast(F32), ALU.subtract).then_inc(w_ready, 1)

            def power(pre, i, n):
                pool.wait_ge(sem(pre + "_ms"), i + 1)
                tt(rs[0:n, i:i + 1], ss[0:n, i:i + 1], mhalf[0:n, i:i + 1], ALU.pow).then_inc(sem(pre + "_rs"), 1)

            def norm_all(pre, full):
                for i in range(NT + 4):
                    if pre == "x" and i == NT - 1:
                        split_lo(0)
                    if i <= NT:
                        power(pre, i, rows_of[i])
                    if i >= 3:
                        t0, t1 = TT_[i - 3]
                        pool.wait_ge(sem(pre + "_hi"), 2 * (i - 3) + 1)
                        tt(h_lo[:, 0:4, t0:t1], full_of(full, i - 3, 0), h_hi[:, 0:4, t0:t1].bitcast(F32),
                           ALU.subtract).then_inc(sem(pre + "_lo_a"), 1)

            link(pool.memset(mhalf[:, :], -0.5))
            norm_all("x", full0)
            phase_end(pool, "pool", 1)
            pool.memset(e_d[:, :, 0:CD - 1], 0.0)
            pool.memset(e_c[:, 0:CC - 1], 0.0).then_inc(sem("pads_zero"), 1)
            pool.wait_ge(sem("pads_zero"), 1)

            def bs_view(f, s):
                if s == 1:
                    return f
                off, n = {2: (0, 544), 4: (544, 272), 8: (816, 136), 16: (952, 64), 32: (1016, 32),
                          64: (1048, 16), 128: (1064, 8)}[s]
                return tree[:, off:off + n]

            def spread_v(x, vz, v, h):
                vv = v.rearrange("p (o v) -> p o v", o=1).broadcast_to([TS, NS, P])
                bb = bmask.rearrange("p (b o) -> p b o", o=1).broadcast_to([TS, NS, P])
                tt(vz[:, :, :], vv, bb, ALU.mult).then_inc(sem(x + "_vz"), 1)

            def diag_q(x, qz, q):
                pool.tensor_copy(qz[:, :].rearrange("p (b n) -> p b n", n=TS + LS)[:, :, 0:LS],
                                 q.rearrange("p (b t) -> p b t", t=LS)).then_inc(sem(x + "_qz"), 1)

            for it in ITEMS:
                if it[0] == "half":
                    _, u, g, hf = it
                    kind, name, idx = UNITS[u]
                    if g == 0 and hf == 0:
                        split_lo(u + 1)
                    if hf == 1 and g == 1 and u and UNITS[u - 1][1] == "ad":
                        idx = UNITS[u - 1][2]
                        pool.wait_ge(sem("glu_done"), 3 * idx + 3)
                        pool.tensor_copy(endd[:, idx, 0:64], e_d[:, idx, CD - 1 + TP - 64:])
                        pool.tensor_copy(endd[:, idx, 64:128].rearrange("p (b t) -> p b t", t=LS),
                                         e_ds[:, idx, :, CD - 1:]).then_inc(sem("ends_ready"), 1)
                    if hf == 1 and g == 1 and name == "bc":
                        pool.wait_ge(sem("short_in"), 3 * idx + 3)
                        pool.tensor_copy(endc[:, idx, 0:64], e_c[:, CC - 1 + TP - 64:])
                        pool.tensor_copy(endc[:, idx, 64:128].rearrange("p (b t) -> p b t", t=LS),
                                         e_cs[:, :, CC - 1:]).then_inc(sem("ends_ready"), 1)
                    if hf == 1 and g == 2 and name == "bc":
                        pool.wait_ge(sem("short_done"), idx + 1)
                        for j, (c0, c1) in enumerate(CH):
                            pool.wait_ge(acc_free[j], FILLS[u] + 1)
                            tt(o_c[:, c0:c1], o_c[:, c0:c1], y_c[:, c0:c1], ALU.mult).then_inc(sem("oc_done"), 1)
                elif it[0] == "pool_tap":
                    j = it[2]
                    w = par[:, 0, R_CDW + j:R_CDW + j + 1]
                    yp, ys = y_d[:, 0, 0:TP], y_d[:, 0, TP:T].rearrange("p (b t) -> p b t", t=LS)
                    xp, xs_ = e_d[:, 0, j:j + TP], e_ds[:, 0, :, j:j + LS]
                    if j == 0:
                        b = par[:, 0, R_CDB:R_CDB + 1]
                        pool.wait_ge(sem("bufs_in"), 1)
                        pool.wait_ge(sem("glu_done"), 3)
                        pool.tensor_scalar(yp, xp, w, b, ALU.mult, ALU.add)
                        ins = pool.tensor_scalar(ys, xs_, w, b, ALU.mult, ALU.add)
                    else:
                        pool.wait_ge(sem("prod_ready"), j)
                        ins = tt(y_d[:, 0, :], tap_prod[:, j % 2, :], y_d[:, 0, :], ALU.add)
                    ins.then_inc(sem("prod_used"), 1)
                    pool.wait_ge(sem("prod_used"), j + 1)
                    if j == CD - 1:
                        pool.nop().then_inc(sem("conv_done"), 1)
                elif it[0] == "ln":
                    _, stage, t = it
                    if stage == "scale":
                        pool.wait_ge(sem("ln_scaled"), t + 1)
                        pool.tensor_scalar(y_d[:, t, :], y_d[:, t, :], par[:, t, R_LNG:R_LNG + 1],
                                           par[:, t, R_LNB:R_LNB + 1], ALU.mult, ALU.add) \
                            .then_inc(sem("ln_affine"), 1)
                elif it[0] == "phase":
                    phase_end(pool, "pool", it[1])
                    if it[1] == 2:
                        pool.wait_ge(sem("phase_sp"), 2)
                        pool.memset(rt, 0.0).then_inc(sem("rt_zero"), 1)
                        pool.memset(qzb[:, :], 0.0)
                        pool.memset(vb[:, :, :, P:P + 1], 1.0)
                        pool.memset(den[:, :], 1.0)
                        pool.memset(cols[:, :, :], 0.0)
                        link(pool.memset(otb[:, :, :], 0.0))
                elif it[0] == "rec":
                    _, x, s, h = it
                    b2 = h % 2
                    if x == "A" and s in ("prepq", "prep"):
                        q, k, f, g_ = qa[:, b2, :], ka[:, b2, :], fa[:, b2, :], ga[:, b2, :]
                    if x == "A" and s == "prepq":
                        pool.wait_ge(sem("a_proj"), 9 * h + 6)
                        tt(q, q, k, ALU.mult)
                        link(pool.tensor_scalar(f, f, lbt[:, 3, h:h + 1], lbt[:, 2, h:h + 1], ALU.mult, ALU.add))
                        if h == 0:
                            pool.wait_ge(sem("od_stored"), 1)
                        pool.tensor_scalar(k, f, -1.0, 1.0, ALU.mult, ALU.add).then_inc(sem("a_prep"), 1)
                    elif x == "A" and s == "prep":
                        pool.wait_ge(sem("a_prep"), h + 1)
                        pool.wait_ge(sem("a_proj"), 9 * h + 9)
                        link(tt(g_, g_, sga[:, b2, :], ALU.mult))
                        tt(sga[:, b2, :], q, f, ALU.mult).then_inc(sem("a_q1"), 1)
                        if h:
                            pool.wait_ge(sem("a_snew"), h)
                        for i in range(7):
                            s_ = 1 << i
                            n = (T if s_ <= 4 else TP) // s_
                            pv = bs_view(f, s_)[:, 0:n].rearrange("p (b two) -> p b two", two=2)
                            out = bs_view(f, 2 * s_)
                            ins = tt(out[:, 0:n // 2], pv[:, :, 0], pv[:, :, 1], ALU.mult)
                            if i < 6:
                                link(ins)
                            else:
                                ins.then_inc(sem("a_tree"), 1)
                        pool.wait_ge(sem("va_ready"), 9 * (h // 2) + 9)
                        spread_v("a", vza, va[0:TS, NT, (h % 2) * P:(h % 2 + 1) * P], h)
                    elif x == "A" and s.startswith("lv"):
                        if s == "lv0" and h == 0:
                            pool.memset(qza[:, :], 0.0)
                            link(pool.memset(ota[:, :, :], 0.0))
                        if s == "lv4":
                            pool.wait_ge(sem("a_lv"), 7 * h + 3)
                            if h:
                                pool.wait_ge(sem("a_out"), h)
                            diag_q("a", qza, sga[:, b2, TP:T])
                    elif x == "B" and s == "prep":
                        if h == 0:
                            pool.wait_ge(sem("b_rows"), 1)
                        if h:
                            pool.wait_ge(sem("b_out"), h)
                        pool.wait_ge(sem("vb_ready"), 9 * (h // 2) + 9)
                        spread_v("b", vzb, vb[0:TS, NT, h % 2, 0:P], h)
                    elif x == "B" and s == "decay":
                        pool.wait_ge(sem("b_decayed"), h + 1)
                        diag_q("b", qzb, qs[:, TP:T])
                    elif s == "norm":
                        x_ = x.lower()
                        pool.wait_ge(sem(x_ + "_ms"), h + 1)
                        tt(rs[:, 0:NT + 1], ss[:, 0:NT + 1], mhalf[:, 0:NT + 1], ALU.pow) \
                            .then_inc(sem(x_ + "_rs"), 1)

            def branch_load(n_i, t):
                pool.dma_start(b_raw[:, t % 2, :], scratch[bass.ds(n_i, 1), t].rearrange("a p n -> (a p) n")) \
                    .then_inc(sem(f"b_in{t % 2}"), 16)

            with pool.Fori(0, M_IT) as i:
                branch_load(i, 0)
                branch_load(i, 1)
                for s in range(M_UN):
                    pair, j = s // 3, s % 3
                    split_lo_loop(M_U, M_G, i, M_UN, M_GN, s + 1, 12 * pair + 3 * j)
                    if s < 2:
                        for t in (2 * s, 2 * s + 1):
                            pool.wait_ge(sem("b_hi_ready"), i * 4 + t + 1)
                            tt(b_lo[:, t, :], b_raw[:, t % 2, :], b_hi[:, t, :].bitcast(F32), ALU.subtract) \
                                .then_inc(sem("branch_ready"), 1)
                            if t < 2:
                                pool.wait_ge(sem("branch_ready"), i * 4 + t + 1)
                                branch_load(i, t + 2)
            phase_end(pool, "pool", 4)
            for k in (2, 5):
                pool.wait_ge(sem("mh_ready"), k + 3)
                tt(h_lo[:, k, :], merged[:, k, :], h_hi[:, k, :].bitcast(F32), ALU.subtract) \
                    .then_inc(sem("merged_low_b"), 1)
            with pool.Fori(0, O_IT) as i:
                for s in range(O_UN):
                    split_lo_loop(O_U, O_G, i, O_UN, O_GN, s + 1, 9 * s)
            norm_all("m", full1)
            pool.sem_inc(sem("u_ready"), 2)
            phase_end(pool, "pool", 5)
            with pool.Fori(0, L_IT) as i:
                for s in range(L_UN):
                    split_lo_loop(L_U, L_G, i, L_UN, L_GN, s + 1, 3 * s if s < 4 else 12 + 9 * (s - 4))
                    if s >= 4:
                        continue
                    for g in range(3):
                        c0, c1 = CH[g]
                        e = 3 * s + g
                        pool.wait_ge(sem("u_high"), e + 1 + i * 12)
                        tt(u_lo[:, s, c0:c1], uu[:, e % 2, 0:c1 - c0], u_hi[:, s, c0:c1].bitcast(F32),
                           ALU.subtract).then_inc(sem("u_ready"), 1)
            pool.wait_ge(sem("gfin_in"), 16)
            for i in range(NT + 1):
                n = rows_of[i]
                pool.wait_ge(sem("f_sq"), i + 1)
                link(pool.tensor_scalar(ss[0:n, i:i + 1], ss[0:n, i:i + 1], 1.0 / D, EPS, ALU.mult, ALU.add))
                tt(rs[0:n, i:i + 1], ss[0:n, i:i + 1], mhalf[0:n, i:i + 1], ALU.pow).then_inc(sem("f_rs"), 1)
                if i in (0, NT - 2):
                    k = min(i, 1)
                    pool.wait_ge(sem("f_rs"), i + 1)
                    link(tt(x1[:, k, :], x1[:, k, :], gfin[:, :], ALU.mult))
                    tt(x1[:, k, :], x1[:, k, :], rs[:, k:k + 1].broadcast_to([P, D]), ALU.mult) \
                        .then_inc(sem("y_done_pool"), 1)

        @block.vector
        def _(dve):
            links = [0]

            def link(ins):
                links[0] += 1
                ins.then_inc(sem("dve_link"), 1)
                dve.wait_ge(sem("dve_link"), links[0])

            def tt(out, x, y, op):
                return dve.tensor_tensor(out, x, y, op)

            def stt(out, x, sc, y, op0, op1):
                return dve.scalar_tensor_tensor(out, x, sc, y, op0, op1)

            def norm_all(pre, src, dst, full, col):
                for i in range(NT + 4):
                    if i <= NT:
                        n = rows_of[i]
                        dve.wait_ge(sem(pre + "_sq"), i + 1)
                        dve.tensor_scalar(ss[0:n, i:i + 1], ss[0:n, i:i + 1], 1.0 / D, EPS, ALU.mult, ALU.add) \
                            .then_inc(sem(pre + "_ms"), 1)
                    if 1 <= i <= NT + 1:
                        k = i - 1
                        n = rows_of[k]
                        dve.wait_ge(sem(pre + "_rs"), k + 1)
                        if k >= 2:
                            dve.wait_ge(sem(pre + "_turned"), 2 * k - 2)
                        dve.tensor_scalar(dst[0:n, k % 2, :], src(k), rs[0:n, k:k + 1], None, ALU.mult) \
                            .then_inc(sem(pre + "_scaled"), 1)
                    if 2 <= i <= NT + 2:
                        k = i - 2
                        n = rows_of[k]
                        if k == 0 and pre == "x":
                            params_out()
                        if k >= 2:
                            dve.wait_ge(sem(pre + "_lo_a"), k - 1)
                            dve.wait_ge(sem(pre + "_lo_b"), k - 1)
                        for hh in range(2):
                            dve.wait_ge(sem(pre + "_turned"), 2 * k + hh + 1)
                            gain = nrm[:, col + 4 * hh:col + 4 * hh + 4].rearrange("p (k o) -> p k o", o=1) \
                                .broadcast_to([P, 4, n])
                            tt(full_of(full, k, hh), pz[:, 1 + 2 * (k % 2) + hh, :]
                               .rearrange("p (k n) -> p k n", k=4)[:, :, 0:n], gain, ALU.mult) \
                                .then_inc(sem(pre + "_full"), 1)
                    if i >= 3:
                        t0, t1 = TT_[i - 3]
                        dve.wait_ge(sem(pre + "_hi"), 2 * (i - 3) + 2)
                        tt(h_lo[:, 4:8, t0:t1], full_of(full, i - 3, 1), h_hi[:, 4:8, t0:t1].bitcast(F32),
                           ALU.subtract).then_inc(sem(pre + "_lo_b"), 1)

            def params_out():
                dve.wait_ge(sem("params_turned"), 1)
                dve.tensor_copy(par[:, :, :], pz[:, 0, 0:FT * NPAR].rearrange("p (t n) -> p t n", t=FT))
                link(dve.tensor_copy(nrm[:, :], pz[:, 0, FT * NPAR:FT * NPAR + 16]))
                lbl = par[:, :, R_LB]
                tt(lbt[:, 0, :], lbl, lbl, ALU.subtract).then_inc(sem("lb_diff"), 1)

            norm_all("x", lambda i: xin[0:rows_of[i], i, :], xt, full0, 0)
            dve.wait_ge(consts_in, 48)
            phase_end(dve, "dve", 1)
            dve.wait_ge(sem("lb_exp"), 1)
            link(dve.reciprocal(lbt[:, 2, :], lbt[:, 1, :]))
            link(tt(lbt[:, 3, :], lbt[:, 1, :], lbt[:, 2, :], ALU.mult))
            link(tt(lbt[:, 2, :], lbt[:, 3, :], lbt[:, 3, :], ALU.subtract))
            dve.tensor_scalar(lbt[:, 3, :], lbt[:, 2, :], -1.0, 1.0, ALU.mult, ALU.add)

            def convs_in():
                dve.wait_ge(consts_in, 64)
                for i in range(7):
                    dve.tensor_copy(lvm[:, i, :].rearrange("p (c n) -> p c n", c=NT),
                                    lvf[:, i:i + 1, :].broadcast_to([P, NT, 64]))
                dve.wait_ge(sem("bufs_turned"), 1)
                for j in range(2):
                    dve.tensor_copy(e_ds[:, :, 4 * j:4 * j + 4, 0:CD - 1],
                                    pz[:, j, 0:480].rearrange("p (t b n) -> p t b n", t=FT, b=4))
                dve.tensor_copy(e_cs_old[:, :, :, :],
                                pz[:, 2, 0:64].rearrange("p (t b n) -> p t b n", t=FT, b=NS)) \
                    .then_inc(sem("bufs_in"), 1)

            def evac(u, g):
                kind, name, idx = UNITS[u]
                if kind == "feat":
                    c0, c1 = CH[g]
                    src = acc[:, g, 0:c1 - c0]
                    if name == "ad":
                        dve.wait_ge(group_ready, GROUPS[u] + g + 1)
                        ed = e_d[:, idx, CD - 1:]
                        if g < 2:
                            tt(ed[:, c0:c1], src, sg_d[:, c0:c1], ALU.mult).then_inc(acc_free[g], 1)
                        else:
                            tt(ed[:, c0:TP], src[:, 0:TP - c0], sg_d[:, c0:TP], ALU.mult)
                            tt(e_ds[:, idx, :, CD - 1:], src[:, TP - c0:T - c0].rearrange("p (b t) -> p b t", t=LS),
                               sg_d[:, TP:T].rearrange("p (b t) -> p b t", t=LS), ALU.mult).then_inc(acc_free[g], 1)
                        dve.wait_ge(acc_free[g], FILLS[u] + 1)
                        dve.nop().then_inc(sem("glu_done"), 1)
                    elif name == "xc":
                        dve.wait_ge(group_ready, GROUPS[u] + g + 1)
                        dve.wait_ge(acc_free[g], FILLS[u])
                        if g == 0:
                            if idx:
                                dve.wait_ge(sem("short_done"), idx)
                            dve.tensor_copy(e_cs[:, :, 0:CC - 1], e_cs_old[:, idx, :, :])
                        ec = e_c[:, CC - 1:]
                        if g < 2:
                            tt(ec[:, c0:c1], src, ec[:, c0:c1], ALU.mult).then_inc(acc_free[g], 1)
                        else:
                            tt(ec[:, c0:TP], src[:, 0:TP - c0], ec[:, c0:TP], ALU.mult)
                            sv = e_cs[:, :, CC - 1:]
                            tt(sv, src[:, TP - c0:T - c0].rearrange("p (b t) -> p b t", t=LS), sv, ALU.mult) \
                                .then_inc(acc_free[g], 1)
                        dve.wait_ge(acc_free[g], FILLS[u] + 1)
                        dve.nop().then_inc(sem("short_in"), 1)
                elif kind == "tok" and idx % 2 == 1:
                    n = rows_of[g]
                    a_ = name == "ia"
                    dve.wait_ge(group_ready, GROUPS[u] + g + 1)
                    dve.wait_ge(acc_free[g % 3], FILLS[u] - 2 + g // 3)
                    dst = va[0:n, g, :] if a_ else vb[0:n, g, :, 0:P]
                    src = acc[0:n, g % 3, 0:256]
                    if not a_:
                        src = src.rearrange("p (h v) -> p h v", h=2)
                    tt(dst, src, dst, ALU.add).then_inc(acc_free[g % 3], 1)
                    if g == 8:
                        for b in range(3):
                            dve.wait_ge(acc_free[b], FILLS[u] + 3)
                        dve.nop().then_inc(sem("va_ready" if a_ else "vb_ready"), 9)

            def tap(t, j):
                w = par[:, t, R_CDW + j:R_CDW + j + 1]
                yp, ys = y_d[:, t, 0:TP], y_d[:, t, TP:T].rearrange("p (b t) -> p b t", t=LS)
                xp, xs_ = e_d[:, t, j:j + TP], e_ds[:, t, :, j:j + LS]
                if j == 0:
                    b = par[:, t, R_CDB:R_CDB + 1]
                    if t == 1:
                        dve.wait_ge(sem("pads_zero"), 1)
                        dve.wait_ge(sem("bufs_in"), 1)
                    dve.wait_ge(sem("glu_done"), 3 * t + 3)
                    dve.tensor_scalar(yp, xp, w, b, ALU.mult, ALU.add)
                    dve.tensor_scalar(ys, xs_, w, b, ALU.mult, ALU.add).then_inc(sem("tap_done"), 1)
                else:
                    dve.wait_ge(sem("tap_done"), CD * (t - 1) + j)
                    stt(yp, xp, w, yp, ALU.mult, ALU.add)
                    stt(ys, xs_, w, ys, ALU.mult, ALU.add).then_inc(sem("tap_done"), 1)
                if j == CD - 1:
                    dve.wait_ge(sem("tap_done"), CD * t)
                    dve.nop().then_inc(sem("conv_done"), 1)

            def short(t):
                yp, ys = y_c[:, 0:TP], y_c[:, TP:T].rearrange("p (b t) -> p b t", t=LS)
                dve.wait_ge(sem("short_in"), 3 * t + 3)
                if t:
                    dve.wait_ge(sem("oc_done"), 3 * t)
                for j in range(CC):
                    w = par[:, t, R_CCW + j:R_CCW + j + 1]
                    xp, xs_ = e_c[:, j:j + TP], e_cs[:, :, j:j + LS]
                    if j == 0:
                        dve.tensor_scalar(yp, xp, w, None, ALU.mult)
                        link(dve.tensor_scalar(ys, xs_, w, None, ALU.mult))
                    else:
                        stt(yp, xp, w, yp, ALU.mult, ALU.add)
                        ins = stt(ys, xs_, w, ys, ALU.mult, ALU.add)
                        if j < CC - 1:
                            link(ins)
                ins.then_inc(sem("short_done"), 1)

            def rms(x, h, ot, sq):
                link(tt(sq[:, :, :], ot[:, :, :], ot[:, :, :], ALU.mult))
                link(dve.tensor_reduce(ss[:, 0:NT + 1], sq[:, :, :], AX, ALU.add))
                dve.tensor_scalar(ss[:, 0:NT + 1], ss[:, 0:NT + 1], 1.0 / P, EPS, ALU.mult, ALU.add) \
                    .then_inc(sem(x + "_ms"), 1)

            def rms_scale(x, h, ot):
                dve.wait_ge(sem(x + "_rs"), h + 1)
                tt(ot[:, :, :], ot[:, :, :], rs[:, 0:NT + 1].rearrange("p (c o) -> p c o", o=1)
                   .broadcast_to([P, NT + 1, P]), ALU.mult).then_inc(sem(x + "_normed"), 1)

            def gate_out(x, h, g_, row):
                dve.wait_ge(sem(x + "_turned"), h + 1)
                gain = par[:, h, row:row + 1]
                stt(g_[:, 0:512], pz[:, 0, :], gain, g_[:, 0:512], ALU.mult, ALU.mult)
                stt(g_[:, 512:TP], pz[:, 1, :], gain, g_[:, 512:TP], ALU.mult, ALU.mult)
                stt(g_[:, TP:T], pz[:, 2, 0:TS], gain, g_[:, TP:T], ALU.mult, ALU.mult).then_inc(sem(x + "_gated"), 1)

            def rec_a(s, h):
                b2 = h % 2
                k, f = ka[:, b2, :], fa[:, b2, :]
                if s == "lv0":
                    dve.wait_ge(sem("a_scored"), 8 * h + 1)
                    idb = ident.rearrange("p (o n) -> p o n", o=1).broadcast_to([P, 4, P])
                    for j in range(2):
                        tt(sa[:, 512 * j:512 * j + 512].rearrange("p (c n) -> p c n", n=P),
                           pz[:, j, :].rearrange("p (c n) -> p c n", n=P), idb, ALU.mult)
                    tt(sa[0:TS, TP:T], pz[0:TS, 2, 0:TS], ident[0:TS, 0:TS], ALU.mult).then_inc(sem("a_masked"), 1)
                elif s.startswith("lv"):
                    i = int(s[2:])
                    sz = 1 << (i - 1)
                    bank, sbank = (3, 4) if i % 2 else (0, 2)
                    dve.wait_ge(sem("a_scored"), 8 * h + i + 1)
                    n = T if sz <= 4 else TP
                    if i == 1:
                        dve.wait_ge(sem("a_tree"), h + 1)
                        dve.wait_ge(sem("a_q1"), h + 1)
                    else:
                        dve.wait_ge(sem("a_lv"), 7 * h + i - 1)
                    kv = k[:, 0:n].rearrange("p (b two s) -> p b two s", two=2, s=sz)[:, :, 0, :]
                    bv = bs_of(f, sz)[:, 0:n // sz].rearrange("p (b two) -> p b two", two=2)[:, :, 1:2] \
                        .broadcast_to([P, n // (2 * sz), sz])
                    q = sga[:, b2, :]
                    qv = q[:, 0:n].rearrange("p (b two s) -> p b two s", two=2, s=sz)[:, :, 1, :]
                    bq = bs_of(f, sz)[:, 0:n // sz].rearrange("p (b two) -> p b two", two=2)[:, :, 0:1] \
                        .broadcast_to([P, n // (2 * sz), sz])
                    tt(kv, kv, bv, ALU.mult)
                    tt(qv, qv, bq, ALU.mult).then_inc(sem("a_lv"), 1)
                    dve.wait_ge(sem("a_masked"), 8 * h + i)
                    mask = lvm[:, i - 1, :]
                    so = sa[:, 0:TP].rearrange("p (b two s) -> p b two s", two=2, s=sz)[:, :, 1, :]
                    ins = dve.copy_predicated(so, mask.rearrange("p (b s) -> p b s", s=sz),
                                              pz[:, bank, :].rearrange("p (b s) -> p b s", s=sz))
                    if i <= 3:
                        so = sa[0:TS, TP:T].rearrange("p (b two s) -> p b two s", two=2, s=sz)[:, :, 1, :]
                        ins = dve.copy_predicated(so, mask[0:TS, 0:32].rearrange("p (b s) -> p b s", s=sz),
                                                  pz[0:TS, sbank, 0:32].rearrange("p (b s) -> p b s", s=sz))
                    ins.then_inc(sem("a_masked"), 1)
                elif s == "state":
                    dve.wait_ge(sem("a_updates"), h + 1)
                    if h:
                        dve.wait_ge(sem("a_stored"), h)
                    link(dve.tensor_copy(sta[:, 0, :], pz[:, 3, 0:P]))
                    b128, b8 = bs_of(f, 128), bs_of(f, 8)
                    for c in range(1, NT):
                        ins = stt(sta[:, c, :], sta[:, c - 1, :], b128[:, c:c + 1],
                                  pz[:, 3 + c // 4, (c % 4) * P:(c % 4 + 1) * P], ALU.mult, ALU.add)
                        if c < NT - 1:
                            link(ins)
                    ins.then_inc(sem("a_states"), 1)
                    dve.wait_ge(sem("s0_in"), 16 * (h + 1))
                    link(tt(sna[:, :, :], s0a[:, :, :], b8[:, 128:136].rearrange("p (b o) -> p b o", o=1)
                            .broadcast_to([P, NS, P]), ALU.mult))
                    for j in range(2):
                        ins = tt(sna[:, 4 * j:4 * j + 4, :], pz[:, j, :].rearrange("p (b v) -> p b v", v=P),
                                 sna[:, 4 * j:4 * j + 4, :], ALU.add)
                    ins.then_inc(sem("a_snew"), 1)
                elif s == "norm":
                    dve.wait_ge(sem("a_oevac"), h + 1)
                    rms("a", h, ota, sqa)
                elif s == "gate":
                    dve.wait_ge(sem("a_q1"), h + 1)
                    gate_out("a", h, ga[:, b2, :], R_NH)

            def rows():
                dve.wait_ge(acc_free[2], FILLS[IF_U] + 1)
                dve.wait_ge(acc_free[1], FILLS[IF_U] + 1)
                dve.wait_ge(acc_free[0], FILLS[IF_U] + 1)
                dve.tensor_scalar(irow, irow, biases[:, 0:1], None, ALU.add)
                dve.tensor_scalar(frow, frow, biases[:, 1:2], None, ALU.add).then_inc(sem("f_biased"), 1)
                dve.wait_ge(sem("f_biased"), 1)
                dve.wait_ge(sem("row_act"), 3)
                link(stt(frow, frow, 0.0, trow, ALU.min, ALU.subtract))
                dve.wait_ge(sem("m0_in"), 32)
                dve.tensor_tensor_scan(mrow[:, 0:TP], frow[:, 0:TP], irow[:, 0:TP], 0.0, ALU.add, ALU.max)
                for b in range(NS):
                    t0 = TP + LS * b
                    dve.tensor_tensor_scan(mrow[:, t0:t0 + LS], frow[:, t0:t0 + LS], irow[:, t0:t0 + LS],
                                           m0[:, b:b + 1], ALU.add, ALU.max)
                link(dve.tensor_tensor_scan(brow, keepr[:, :], frow, 0.0, ALU.mult, ALU.add))
                dve.nop().then_inc(sem("m_done"), 1)
                tt(nM[:, :], brow, mrow[:, :], ALU.subtract)
                tt(arow, irow, brow, ALU.subtract)
                dve.memset(mp[:, 0:1], 0.0)
                dve.tensor_copy(mp[:, 1:NT], mrow[:, P - 1:TP - P:P])
                link(dve.tensor_copy(mp[:, NT:16], m0[:, 0:NS]))
                dve.tensor_copy(nlast[:, 0:NT], nM[:, P - 1:TP:P])
                link(dve.tensor_copy(nlast[:, NT:16], nM[:, TP + LS - 1:T:LS]))

                def spread(v, j):
                    return (v[:, 0:NT].rearrange("p (c o) -> p c o", o=1).broadcast_to([H, NT, P]) if j == 0 else
                            v[:, NT:16].rearrange("p (c o) -> p c o", o=1).broadcast_to([H, NS, LS]))

                def view(r, j):
                    return r[:, 0:TP].rearrange("p (c n) -> p c n", n=P) if j == 0 else \
                        r[:, TP:T].rearrange("p (c n) -> p c n", n=LS)
                for j in range(2):
                    tt(view(trow, j), view(nM, j), spread(mp, j), ALU.add)
                    ins = tt(view(urow, j), view(arow, j), spread(nlast, j), ALU.add)
                link(ins)
                tt(nlast[:, :], nlast[:, :], mp[:, :], ALU.add).then_inc(sem("row_exps"), 1)

            def rows_out():
                dve.wait_ge(sem("rows_turned"), 1)
                dve.tensor_copy(cols[:, 0:4, :], pz[:, 0, :].rearrange("p (c n) -> p c n", n=P))
                dve.tensor_copy(cols[:, 4:8, :], pz[:, 1, :].rearrange("p (c n) -> p c n", n=P))
                dve.tensor_copy(cols[0:TS, NT, :], pz[0:TS, 2, 0:P])
                dve.tensor_copy(cdc[:, :, :], pz[:, 3, 0:64].rearrange("p (h c) -> p h c", h=H)) \
                    .then_inc(sem("b_rows"), 1)

            def rec_b(s, h):
                b2 = h % 2
                q = qb[:, b2, :]
                if s == "decay":
                    dve.wait_ge(sem("b_spread"), h + 1)
                    if h == 0:
                        dve.wait_ge(sem("b_rows"), 1)
                    for c in range(NT):
                        stt(wb[:, c * P:(c + 1) * P], pz[:, c // 4, (c % 4) * P:(c % 4 + 1) * P],
                            cols[:, c, h:h + 1], negm, ALU.add, ALU.min)
                    stt(wb[0:TS, TP:T], pz[0:TS, 2, 0:TS], cols[0:TS, NT, h:h + 1], negs, ALU.add, ALU.min)
                    dve.wait_ge(sem("b_proj"), 9 * h + 6)
                    tt(qs[:, 0:512], pz[:, 3, :], q[:, 0:512], ALU.mult)
                    tt(qs[:, 512:TP], pz[:, 4, :], q[:, 512:TP], ALU.mult)
                    tt(qs[:, TP:T], pz[:, 2, 64:128], q[:, TP:T], ALU.mult).then_inc(sem("b_decayed"), 1)
                elif s == "score":
                    dve.wait_ge(sem("b_exp"), h + 1)
                    dve.wait_ge(sem("b_scored"), h + 1)
                    tt(wb[:, 0:512], pz[:, 0, :], wb[:, 0:512], ALU.mult)
                    tt(wb[:, 512:TP], pz[:, 1, :], wb[:, 512:TP], ALU.mult)
                    tt(wb[0:TS, TP:T], pz[0:TS, 2, 0:TS], wb[0:TS, TP:T], ALU.mult).then_inc(sem("b_weighted"), 1)
                elif s == "turn":
                    dve.wait_ge(sem("b_kturned"), h + 1)

                    def ws(c0, c1, n=P):
                        return cols[0:n, c0:c1, 64 + h:65 + h].broadcast_to([n, c1 - c0, P])
                    tt(ktb[:, 0:4, :], pz[:, 3, :].rearrange("p (c n) -> p c n", n=P), ws(0, 4), ALU.mult)
                    tt(ktb[:, 4:8, :], pz[:, 4, :].rearrange("p (c n) -> p c n", n=P), ws(4, 8), ALU.mult)
                    dve.tensor_scalar(ktb[0:TS, NT, :], pz[0:TS, 2, 128:256], cols[0:TS, NT, 64 + h:65 + h], None,
                                      ALU.mult).then_inc(sem("b_kt"), 1)
                elif s == "state":
                    dve.wait_ge(sem("b_updates"), h + 1)
                    if h:
                        dve.wait_ge(sem("b_stored"), h)
                    dve.tensor_copy(nup[:, :], pz[:, 3, 400:408])
                    link(dve.tensor_copy(cnb[:, 0, 0:P + 1], pz[:, 0, 0:P + 1]))
                    for c in range(1, NT):
                        ins = stt(cnb[:, c, 0:P + 1], cnb[:, c - 1, 0:P + 1], cdc[:, h, c:c + 1],
                                  pz[:, (0, 1, 3)[c // 3], (c % 3) * 129:(c % 3) * 129 + 129], ALU.mult, ALU.add)
                        if c < NT - 1:
                            link(ins)
                    ins.then_inc(sem("b_states"), 1)
                    dve.wait_ge(sem("c0_in"), 32 * (h + 1))
                    link(tt(cnew[:, :, 0:P + 1], c0b[:, :, 0:P + 1],
                            cdc[:, h, NT:16].rearrange("p (b o) -> p b o", o=1).broadcast_to([P, NS, P + 1]),
                            ALU.mult))
                    for j, bk in enumerate((2, 4)):
                        tt(cnew[:, 4 * j:4 * j + 4, 0:P], pz[:, bk, :].rearrange("p (b v) -> p b v", v=P),
                           cnew[:, 4 * j:4 * j + 4, 0:P], ALU.add)
                    tt(cnew[:, :, P], nup[:, :], cnew[:, :, P], ALU.add)
                elif s == "norm":
                    dve.wait_ge(sem("b_absden"), h + 1)
                    link(tt(den[:, 0:NT + 1], den[:, 0:NT + 1], cols[:, :, 32 + h], ALU.max))
                    link(dve.reciprocal(den[:, 0:NT + 1], den[:, 0:NT + 1]))
                    for c0, c1, bk in ((0, 3, 0), (3, 6, 1), (6, 8, 3)):
                        n = c1 - c0
                        tt(otb[:, c0:c1, :], pz[:, bk, 0:129 * n].rearrange("p (c n) -> p c n", n=129)[:, :, 0:P],
                           den[:, c0:c1].rearrange("p (c o) -> p c o", o=1).broadcast_to([P, n, P]), ALU.mult)
                    link(dve.tensor_scalar(otb[0:TS, NT, :], pz[0:TS, 3, 258:386], den[0:TS, NT:NT + 1], None,
                                           ALU.mult))
                    rms("b", h, otb, sqb)
                elif s == "gate":
                    dve.wait_ge(sem("b_proj"), 9 * h + 9)
                    gate_out("b", h, gb[:, b2, :], R_NM)

            def bs_of(f, s):
                if s == 1:
                    return f
                off, n = {2: (0, 544), 4: (544, 272), 8: (816, 136), 16: (952, 64), 32: (1016, 32),
                          64: (1048, 16), 128: (1064, 8)}[s]
                return tree[:, off:off + n]

            for it in ITEMS:
                if it[0] == "half":
                    if it == ("half", 1, 0, 0):
                        convs_in()
                    if it[3] == 1:
                        evac(it[1], it[2])
                elif it[0] == "tap":
                    tap(it[1], it[2])
                elif it[0] == "short":
                    short(it[1])
                elif it[0] == "ln":
                    _, stage, t = it
                    cuts = ((0, 512), (512, 1024), (1024, T))
                    if stage == "centre":
                        dve.wait_ge(sem("ln_mean"), 1)
                        for k in range(FT):
                            for j, (c0, c1) in enumerate(cuts):
                                ins = stt(y_d[:, k, c0:c1], pz[:, j, 0:c1 - c0], -1.0 / W, y_d[:, k, c0:c1],
                                          ALU.mult, ALU.add)
                            ins.then_inc(sem("ln_centred"), 1)
                    elif stage == "root":
                        dve.wait_ge(sem("ln_var"), FT)
                        for j, (c0, c1) in enumerate(cuts):
                            ins = dve.tensor_scalar(ln_t[:, c0:c1], pz[:, j, 0:c1 - c0], 1.0 / W, EPS, ALU.mult,
                                                    ALU.add)
                        ins.then_inc(sem("ln_eps"), 1)
                    elif stage == "invert":
                        dve.wait_ge(sem("ln_sqrt"), 1)
                        q = slice(t * T // 4, (t + 1) * T // 4)
                        dve.reciprocal(ln_r[:, q], ln_t[:, q]).then_inc(sem("ln_inverse"), 1)
                    elif stage == "scale":
                        dve.wait_ge(sem("ln_inverse"), 4)
                        tt(y_d[:, t, :], y_d[:, t, :], ln_r[:, :], ALU.mult).then_inc(sem("ln_scaled"), 1)
                    elif stage == "gate":
                        dve.wait_ge(sem("ln_sig"), t + 1)
                        tt(y_d[:, t, :], y_d[:, t, :], (sg_d, y_c)[t % 2][:, :], ALU.mult).then_inc(sem("od_done"), 1)
                elif it[0] == "phase":
                    phase_end(dve, "dve", it[1])
                elif it[0] == "rows":
                    rows()
                elif it[0] == "rows_out":
                    rows_out()
                elif it[0] == "rec" and it[2] == "scale":
                    rms_scale(it[1].lower(), it[3], ota if it[1] == "A" else otb)
                elif it[0] == "rec":
                    (rec_a if it[1] == "A" else rec_b)(it[2], it[3])

            dve.sem_inc(sem("m_gated"), 1)
            dve.wait_ge(sem("stored"), n_branches[0])
            dve.memset(merged[:, :, :], 0.0).then_inc(sem("merged_zero"), 1)
            with dve.Fori(0, M_IT) as i:
                dve.wait_ge(sem("merged_zero"), 1)
                for pair in range(4):
                    for r in range(2):
                        for g in range(3):
                            c0, c1 = CH[g]
                            e = 6 * pair + 3 * r + g
                            dve.wait_ge(group_ready, M_G + 12 * pair + 6 + 3 * r + g + 1 + i * M_GN)
                            tt(gtmp[:, e % 2, 0:c1 - c0], acc[:, g, 0:c1 - c0], gsig[:, r, c0:c1], ALU.mult) \
                                .then_inc(acc_free[g], 1)
                            dve.wait_ge(acc_free[g], M_B + 4 * pair + 2 + r + 1 + i * M_BN)
                            mv = merged[:, 2 * pair + r, c0:c1]
                            tt(mv, gtmp[:, e % 2, 0:c1 - c0], mv, ALU.add).then_inc(sem("m_gated"), 1)
            phase_end(dve, "dve", 4)
            for n, (k, t0, t1) in enumerate(MERGED_PARTS):
                if k in (2, 5):
                    continue
                dve.wait_ge(sem("mh_ready"), n + 1)
                tt(h_lo[:, k, t0:t1], merged[:, k, t0:t1], h_hi[:, k, t0:t1].bitcast(F32), ALU.subtract) \
                    .then_inc(sem("merged_low_a"), 1)
            with dve.Fori(0, O_IT) as i:
                for s in range(O_UN):
                    for c in range(NT + 1):
                        n = rows_of[c]
                        if s == 0:
                            dve.wait_ge(x_in[c], 32)
                        if s == O_UN - 1 and c == 0:
                            dve.wait_ge(sem("xres_in"), 16 * (NT + 1))
                        dve.wait_ge(group_ready, O_G + 9 * s + c + 1 + i * O_GN)
                        if s:
                            dve.wait_ge(sem("o_added"), i * O_GN + 9 * (s - 1) + c + 1)
                        xv = x1[0:n, c, bass.ds(i * 512, 512)]
                        tt(xv, acc[0:n, c % 3, :], xv, ALU.add).then_inc(acc_free[c % 3], 1)
                        dve.wait_ge(acc_free[c % 3], O_B + 3 * s + c // 3 + 1 + i * O_BN)
                        dve.nop().then_inc(sem("o_added"), 1)
            norm_all("m", lambda i: x1[0:rows_of[i], i, :], xt1, full1, 8)
            dve.sem_inc(sem("l_added"), 1)
            phase_end(dve, "dve", 5)
            with dve.Fori(0, L_IT) as i:
                for s in range(4):
                    for g in range(3):
                        c0, c1 = CH[g]
                        e = 3 * s + g
                        dve.wait_ge(sem("u_relu"), e + 1 + i * 12)
                        dve.wait_ge(sem("u_ready"), e + 1 + i * 12)
                        tt(uu[:, e % 2, 0:c1 - c0], acc[:, g, 0:c1 - c0], ur[:, e % 2, 0:c1 - c0], ALU.mult) \
                            .then_inc(acc_free[g], 1)
                        dve.wait_ge(acc_free[g], L_B + s + 1 + i * L_BN)
                        dve.nop().then_inc(sem("u_squared"), 1)
                for s in range(4):
                    for c in range(NT + 1):
                        n = rows_of[c]
                        dve.wait_ge(group_ready, L_G + 12 + 9 * s + c + 1 + i * L_GN)
                        if s == 0 and c == 0:
                            dve.wait_ge(sem("l_added"), i * 36 + 1)
                        if s >= 2:
                            dve.wait_ge(sem("l_added"), i * 36 + 9 * (s - 2) + c + 2)
                        xv = x1[0:n, c, (s % 2) * 512:(s % 2 + 1) * 512]
                        tt(xv, acc[0:n, c % 3, :], xv, ALU.add).then_inc(acc_free[c % 3], 1)
                        dve.wait_ge(acc_free[c % 3], L_B + 4 + 3 * s + c // 3 + 1 + i * L_BN)
                        dve.nop().then_inc(sem("l_added"), 1)
            dve.wait_ge(sem("gfin_in"), 16)
            for i in range(2, NT + 1):
                n = rows_of[i]
                dve.wait_ge(sem("f_rs"), i + 1)
                stt(x1[0:n, i, :], x1[0:n, i, :], rs[0:n, i:i + 1], gfin[0:n, :], ALU.mult, ALU.mult) \
                    .then_inc(sem("y_done"), 1)


INS = ["x_prompt", "x_sample", "state_hgrn", "state_mlstm_c", "state_mlstm_n", "state_mlstm_m",
       "state_conv_short", "state_conv_conformer", "w_in", "w_branch", "w_out", "lb_logits", "norm_hgrn",
       "mlstm_i_bias", "mlstm_f_bias", "norm_mlstm", "conv_short_w", "conv_conformer_w", "conv_conformer_b",
       "ln_conformer_g", "ln_conformer_b", "norm_mix", "norm_mlp", "w_up", "w_down", "norm_final"]
OUTS = [("y_p", (1, TP, D)), ("y_s", (NS, LS, D)), ("hg_p", (1, 1, H, P, P)), ("hg_s", (1, NS, H, P, P)),
        ("mc_p", (1, 1, H, P, P)), ("mc_s", (1, NS, H, P, P)), ("mn_p", (1, 1, H, P)), ("mn_s", (1, NS, H, P)),
        ("mm_p", (1, 1, H)), ("mm_s", (1, NS, H)), ("cc_p", (1, 1, CC - 1, W)), ("cc_s", (1, NS, CC - 1, W)),
        ("cd_p", (1, 1, CD - 1, W)), ("cd_s", (1, NS, CD - 1, W))]


def kernel(**inputs):
    import concourse.bacc as bacc
    from concourse.bass_utils import run_bass_kernel_spmd

    nc = bacc.Bacc("TRN2", target_bir_lowering=False, num_devices=1)
    arrays, a, o = {}, {}, {}
    lvm, con, keep = constants()
    given = {n: np.ascontiguousarray(inputs[n]) for n in INS}
    given.update(lvm=lvm, con=con, keep=keep)
    for name, v in given.items():
        arrays["in_" + name] = v
        a[name] = nc.dram_tensor("in_" + name, v.shape, mybir.dt.from_np(v.dtype), kind="ExternalInput").ap()
    for name, shape in OUTS:
        o[name] = nc.dram_tensor("out_" + name, shape, F32, kind="ExternalOutput").ap()
    scratch = nc.dram_tensor("branch_outputs", (4, FT, P, T), F32, kind="Internal").ap()
    build(nc, a, o, scratch)
    r = run_bass_kernel_spmd(nc, [arrays], core_ids=[0])
    return tuple(r.results[0]["out_" + name] for name, _ in OUTS)
```
